# Optimizing a Trainium2 kernel written in Bass

```python
import jax
import jax.numpy as jnp
from jax import lax
import numpy as np

D_MODEL = 1024
BATCH = 1
SEQ = 256
DEPTH = 1
DEC_BATCH = 8
DEC_SEQ = 16
PAST_LEN = 512

CHUNK = 64
Q_BLOCK = 128
TOK_BLOCK = 128
EPS = 1e-6

H_A = 8
KVH_A = 2
GRP_A = H_A // KVH_A
DH_A = 64
H_IDX = 8
D_IDX = 64
TOPK_MAX = 256

H_B = 4
DK_B = 64
DV_B = 128
ROT_BASE = 10000.0

W_A = H_A * DH_A
W_B = H_B * DV_B
D_MIX = W_A + W_B

SPLIT_SIZES = (H_A * DH_A, KVH_A * DH_A, KVH_A * DH_A, H_IDX * D_IDX, D_IDX, H_IDX,
               H_B * DK_B, H_B * DK_B, H_B * DV_B, W_B)
D_IN = H_A * DH_A + 2 * KVH_A * DH_A + H_IDX * D_IDX + D_IDX + H_IDX + 2 * H_B * DK_B + H_B * DV_B + W_B

N_KEYS = 128
N_EXPERTS = N_KEYS * N_KEYS
PEER_HEADS = 8
PEER_TOPK = 16
D_PKEY = 256
D_PHALF = D_PKEY // 2

kernel_name = 'hybrid_dsa_retention_peer_stream_step'

def rmsnorm(x, g):
    xf = x.astype(jnp.float32)
    xf = xf * lax.rsqrt(jnp.mean(xf * xf, axis=-1, keepdims=True) + EPS)
    return xf.astype(x.dtype) * g

def project(h, w_in):
    B, T, _ = h.shape
    offs = []
    acc = 0
    for s in SPLIT_SIZES[:-1]:
        acc += s
        offs.append(acc)
    q_a, k_a, v_a, q_i, k_i, w_i, q_b, k_b, v_b, g_b = jnp.split(h @ w_in, offs, axis=-1)
    return (q_a.reshape(B, T, H_A, DH_A), k_a.reshape(B, T, KVH_A, DH_A), v_a.reshape(B, T, KVH_A, DH_A),
            q_i.reshape(B, T, H_IDX, D_IDX), k_i, w_i,
            q_b.reshape(B, T, H_B, DK_B), k_b.reshape(B, T, H_B, DK_B), v_b.reshape(B, T, H_B, DV_B), g_b)

def dsa_block(q, qi, wi, qpos, k_all, v_all, ki_all, kpos, topk):
    B, Tq = q.shape[:2]
    dots = jnp.einsum('bthd,bsd->bths', qi.astype(jnp.float32), ki_all.astype(jnp.float32))
    score = jnp.einsum('bth,bths->bts', wi.astype(jnp.float32), jax.nn.relu(dots))
    allowed = (kpos[None, :] // CHUNK) <= (qpos[:, None] // CHUNK)
    score = jnp.where(allowed[None], score, -jnp.inf)
    top_s, idx = lax.top_k(score, topk)
    valid = jnp.isfinite(top_s)
    gather = jax.vmap(lambda a, i: a[i])
    k_sel = gather(k_all, idx)
    v_sel = gather(v_all, idx)
    qg = q.reshape(B, Tq, KVH_A, GRP_A, DH_A)
    s = jnp.einsum('btkgd,btnkd->btkgn', qg, k_sel).astype(jnp.float32) * (DH_A ** -0.5)
    s = jnp.where(valid[:, :, None, None, :], s, -jnp.inf)
    p = jax.nn.softmax(s, axis=-1)
    o = jnp.einsum('btkgn,btnkd->btkgd', p.astype(v_sel.dtype), v_sel)
    return o.reshape(B, Tq, W_A)

def dsa_prompt(q, qi, wi, k, v, ki):
    B, T = q.shape[:2]
    nb = T // Q_BLOCK
    topk = min(TOPK_MAX, T // 4)
    pos = jnp.arange(T, dtype=jnp.int32)

    def blk(a):
        return a.reshape(B, nb, Q_BLOCK, *a.shape[2:]).swapaxes(0, 1)

    def body(args):
        qb, qib, wib, pb = args
        return dsa_block(qb, qib, wib, pb, k, v, ki, pos, topk)

    o = lax.map(body, (blk(q), blk(qi), blk(wi), pos.reshape(nb, Q_BLOCK)))
    return o.swapaxes(0, 1).reshape(B, T, W_A)

def dsa_sample(q, qi, wi, k, v, ki, cache_k, cache_v, cache_ki):
    P = cache_k.shape[1]
    T = q.shape[1]
    k_all = jnp.concatenate([cache_k, k], axis=1)
    v_all = jnp.concatenate([cache_v, v], axis=1)
    ki_all = jnp.concatenate([cache_ki, ki], axis=1)
    kpos = jnp.arange(P + T, dtype=jnp.int32)
    qpos = P + jnp.arange(T, dtype=jnp.int32)
    topk = min(TOPK_MAX, (P + T) // 4)
    return dsa_block(q, qi, wi, qpos, k_all, v_all, ki_all, kpos, topk)

def rotate(x, pos):
    half = DK_B // 2
    inv = 1.0 / (ROT_BASE ** jnp.linspace(0.0, 1.0, half, dtype=jnp.float32))
    ang = pos.astype(jnp.float32)[:, None] * inv[None, :]
    cos = jnp.cos(ang)[None, :, None, :]
    sin = jnp.sin(ang)[None, :, None, :]
    xf = x.astype(jnp.float32)
    x1, x2 = xf[..., :half], xf[..., half:]
    return jnp.concatenate([x1 * cos - x2 * sin, x1 * sin + x2 * cos], axis=-1)

def retention_chunk(S, q, k, v, lg):
    C = q.shape[1]
    i = jnp.arange(C, dtype=jnp.float32)
    diff = i[:, None] - i[None, :]
    dmask = jnp.where(diff >= 0, jnp.exp(jnp.maximum(diff, 0.0)[None] * lg[:, None, None]), 0.0)
    qk = jnp.einsum('bihd,bjhd->bhij', q, k) * dmask[None]
    intra = jnp.einsum('bhij,bjhv->bihv', qk, v)
    inter = jnp.einsum('bihd,bhdv->bihv', q, S) * jnp.exp((i + 1.0)[:, None] * lg[None, :])[None, :, :, None]
    k_dec = k * jnp.exp((C - 1.0 - i)[:, None] * lg[None, :])[None, :, :, None]
    S_new = jnp.exp(C * lg)[None, :, None, None] * S + jnp.einsum('bjhd,bjhv->bhdv', k_dec, v)
    return intra + inter, S_new

def retention_mix(q_b, k_b, v_b, g_b, pos, S0, chunk):
    B, T = q_b.shape[:2]
    lg = jnp.log(1.0 - 2.0 ** (-5.0 - jnp.arange(H_B, dtype=jnp.float32)))
    q = rotate(q_b, pos)
    k = rotate(k_b, pos) * (DK_B ** -0.5)
    v = v_b.astype(jnp.float32)
    nc = T // chunk

    def to_chunks(a):
        return a.reshape(B, nc, chunk, *a.shape[2:]).swapaxes(0, 1)

    def step(S, inp):
        o, S_new = retention_chunk(S, inp[0], inp[1], inp[2], lg)
        return S_new, o

    S_fin, o = lax.scan(step, S0.astype(jnp.float32), (to_chunks(q), to_chunks(k), to_chunks(v)))
    o = o.swapaxes(0, 1).reshape(B, T, H_B, DV_B)
    mu = jnp.mean(o, axis=-1, keepdims=True)
    var = jnp.mean(jnp.square(o - mu), axis=-1, keepdims=True)
    o = ((o - mu) * lax.rsqrt(var + EPS)).reshape(B, T, W_B)
    return jax.nn.silu(g_b.astype(jnp.float32)) * o, S_fin

def peer(h, w_query, keys1, keys2, exp_u, exp_v):
    T = h.shape[0]
    q = (h @ w_query).reshape(T, PEER_HEADS, 2, D_PHALF).astype(jnp.float32)
    s1 = jnp.einsum('thd,nd->thn', q[:, :, 0], keys1.astype(jnp.float32))
    s2 = jnp.einsum('thd,nd->thn', q[:, :, 1], keys2.astype(jnp.float32))
    v1, i1 = lax.top_k(s1, PEER_TOPK)
    v2, i2 = lax.top_k(s2, PEER_TOPK)
    cand_s = (v1[..., :, None] + v2[..., None, :]).reshape(T, PEER_HEADS, PEER_TOPK * PEER_TOPK)
    cand_i = (i1[..., :, None] * N_KEYS + i2[..., None, :]).reshape(T, PEER_HEADS, PEER_TOPK * PEER_TOPK)
    top_s, sel = lax.top_k(cand_s, PEER_TOPK)
    e_idx = jnp.take_along_axis(cand_i, sel, axis=-1)
    gate = jax.nn.softmax(top_s, axis=-1)
    u = exp_u[e_idx]
    act = jax.nn.gelu(jnp.einsum('thkd,td->thk', u, h).astype(jnp.float32), approximate=False)
    return jnp.einsum('thk,thkd->td', (gate * act).astype(h.dtype), exp_v[e_idx])

def layer_prompt(x, ln1_g, w_in, w_out, ln2_g, pq, pk1, pk2, pu, pv):
    B, T, _ = x.shape
    pos = jnp.arange(T, dtype=jnp.int32)
    h = rmsnorm(x, ln1_g)
    q_a, k_a, v_a, q_i, k_i, w_i, q_b, k_b, v_b, g_b = project(h, w_in)
    o_a = dsa_prompt(q_a, q_i, w_i, k_a, v_a, k_i)
    S0 = jnp.zeros((B, H_B, DK_B, DV_B), jnp.float32)
    o_b, S_fin = retention_mix(q_b, k_b, v_b, g_b, pos, S0, CHUNK)
    x = x + jnp.concatenate([o_a, o_b.astype(x.dtype)], axis=-1) @ w_out
    h2 = rmsnorm(x, ln2_g)
    nb = (B * T) // TOK_BLOCK
    f = lax.map(lambda hb: peer(hb, pq, pk1, pk2, pu, pv), h2.reshape(nb, TOK_BLOCK, D_MODEL))
    x = x + f.reshape(B, T, D_MODEL)
    return x, k_a, v_a, k_i, S_fin.astype(x.dtype)

def layer_sample(x, ck, cv, cki, cs, ln1_g, w_in, w_out, ln2_g, pq, pk1, pk2, pu, pv):
    B, T, _ = x.shape
    P = ck.shape[1]
    pos = P + jnp.arange(T, dtype=jnp.int32)
    h = rmsnorm(x, ln1_g)
    q_a, k_a, v_a, q_i, k_i, w_i, q_b, k_b, v_b, g_b = project(h, w_in)
    o_a = dsa_sample(q_a, q_i, w_i, k_a, v_a, k_i, ck, cv, cki)
    o_b, S_new = retention_mix(q_b, k_b, v_b, g_b, pos, cs, T)
    x = x + jnp.concatenate([o_a, o_b.astype(x.dtype)], axis=-1) @ w_out
    h2 = rmsnorm(x, ln2_g)
    f = peer(h2.reshape(B * T, D_MODEL), pq, pk1, pk2, pu, pv)
    x = x + f.reshape(B, T, D_MODEL)
    return x, k_a, v_a, k_i, S_new.astype(cs.dtype)

def setup_inputs(seed: int = 0) -> dict:
    key = jax.random.key(seed)
    ks = jax.random.split(key, 16)

    def nrm(k, shape, s):
        return jax.random.normal(k, shape, jnp.float32) * s

    return {
        'x_prompt': nrm(ks[0], (BATCH, SEQ, D_MODEL), 1.0),
        'x_sample': nrm(ks[1], (DEC_BATCH, DEC_SEQ, D_MODEL), 1.0),
        'cache_attn_k': nrm(ks[2], (DEPTH, DEC_BATCH, PAST_LEN, KVH_A, DH_A), 1.0),
        'cache_attn_v': nrm(ks[3], (DEPTH, DEC_BATCH, PAST_LEN, KVH_A, DH_A), 1.0),
        'cache_idx_k': nrm(ks[4], (DEPTH, DEC_BATCH, PAST_LEN, D_IDX), 1.0),
        'state_retention': nrm(ks[5], (DEPTH, DEC_BATCH, H_B, DK_B, DV_B), 0.5),
        'ln1_g': 1.0 + nrm(ks[6], (DEPTH, D_MODEL), 0.02),
        'w_in': nrm(ks[7], (DEPTH, D_MODEL, D_IN), D_MODEL ** -0.5),
        'w_out': nrm(ks[8], (DEPTH, D_MIX, D_MODEL), D_MIX ** -0.5),
        'ln2_g': 1.0 + nrm(ks[9], (DEPTH, D_MODEL), 0.02),
        'peer_w_query': nrm(ks[10], (DEPTH, D_MODEL, PEER_HEADS * D_PKEY), D_MODEL ** -0.5),
        'peer_keys1': nrm(ks[11], (DEPTH, N_KEYS, D_PHALF), D_PHALF ** -0.5),
        'peer_keys2': nrm(ks[12], (DEPTH, N_KEYS, D_PHALF), D_PHALF ** -0.5),
        'peer_u': nrm(ks[13], (DEPTH, N_EXPERTS, D_MODEL), D_MODEL ** -0.5),
        'peer_v': nrm(ks[14], (DEPTH, N_EXPERTS, D_MODEL), PEER_HEADS ** -0.5),
        'ln_final_g': 1.0 + nrm(ks[15], (D_MODEL,), 0.02),
    }

def reference(x_prompt, x_sample, cache_attn_k, cache_attn_v, cache_idx_k, state_retention,
              ln1_g, w_in, w_out, ln2_g, peer_w_query, peer_keys1, peer_keys2, peer_u, peer_v, ln_final_g):
    xp = x_prompt
    xs = x_sample
    kp, vp, kip, sp = [], [], [], []
    ksm, vsm, kism, ssm = [], [], [], []
    for l in range(DEPTH):
        xp, k_a, v_a, k_i, S_p = layer_prompt(xp, ln1_g[l], w_in[l], w_out[l], ln2_g[l], peer_w_query[l],
                                              peer_keys1[l], peer_keys2[l], peer_u[l], peer_v[l])
        kp.append(k_a)
        vp.append(v_a)
        kip.append(k_i)
        sp.append(S_p)
        xs, k_s, v_s, ki_s, S_s = layer_sample(xs, cache_attn_k[l], cache_attn_v[l], cache_idx_k[l],
                                               state_retention[l], ln1_g[l], w_in[l], w_out[l], ln2_g[l],
                                               peer_w_query[l], peer_keys1[l], peer_keys2[l], peer_u[l], peer_v[l])
        ksm.append(k_s)
        vsm.append(v_s)
        kism.append(ki_s)
        ssm.append(S_s)
    y_prompt = rmsnorm(xp, ln_final_g)
    y_sample = rmsnorm(xs, ln_final_g)
    return (y_prompt, y_sample,
            jnp.stack(kp), jnp.stack(vp), jnp.stack(kip), jnp.stack(sp),
            jnp.stack(ksm), jnp.stack(vsm), jnp.stack(kism), jnp.stack(ssm))


_drawn_inputs = setup_inputs


def setup_inputs(seed=0):
    import zlib

    import numpy as np

    out = dict(_drawn_inputs(seed))
    spreads = {}
    factors = {}
    for name, (base, spread) in spreads.items():
        noise = np.random.default_rng([zlib.crc32(name.encode()), seed]).standard_normal(out[name].shape)
        drawn = base * np.exp(spread * noise) if base else spread * noise
        out[name] = jnp.asarray(drawn.astype(out[name].dtype))
    for name, factor in factors.items():
        out[name] = (out[name] * factor).astype(out[name].dtype)
    return out
```

```python
from contextlib import ExitStack

import numpy as np

import concourse.bass as bass
from concourse import mybir

F32 = mybir.dt.float32
BF16 = mybir.dt.bfloat16
U32 = mybir.dt.uint32
ALU = mybir.AluOpType
ACT = mybir.ActivationFunctionType
AX = mybir.AxisListType

P = 128
D = 1024
KC = D // P
TILES = 3
NTOK = TILES * P
STREAMS, STEPS, PAST = 8, 16, 512
HA, KVH, GRP, DH = 8, 2, 4, 64
HI = 8
HB, DK, DV = 4, 64, 128
CHUNK = 64
TOPK = (64, 64, 132)
KEYS = (128, 256, 640)
NKV = 2 * P + DH + HI
HP, KP, NK = 8, 16, 128
UNITS = TILES * HP
G = 8
GROUPS = KP // G
EPS = 1e-6
TAKEN = -3.39e38
BARRED = -3.0e38
OFF = -1.0e30
LG = [float(np.log(np.float32(1.0) - np.float32(2.0) ** np.float32(-5.0 - h))) for h in range(HB)]


def constants():
    t = np.arange(P)
    pos = np.stack([t, P + t, PAST + t % STEPS]).astype(np.float32)
    inv = (1.0 / (np.float32(10000.0) ** np.linspace(0.0, 1.0, DK // 2, dtype=np.float32))).astype(np.float32)
    ang = (pos[:, :, None] * inv).astype(np.float32)
    cs = np.stack([np.cos(ang), np.sin(ang)], 1)
    cs = np.stack([cs, cs * np.float32(DK ** -0.5)], 2)
    c = {"cs": cs.transpose(3, 0, 1, 2, 4).reshape(P, -1)}
    lg = np.array(LG)
    kd = np.exp((2 * P - 1 - (np.arange(2)[None, :, None] * P + t[:, None, None])) * lg)
    own = (t[:, None] // STEPS == np.arange(STREAMS)[None, :])
    kds = own[:, :, None] * np.exp((STEPS - 1 - t % STEPS)[:, None, None] * lg)
    c["kd"] = np.concatenate([kd.reshape(P, -1), kds.reshape(P, -1)], 1)
    diff = t[None, :] - t[:, None]
    near = np.where(diff[:, None, :] >= 0, np.exp(np.maximum(diff, 0)[:, None, :] * lg[None, :, None]), 0.0)
    far = np.exp((diff + P)[:, None, :] * lg[None, :, None])
    c["dmask"] = np.concatenate([near, far], 2).reshape(P, -1)
    same = (t[None, :] // STEPS == t[:, None] // STEPS)
    c["dmask_s"] = (near * same[:, None, :]).reshape(P, -1)
    half = (t // STEPS % 2)[None, :] == (t[:, None] // DK)
    c["qmask"] = (half[:, None, :] * np.exp((t % STEPS + 1)[None, None, :] * lg[None, :, None])).reshape(P, -1)
    causal = np.where(t[None, :] // CHUNK <= t[:, None] // CHUNK, 0.0, BARRED)
    c["bar"] = np.concatenate([causal, np.where(same, 0.0, BARRED)], 1)
    e8 = np.zeros((P, P))
    e8[DH:DH + HI] = (np.arange(HI)[:, None] == t[None, :] // STEPS)
    c["e8"] = e8
    c["m16"] = (t[:, None] % STEPS == np.arange(STEPS)[None, :])
    c["iota"] = np.broadcast_to(np.arange(KP), (P, KP))
    c["ident"] = np.eye(P)
    c["half"] = np.full((P, HB), -0.5)
    return {k: np.ascontiguousarray(v, dtype=np.float32) for k, v in c.items()}


def build(nc, a, o):
    with ExitStack() as ctx:
        def sb(name, shape, dt=F32):
            return ctx.enter_context(nc.sbuf_tensor(name, shape, dt))

        def sem(name):
            return ctx.enter_context(nc.semaphore(name))

        x = sb("x", [P, TILES, D])
        ident = sb("ident", [P, P])
        ident_bf = sb("ident_bf", [P, P], BF16)
        keysT = sb("keysT", [P, 2, NK])
        ids = sb("ids", [P, UNITS * KP], U32)
        gates = sb("gates", [P, UNITS * KP])
        cs = sb("cs", [P, TILES, 2, 2, DK // 2])
        kd = sb("kd", [P, 2 * HB + STREAMS * HB])
        g2b = sb("g2b", [P, D])
        dmask = sb("dmask", [P, HB, 2 * P])
        qmask = sb("qmask", [P, HB, P])
        e8 = sb("e8", [P, P])
        m16 = sb("m16", [P, STEPS])
        iota = sb("iota", [P, KP])
        half4 = sb("half4", [P, HB])
        stage = sb("stage", [P, 2, G], U32)
        zdot = sb("zdot", [P, G])
        zact = sb("zact", [P, G])
        sumsq, ms, rstd = sb("sumsq", [P, 9]), sb("ms", [P, 9]), sb("rstd", [P, 9])
        bn6, mv = sb("bn6", [P, 6]), sb("mv", [P, HB, 2])
        veps, rstd4 = sb("veps", [P, HB]), sb("rstd4", [P, HB])
        rowmax, negmax = sb("rowmax", [P, 2]), sb("negmax", [P, 2, 2])
        esum, resum = sb("esum", [P, 2, 2]), sb("resum", [P, 2])
        top8 = sb("top8", [P, 8])
        negbest, gsum, rgsum = sb("negbest", [P, 1]), sb("gsum", [P, 2]), sb("rgsum", [P, 1])
        rows = sb("rows", [P, G, 2 * D])
        wt = sb("wt", [P, 6, KC * 512])
        work = sb("work", [P, 4608])
        ps = ctx.enter_context(nc.psum_tensor("ps", [P, 8, 512], F32))
        psf = ps[:, :, :].rearrange("p b n -> p (b n)")

        rowf = rows[:, :, :].rearrange("p g n -> p (g n)")
        wtf = wt[:, :, :].rearrange("p s n -> p (s n)")
        SLOT = KC * 512

        def at(region, off, n):
            return region[:, off:off + n]

        hT = at(rowf, 0, KC * NTOK).rearrange("p (c t) -> p c t", c=KC)
        hnat = at(rowf, 3072, 2 * D).rearrange("p (b n) -> p b n", b=2)
        g1b = at(rowf, 5120, D)
        qaT = at(rowf, 6144, GRP * NTOK).rearrange("p (g t) -> p g t", g=GRP)
        qiT = at(rowf, 7680, HI * NTOK).rearrange("p (g h t) -> p g h t", h=HI, t=STEPS)
        kaT = at(rowf, 10752, NTOK)
        kiwT = at(rowf, 11136, NTOK)
        biasb = at(rowf, 11520, 512).bitcast(BF16)
        bias = (biasb[:, 0:128], biasb[:, 128:384], biasb[:, 384:1024])
        mixT = at(rowf, 12288, KC * NTOK).rearrange("p (c t) -> p c t", c=KC)
        kvnat = at(rowf, 15360, TILES * NKV).rearrange("p (t n) -> p t n", t=TILES)
        qz = at(rowf, 0, HB * 640).rearrange("p (h n) -> p h n", h=HB)
        qzb = at(rowf, 2560, D).rearrange("p (b k g t) -> p b k g t", b=STREAMS, k=KVH, g=GRP)
        kdn = at(rowf, 3584, 512).rearrange("p (t h d) -> p t h d", t=2, h=HB)
        mixnat = at(rowf, 4096, TILES * 512).rearrange("p (t n) -> p t n", t=TILES)
        rotq2 = at(rowf, 5632, 512).rearrange("p (h b e d) -> p h b e d", h=HB, b=2, e=2)
        WZ = 8 * 144
        wz = at(wtf, 0, TILES * WZ).rearrange("p (t n) -> p t n", t=TILES)
        relu = at(wtf, 3456, 2 * 640).rearrange("p (b n) -> p b n", b=2)
        score = at(wtf, 4736, 640)
        cki = at(wtf, 5376, 2 * PAST).rearrange("p (b n) -> p b n", b=2)
        bar = at(wtf, 6400, 2 * P)
        kz = at(wtf, 2 * SLOT, 2048).rearrange("p (q h e d) -> p q h e d", q=4, h=HB, e=2)
        s0 = at(wtf, 2 * SLOT + 2048, 2048).rearrange("p (q h v) -> p q h v", q=4, h=HB)
        snew = at(wtf, 3 * SLOT, 2048).rearrange("p (q h v) -> p q h v", q=4, h=HB)
        prob = at(wtf, 3 * SLOT + 2048, 1280).rearrange("p (b n) -> p b n", b=2)
        selb = at(wtf, 3 * SLOT + 3328, 512).bitcast(BF16).rearrange("p (b k t) -> p b k t", b=STREAMS, k=8)
        snp = at(wtf, 3 * SLOT + 3840, 256).rearrange("p (q v) -> p q v", q=2)
        ckv = at(wtf, 4 * SLOT, 2048).rearrange("p (b k n) -> p b k n", b=2, k=2)
        probT = at(wtf, 4 * SLOT + 2048, 1280).rearrange("p (b n) -> p b n", b=2)
        dmask_s = at(wtf, 4 * SLOT + 3328, 512)
        rT = at(wtf, 5 * SLOT, 1024).rearrange("p (t s n) -> p t s n", t=2, s=4)
        qTd = at(wtf, 5 * SLOT + 1024, 512).rearrange("p (h t) -> p h t", h=HB)
        kTs = at(wtf, 5 * SLOT + 1536, 256).rearrange("p (s t) -> p s t", s=2)
        am0 = at(wtf, 5 * SLOT + 1792, 1024).rearrange("p (h i) -> p h i", h=HB)
        am1 = at(wtf, 5 * SLOT + 2816, 512).rearrange("p (h i) -> p h i", h=HB)
        am2 = at(wtf, 5 * SLOT + 3328, 512).rearrange("p (h i) -> p h i", h=HB)
        diag = at(wtf, 0, G * P).rearrange("p (g n) -> p g n", g=G)
        gfb = at(wtf, 2048, D)
        vb = at(work, 0, TILES * 512).rearrange("p (t n) -> p t n", t=TILES)
        gs = at(work, 1536, TILES * 512).rearrange("p (t n) -> p t n", t=TILES)
        rot = at(work, 3072, TILES * 512).rearrange("p (t h e d) -> p t h e d", t=TILES, h=2 * HB, e=2)
        h2 = (at(work, 0, D), at(wtf, 1024, D))
        h2T = at(work, 1024, D).rearrange("p (c t) -> p c t", c=KC)
        qT = at(work, 2048, 512).rearrange("p (b e t) -> p b e t", b=2, e=2)
        rest = at(work, 2560, P)
        cand = at(work, 2688, 256)
        cand2 = at(work, 2944, 256)
        hot = at(work, 3200, 512).rearrange("p (e k r) -> p e k r", e=2, k=KP)
        hoti = at(work, 3712, 512).rearrange("p (e k r) -> p e k r", e=2, k=KP)
        top = at(work, 4224, 32).rearrange("p (e k) -> p e k", e=2)
        topi = at(work, 4256, 32).bitcast(U32).rearrange("p (e k) -> p e k", e=2)
        topf = at(work, 4288, 32).rearrange("p (e k) -> p e k", e=2)
        best = at(work, 4320, KP)
        besti = at(work, 4336, KP).bitcast(U32)
        rank = at(work, 4352, 32).bitcast(U32).rearrange("p (e k) -> p e k", e=2)
        rankf = at(work, 4384, 32).rearrange("p (e k) -> p e k", e=2)
        half_id = at(work, 4416, 32).rearrange("p (e k) -> p e k", e=2)
        ebest = at(work, 4448, 2 * KP).rearrange("p (b k) -> p b k", b=2)
        NAMES = ["kv", "qi", "qa", "vb", "gb", "qkb", "out0", "out1", "q0", "q1", "q2", "q3"]
        w_in = {n: sem("w_" + n) for n in NAMES}
        x_in = [sem(f"x_in{t}") for t in range(TILES)]
        g1_in, ident_in, small_in, bar_in, keys_in = (sem(n) for n in ("g1_in", "ident_in", "small_in", "bar_in", "keys_in"))
        gf_in, s0_in, dms_in = sem("gf_in"), sem("s0_in"), sem("dms_in")
        cki_in = [sem(f"cki_in{i}") for i in range(2)]
        ckv_in = [sem(f"ckv_in{i}") for i in range(2)]
        out_done = sem("out_done")
        sqd, msd, rsd, hready, x1_done = (sem(n) for n in ("squares", "mean_square", "rstd", "h_ready", "x1_done"))
        ht_ps, ht_act, ht_dve = sem("ht_ps"), sem("ht_act"), sem("ht_dve")
        proj, proj_act, proj_dve = sem("proj"), sem("proj_act"), sem("proj_dve")
        kt_ps, kt_sb = sem("kt_ps"), sem("kt_sb")
        w_ps, wz_zero, wz_set = sem("w_ps"), sem("wz_zero"), sem("wz_set")
        dots, relued, combined, scored, biased = (sem(n) for n in ("dots", "relued", "combined", "scored", "biased"))
        rt_ps, rt_sb, s_ps, s_masked = sem("rt_ps"), sem("rt_sb"), sem("s_ps"), sem("s_masked")
        zeroed, kdec, qz_set, qzb_set, sel_set = (sem(n) for n in ("zeroed", "kdec", "qz_set", "qzb_set", "sel_set"))
        o_ps, o_norm, o_var, o_rstd, sp_ps, sp_sb, ss_ps, ss_sb = (sem(n) for n in (
            "o_ps", "o_norm", "o_var", "o_rstd", "sp_ps", "sp_sb", "ss_ps", "ss_sb"))
        mt_ps, mt_sb, q_twice = sem("mt_ps"), sem("mt_sb"), sem("q_twice")
        sc_ps, smax, expd, pscaled, pt_ps, pt_sb, pv_ps, pv_sb = (sem(n) for n in (
            "sc_ps", "smax", "expd", "pscaled", "pt_ps", "pt_sb", "pv_ps", "pv_sb"))
        wout, h2t_ps, h2t_act, h2t_dve = sem("wout"), sem("h2t_ps"), sem("h2t_act"), sem("h2t_dve")
        q_ps, q_sb, sc2_ps, topped, best_set, gexp, picked = (sem(n) for n in (
            "q_ps", "q_sb", "sc2_ps", "topped", "best_set", "gexp", "picked"))
        staged, seen, dotted, gelued, diagd, acc, y_init, y_read, y_out = (sem(n) for n in (
            "staged", "seen", "dotted", "gelued", "diagd", "acc", "y_init", "y_read", "y_out"))
        landed = [sem(f"landed{s}") for s in range(G)]
        chain = sem("dve_chain")

        slot_of = {"kv": 0, "qi": 1, "qa": 2, "vb": 3, "gb": 4, "qkb": 5, "out0": 0, "out1": 1,
                   "q0": 2, "q1": 3, "q2": 4, "q3": 5}
        width = {"kv": NKV}

        def wv(name):
            w = width.get(name, 512)
            return wt[:, slot_of[name], 0:KC * w].rearrange("p (c n) -> p c n", c=KC)

        def load_w(eng, name):
            w = width.get(name, 512)
            eng.dma_start(wt[:, slot_of[name], 0:KC * w], a["w_" + name]).then_inc(w_in[name], 16)

        UN = ([("kv", "n", t) for t in range(TILES)] + [("qi", "t", j) for j in range(4)]
              + [("qa", "t", g) for g in range(GRP)] + [("vb", "n", t) for t in range(TILES)]
              + [("gb", "n", t) for t in range(TILES)] + [("qkb", "n", t) for t in range(TILES)])
        N_ACT = 17
        ATT = [(t, g) for t in range(2) for g in range(GRP)] + [(2, b) for b in range(STREAMS)]

        block = ctx.enter_context(nc.Block())

        @block.sync
        def _(sp):
            sp.dma_start(x[:, 0, :], a["x"][0]).then_inc(x_in[0], 16)
            sp.dma_start(g1b, a["ln1_g"].partition_broadcast(P)).then_inc(g1_in, 16)
            sp.dma_start(ident[:], a["ident"]).then_inc(ident_in, 16)
            sp.dma_start(half4[:], a["half"]).then_inc(ident_in, 16)
            for t in (1, 2):
                sp.dma_start(x[:, t, :], a["x"][t]).then_inc(x_in[t], 16)
            load_w(sp, "kv")
            load_w(sp, "qi")
            for name, dst in (("e8", e8[:]), ("m16", m16[:]), ("iota", iota[:]), ("kd", kd[:]),
                              ("cs", cs[:, :, :, :, :].rearrange("p a b c d -> p (a b c d)")),
                              ("dmask", dmask[:, :, :].rearrange("p a b -> p (a b)")),
                              ("qmask", qmask[:, :, :].rearrange("p a b -> p (a b)"))):
                sp.dma_start(dst, a[name]).then_inc(small_in, 16)
            for name in ("qa", "vb", "gb", "qkb"):
                load_w(sp, name)
            sp.dma_start(keysT[:, :, :].rearrange("p a b -> p (a b)"), a["keysT"]).then_inc(keys_in, 16)
            sp.dma_start(g2b[:], a["ln2_g"].partition_broadcast(P)).then_inc(keys_in, 16)
            sp.wait_ge(proj, 7)
            sp.dma_start(bar, a["bar"]).then_inc(bar_in, 16)
            sp.wait_ge(proj, 11)
            for e in range(2):
                sp.dma_start(s0[64 * e:64 * e + 64, :, :, :], a["s0"][e]).then_inc(s0_in, 16)
            sp.wait_ge(proj, 17)
            sp.dma_start(dmask_s, a["dmask_s"]).then_inc(dms_in, 16)
            sp.wait_ge(biased, 3)
            load_w(sp, "out0")
            load_w(sp, "out1")
            sp.wait_ge(proj_act, 3)
            for t in range(TILES):
                for k, (c0, c1) in enumerate(((0, P), (P, 2 * P), (2 * P, 2 * P + DH))):
                    sp.dma_start(o["kv"][t][k], kvnat[:, t, c0:c1]).then_inc(out_done, 16)
            sp.wait_ge(sp_sb, 2)
            sp.dma_start(o["state_p"], snp).then_inc(out_done, 16)
            sp.wait_ge(ss_sb, HB)
            for e in range(2):
                sp.dma_start(o["state_s"][e], snew[64 * e:64 * e + 64, :, :, :]).then_inc(out_done, 16)
            sp.wait_ge(out_done, 16 * 12)
            sp.wait_ge(pv_sb, 2 * len(ATT))
            sp.wait_ge(mt_sb, TILES)
            for j in range(4):
                load_w(sp, f"q{j}")
            sp.wait_ge(wout, TILES)
            sp.dma_start(gfb, a["ln_final_g"].partition_broadcast(P)).then_inc(gf_in, 16)
            for t in range(TILES):
                sp.wait_ge(y_out, t + 1)
                sp.dma_start(o["y"][t], x[:, t, :]).then_inc(out_done, 16)
            sp.wait_ge(out_done, 16 * 15)

        @block.gpsimd
        def _(pool):
            def take_rstd(n):
                pool.wait_ge(msd, n + 1)
                pool.tensor_tensor(rstd[:, n:n + 1], ms[:, n:n + 1], half4[:, 0:1], ALU.pow).then_inc(rsd, 1)

            pool.wait_ge(ident_in, 32)
            for n in range(TILES):
                take_rstd(n)
            pool.wait_ge(proj, 3)
            pool.memset(at(wtf, 0, TILES * WZ), 0.0).then_inc(wz_zero, 1)
            pool.wait_ge(proj, 7)
            for b in range(STREAMS):
                if b >= 2:
                    pool.wait_ge(dots, 16 + b - 1)
                pool.dma_start(cki[0:DH, b % 2, :], a["cki"][b]).then_inc(cki_in[b % 2], 16)
            pool.wait_ge(proj, len(UN))
            pool.memset(at(rowf, 0, 3584), 0.0).then_inc(zeroed, 1)
            for b in range(2):
                for k in range(2):
                    pool.dma_start(ckv[:, b, k, :], a["ckv"][b][k]).then_inc(ckv_in[b], 16)
            for t in range(TILES):
                pool.wait_ge(o_var, t + 1)
                pool.tensor_tensor(rstd4[:], veps[:], half4[:], ALU.pow).then_inc(o_rstd, 1)
            for b in range(2, STREAMS):
                pool.wait_ge(pv_ps, 8 + b - 1)
                for k in range(2):
                    pool.dma_start(ckv[:, b % 2, k, :], a["ckv"][b][k]).then_inc(ckv_in[b % 2], 16)
            for n in range(TILES, 2 * TILES):
                take_rstd(n)

            def gathers(par, g, unit, first=False):
                pool.wait_ge(picked, unit + 1)
                if not first:
                    pool.sem_inc(seen)
                pool.tensor_copy(stage[:, par, :], ids[:, bass.ds(g * G, G)]).then_inc(staged, 1)
                for s in range(G):
                    if s == 0:
                        pool.wait_ge(staged, g + 1)
                        if first:
                            pool.wait_ge(wout, TILES)
                            pool.wait_ge(out_done, 16 * 12)
                    if not first:
                        pool.wait_ge(acc, (g - 1) * G + s + 1)
                    pool.sem_inc(seen)
                    pool.indirect_dma_start(rows[:, s, :], None, a["uv"], bass.IndirectOffsetOnAxis(
                        ap=stage[:, par, s:s + 1], axis=0)).then_inc(landed[s], 16)

            def span(g0, g1):
                pairs = (g1 - g0) // 2
                with pool.Fori(0, pairs) as i:
                    gathers(1, i * 2 + g0, i + (g0 - 1) // 2)
                    gathers(0, i * 2 + (g0 + 1), i + (g0 + 1) // 2)
                if (g1 - g0) % 2:
                    gathers(1, g1 - 1, (g1 - 1) // 2)

            per_tile = HP * GROUPS
            gathers(0, 0, 0, first=True)
            span(1, per_tile + 5)
            take_rstd(2 * TILES)
            span(per_tile + 5, 2 * per_tile + 5)
            take_rstd(2 * TILES + 1)
            span(2 * per_tile + 5, 3 * per_tile)
            take_rstd(2 * TILES + 2)

        @block.tensor
        def _(pe):
            def mm(out, lhsT, rhs, start=True, stop=True):
                return nc.tensor.matmul(out, lhsT, rhs, start=start, stop=stop)

            def tr(out, in_, k=P):
                return nc.tensor.transpose(out, in_, ident[0:k, 0:k])

            pe.wait_ge(ident_in, 32)
            for t in range(TILES):
                pe.wait_ge(hready, t + 1)
                if t == 2:
                    pe.wait_ge(ht_act, 1)
                    pe.wait_ge(ht_dve, 1)
                for c in range(KC):
                    last = tr(ps[:, 2 * (t % 2) + c // 4, (c % 4) * P:(c % 4 + 1) * P], hnat[:, t % 2, c * P:(c + 1) * P])
                last.then_inc(ht_ps, 1)

            def unit(n):
                name, kind, i = UN[n]
                if i == 0:
                    pe.wait_ge(w_in[name], 16)
                if n == 0:
                    pe.wait_ge(ht_act, TILES)
                    pe.wait_ge(ht_dve, TILES)
                if n >= 2:
                    if n - 2 < N_ACT:
                        pe.wait_ge(proj_act, n - 1)
                    else:
                        pe.wait_ge(proj_dve, n - 1 - N_ACT)
                w, bank = wv(name), 6 + n % 2
                for c in range(KC):
                    if kind == "n":
                        last = mm(ps[:, bank, 0:width.get(name, 512)], hT[:, c, i * P:(i + 1) * P], w[:, c, :],
                                  c == 0, c == KC - 1)
                    else:
                        last = mm(ps[:, bank, 0:NTOK], w[:, c, i * P:(i + 1) * P], hT[:, c, :], c == 0, c == KC - 1)
                last.then_inc(proj, 1)

            for n in range(3):
                unit(n)
            pe.wait_ge(proj_act, 3)
            for t in range(TILES):
                tr(ps[:, 0, t * P:(t + 1) * P], kvnat[:, t, 0:P])
                last = tr(ps[0:DH + HI, 1, t * P:(t + 1) * P], kvnat[:, t, 2 * P:NKV])
            last.then_inc(kt_ps, 1)
            for n in range(3, 7):
                unit(n)
            pe.wait_ge(kt_sb, 2)
            pe.wait_ge(small_in, 16 * 7)
            mm(ps[:, 2, 0:NTOK], e8[DH:DH + HI, :], kiwT[DH:DH + HI, :]).then_inc(w_ps, 1)

            def index_dots(m):
                t, g = divmod(m, 8)
                if m == 0:
                    pe.wait_ge(proj_act, 7)
                if m == 1:
                    pe.wait_ge(wz_set, TILES)
                if m >= 2:
                    pe.wait_ge(relued, m - 1)
                lhs = qiT[0:DH, m, :, :]
                b = 2 * (m % 2)
                if t < 2:
                    last = mm(ps[:, b, 0:KEYS[t]], lhs, kiwT[0:DH, 0:KEYS[t]])
                else:
                    pe.wait_ge(cki_in[g % 2], 16 * (g // 2 + 1))
                    mm(ps[:, b, :], lhs, cki[0:DH, g % 2, :])
                    last = mm(ps[:, b + 1, 0:P], lhs, kiwT[0:DH, 2 * P:3 * P])
                last.then_inc(dots, 1)

            def index_sum(m):
                t, g = divmod(m, 8)
                if m == 0:
                    pe.wait_ge(wz_set, TILES)
                if g == 0 and t > 0:
                    pe.wait_ge(scored, t)
                pe.wait_ge(relued, m + 1)
                lhs = wz[:, t, g * P:(g + 1) * P]
                if t < 2:
                    last = mm(ps[:, 4, 0:KEYS[t]], lhs, relu[:, m % 2, 0:KEYS[t]], g == 0, g == 7)
                else:
                    mm(ps[:, 4, :], lhs, relu[:, m % 2, 0:512], g == 0, g == 7)
                    last = mm(ps[:, 5, 0:P], lhs, relu[:, m % 2, 512:640], g == 0, g == 7)
                last.then_inc(combined, 1)

            for m in range(25):
                if m < 24:
                    index_dots(m)
                if m >= 1:
                    index_sum(m - 1)
            for n in range(7, len(UN)):
                unit(n)

            pe.wait_ge(relued, 24)
            for t in range(2):
                pe.wait_ge(proj_dve, t + 1)
                for s in range(4):
                    last = tr(ps[:, t, s * P:(s + 1) * P], rot[:, t, 2 * s:2 * s + 2, :, :])
                last.then_inc(rt_ps, 1)
            pe.wait_ge(q_twice, 2)
            for h in range(HB):
                last = tr(ps[:, 2, h * P:(h + 1) * P], rotq2[:, h, :, :, :])
            last.then_inc(rt_ps, 1)
            for s in range(2):
                last = tr(ps[:, 3, s * P:(s + 1) * P], rot[:, 2, HB + 2 * s:HB + 2 * s + 2, :, :])
            last.then_inc(rt_ps, 1)
            pe.wait_ge(rt_sb, 4)
            pe.wait_ge(scored, 3)
            for h in range(HB):
                r = slice(64 * (h % 2), 64 * (h % 2) + 64)
                last = mm(ps[:, 4 + h % 2, (h // 2) * 256:(h // 2) * 256 + 256],
                          rT[r, 0, 2 + h // 2, :], rT[r, :, h // 2, :])
            last.then_inc(s_ps, 1)
            for h in range(HB):
                r = slice(64 * (h % 2), 64 * (h % 2) + 64)
                last = mm(ps[:, 6 + h % 2, (h // 2) * P:(h // 2 + 1) * P], rT[r, 1, 2 + h // 2, :], rT[r, 1, h // 2, :])
            last.then_inc(s_ps, 1)
            for h in range(HB):
                r = slice(64 * (h % 2), 64 * (h % 2) + 64)
                last = mm(ps[:, 6 + h % 2, (2 + h // 2) * P:(3 + h // 2) * P], kTs[r, h // 2, :], qTd[r, h, :])
            last.then_inc(s_ps, 1)
            pe.wait_ge(s_masked, 3)
            for h in range(HB):
                last = mm(ps[:, 0, h * P:(h + 1) * P], am0[:, h, 0:P], vb[:, 0, h * P:(h + 1) * P])
            last.then_inc(o_ps, 1)
            for h in range(HB):
                mm(ps[:, 1, h * P:(h + 1) * P], am0[:, h, P:2 * P], vb[:, 0, h * P:(h + 1) * P], True, False)
                last = mm(ps[:, 1, h * P:(h + 1) * P], am1[:, h, :], vb[:, 1, h * P:(h + 1) * P], False, True)
            last.then_inc(o_ps, 1)
            pe.wait_ge(s_masked, 4)
            pe.wait_ge(qz_set, HB)
            pe.wait_ge(s0_in, 32)
            for h in range(HB):
                mm(ps[:, 2, h * P:(h + 1) * P], am2[:, h, :], vb[:, 2, h * P:(h + 1) * P], True, False)
                for q in range(4):
                    last = mm(ps[:, 2, h * P:(h + 1) * P], qz[:, h, q * P:(q + 1) * P], s0[:, q, h, :], False, q == 3)
            last.then_inc(o_ps, 1)
            pe.wait_ge(kdec, 2 + STREAMS)
            for q in range(2):
                for t in range(2):
                    last = mm(ps[:, 3, q * 256:(q + 1) * 256], kdn[:, t, 2 * q:2 * q + 2, :],
                              vb[:, t, q * 256:(q + 1) * 256], t == 0, t == 1)
            last.then_inc(sp_ps, 1)
            for q in range(4):
                for h in range(HB):
                    last = mm(ps[:, 4 + q, h * P:(h + 1) * P], kz[:, q, h, :, :], vb[:, 2, h * P:(h + 1) * P])
            last.then_inc(ss_ps, 1)

            def att_scores(n):
                t, i = ATT[n]
                b = 2 * (n % 2)
                if n == 0:
                    pe.wait_ge(o_norm, TILES)
                    pe.wait_ge(sp_sb, 2)
                    pe.wait_ge(sel_set, 1)
                    pe.wait_ge(biased, TILES)
                if n >= 2:
                    pe.wait_ge(expd, n - 1)
                if t < 2:
                    for k in range(KVH):
                        r = slice(64 * k, 64 * k + 64)
                        out = ps[:, b + k, 0:KEYS[t]]
                        mm(out, qaT[r, i, t * P:(t + 1) * P], kaT[r, 0:KEYS[t]], True, False)
                        last = mm(out, ident_bf[:], bias[t], False, True)
                else:
                    if i == 0:
                        pe.wait_ge(qzb_set, 2)
                    pe.wait_ge(ckv_in[i % 2], 32 * (i // 2 + 1))
                    lhs = qzb[:, i, :, :, :]
                    mm(ps[:, b, :], lhs, ckv[:, i % 2, 0, :], True, False)
                    mm(ps[:, b, :], selb[:, i, :, :], bias[2][:, 0:512], False, True)
                    mm(ps[:, b + 1, 0:P], lhs, kaT[:, 2 * P:3 * P], True, False)
                    last = mm(ps[:, b + 1, 0:P], selb[:, i, :, :], bias[2][:, 512:640], False, True)
                last.then_inc(sc_ps, 1)

            def att_out(n):
                t, i = ATT[n]
                pe.wait_ge(pscaled, n + 1)
                if n == 0:
                    pe.wait_ge(ss_sb, HB)
                if n >= 1:
                    pe.wait_ge(pt_sb, n)
                if t < 2:
                    for c in range(t + 1):
                        for k in range(KVH):
                            last = tr(ps[:, 4, c * 256 + k * P:c * 256 + (k + 1) * P],
                                      prob[:, n % 2, k * 256 + c * P:k * 256 + (c + 1) * P])
                else:
                    for c in range(5):
                        last = tr(psf[:, 4 * 512 + c * P:4 * 512 + (c + 1) * P], prob[:, n % 2, c * P:(c + 1) * P])
                last.then_inc(pt_ps, 1)
                pe.wait_ge(pt_sb, n + 1)
                if n >= 1:
                    pe.wait_ge(pv_sb, 2 * n)
                if t < 2:
                    for c in range(t + 1):
                        last = mm(ps[:, 6, 0:256], kvnat[:, c, P:2 * P], probT[:, n % 2, c * 256:(c + 1) * 256], c == 0, c == t)
                else:
                    for c in range(5):
                        lhs = ckv[:, i % 2, 1, c * P:(c + 1) * P] if c < 4 else kvnat[:, 2, P:2 * P]
                        last = mm(ps[:, 6, 0:P], lhs, probT[:, n % 2, c * P:(c + 1) * P], c == 0, c == 4)
                last.then_inc(pv_ps, 1)

            def mix_t(t):
                if t == 0:
                    pe.wait_ge(ss_sb, HB)
                else:
                    pe.wait_ge(mt_sb, t)
                for c in range(4):
                    last = tr(ps[:, 7, c * P:(c + 1) * P], mixnat[:, t, c * P:(c + 1) * P])
                last.then_inc(mt_ps, 1)

            for n in range(len(ATT) + 1):
                if n < len(ATT):
                    att_scores(n)
                if n >= 1:
                    att_out(n - 1)
                if n in (2, 4, 6):
                    mix_t(n // 2 - 1)

            def out_proj(t, bank):
                if t == 0:
                    pe.wait_ge(w_in["out0"], 16)
                    pe.wait_ge(w_in["out1"], 16)
                    pe.wait_ge(mt_sb, TILES)
                    pe.wait_ge(pv_sb, 2 * len(ATT))
                for e in range(2):
                    w = wv(f"out{e}")
                    for c in range(KC):
                        last = mm(ps[:, bank + e, :], mixT[:, c, t * P:(t + 1) * P], w[:, c, :], c == 0, c == KC - 1)
                last.then_inc(wout, 1)

            def h2_t(t):
                pe.wait_ge(hready, TILES + t + 1)
                if t > 0:
                    pe.wait_ge(x1_done, TILES)
                for c in range(KC):
                    last = tr(ps[:, c // 4, (c % 4) * P:(c % 4 + 1) * P], h2[t % 2][:, c * P:(c + 1) * P])
                last.then_inc(h2t_ps, 1)

            def query(u):
                t, h = divmod(u, HP)
                if h == 0:
                    pe.wait_ge(h2t_act, t + 1)
                    pe.wait_ge(h2t_dve, t + 1)
                if t == 0 and h % 2 == 0:
                    pe.wait_ge(w_in[f"q{h // 2}"], 16)
                w = wv(f"q{h // 2}")
                for e in range(2):
                    col = (h % 2) * 256 + e * P
                    for c in range(KC):
                        last = mm(ps[:, 2 + u % 2, e * P:(e + 1) * P], w[:, c, col:col + P], h2T[:, c, :], c == 0, c == KC - 1)
                last.then_inc(q_ps, 1)
                if u >= 2:
                    pe.wait_ge(topped, u - 1)
                pe.wait_ge(q_sb, u + 1)
                for e in range(2):
                    last = mm(ps[:, 4 + u % 2, e * P:(e + 1) * P], qT[:, u % 2, e, :], keysT[:, e, :])
                last.then_inc(sc2_ps, 1)

            def y_start(t):
                if t > 0:
                    pe.wait_ge(y_read, t)
                pe.wait_ge(x1_done, t + 1)
                for e in range(2):
                    last = mm(ps[:, 6 + e, :], ident[:], x[:, t, e * 512:(e + 1) * 512], True, False)
                last.then_inc(y_init, 1)

            def add_expert(n, s, stop=False):
                pe.wait_ge(diagd, n + 1)
                for e in range(2):
                    last = mm(ps[:, 6 + e, :], diag[:, s, :], rows[:, s, D + e * 512:D + (e + 1) * 512], False, stop)
                last.then_inc(acc, 1)
                return last

            def picks(u):
                final = u % HP == HP - 1
                if final:
                    for s in range(G):
                        add_expert(u * KP + s, s)
                    for s in range(G):
                        add_expert(u * KP + G + s, s, s == G - 1)
                else:
                    with pe.Fori(0, GROUPS) as i:
                        for s in range(G):
                            add_expert(i * G + (u * KP + s), s)

            out_proj(0, 0)
            out_proj(1, 6)
            h2_t(0)
            pe.wait_ge(keys_in, 32)
            query(0)
            pe.wait_ge(h2t_act, 1)
            pe.wait_ge(h2t_dve, 1)
            out_proj(2, 0)
            query(1)
            pe.wait_ge(x1_done, 2)
            for u in range(UNITS):
                t, h = divmod(u, HP)
                if h == 0:
                    y_start(t)
                picks(u)
                if u + 2 < UNITS:
                    if (u + 2) % HP == 0:
                        h2_t((u + 2) // HP)
                    query(u + 2)

        @block.scalar
        def _(act):
            def A(*args, **kw):
                return nc.scalar.activation(*args, **kw)

            def copy(out, in_):
                return A(out, in_, ACT.Copy)

            def take_hT(t):
                act.wait_ge(ht_ps, t + 1)
                copy(hT[:, 0:4, t * P:(t + 1) * P], ps[:, 2 * (t % 2), :].rearrange("p (c t) -> p c t", c=4)).then_inc(ht_act, 1)

            for t in range(TILES):
                act.wait_ge(x_in[t], 16)
                if t == 2:
                    act.wait_ge(ht_ps, 1)
                A(hnat[:, t % 2, :], x[:, t, :], ACT.Square, accum_out=sumsq[:, t:t + 1]).then_inc(sqd, 1)
                if t >= 1:
                    take_hT(t - 1)
            take_hT(2)

            def take(n):
                name, kind, i = UN[n]
                act.wait_ge(proj, n + 1)
                src = ps[:, 6 + n % 2, :]
                if name == "kv":
                    copy(kvnat[:, i, :], src[:, 0:NKV]).then_inc(proj_act, 1)
                elif name == "qi":
                    for e in range(2):
                        ins = copy(qiT[0:64, :, 2 * i + e, :],
                                   src[64 * e:64 * e + 64, 0:NTOK].rearrange("p (g t) -> p g t", t=STEPS))
                    ins.then_inc(proj_act, 1)
                elif name == "qa":
                    copy(qaT[:, i, :], src[:, 0:NTOK]).then_inc(proj_act, 1)
                elif name == "vb":
                    copy(vb[:, i, :], src).then_inc(proj_act, 1)
                else:
                    A(gs[:, i, :], src, ACT.Silu).then_inc(proj_act, 1)

            for n in range(7):
                take(n)
            for m in range(24):
                t, g = divmod(m, 8)
                act.wait_ge(dots, m + 1)
                if m >= 2:
                    act.wait_ge(combined, m - 1)
                k = KEYS[t]
                A(relu[:, m % 2, 0:k], psf[:, 1024 * (m % 2):1024 * (m % 2) + k], ACT.Relu).then_inc(relued, 1)
            for n in range(7, N_ACT):
                take(n)

            act.wait_ge(proj, len(UN))
            for t in range(2):
                act.wait_ge(rt_ps, t + 1)
                copy(rT[:, t, :, :], ps[:, t, :].rearrange("p (s t) -> p s t", s=4)).then_inc(rt_sb, 1)
            act.wait_ge(rt_ps, 3)
            copy(qTd, ps[:, 2, :].rearrange("p (h t) -> p h t", h=HB)).then_inc(rt_sb, 1)
            act.wait_ge(rt_ps, 4)
            copy(kTs, ps[:, 3, 0:256].rearrange("p (s t) -> p s t", s=2)).then_inc(rt_sb, 1)
            act.wait_ge(sp_ps, 1)
            for e in range(2):
                copy(snp[64 * e:64 * e + 64, :, :], ps[64 * e:64 * e + 64, 3, :].rearrange(
                    "p (q e v) -> p q e v", q=2, e=2)[:, :, e, :]).then_inc(sp_sb, 1)

            def att_exp(n):
                t, i = ATT[n]
                act.wait_ge(smax, n + 1)
                if n >= 2:
                    act.wait_ge(pt_ps, n - 1)
                c = n % 2
                if t < 2:
                    for k in range(KVH):
                        ins = A(prob[:, c, k * 256:k * 256 + KEYS[t]], ps[:, 2 * c + k, 0:KEYS[t]], ACT.Exp,
                                bias=negmax[:, c, k:k + 1], scale=DH ** -0.5, accum_out=esum[:, c, k:k + 1])
                else:
                    ins = A(prob[:, c, :], psf[:, 1024 * c:1024 * c + 640], ACT.Exp,
                            bias=negmax[:, c, 0:1], scale=DH ** -0.5, accum_out=esum[:, c, 0:1])
                ins.then_inc(expd, 1)

            def att_take(n):
                t, i = ATT[n]
                c = n % 2
                act.wait_ge(pt_ps, n + 1)
                if n >= 2:
                    act.wait_ge(pv_ps, n - 1)
                k = 256 * (t + 1) if t < 2 else 640
                copy(probT[:, c, 0:k], psf[:, 2048:2048 + k]).then_inc(pt_sb, 1)
                act.wait_ge(pv_ps, n + 1)
                for k in range(KVH):
                    r = slice(64 * k, 64 * k + 64)
                    if t < 2:
                        copy(mixT[r, i, t * P:(t + 1) * P], ps[r, 6, k * P:(k + 1) * P]).then_inc(pv_sb, 1)
                    else:
                        copy(mixT[r, 0:GRP, 2 * P + i * STEPS:2 * P + (i + 1) * STEPS],
                             ps[r, 6, k * 64:(k + 1) * 64].rearrange("p (g t) -> p g t", g=GRP)).then_inc(pv_sb, 1)

            for n in range(len(ATT) + 1):
                if n < len(ATT):
                    att_exp(n)
                if n >= 1:
                    att_take(n - 1)
                if n in (2, 4, 6):
                    t = n // 2 - 1
                    act.wait_ge(mt_ps, t + 1)
                    copy(mixT[:, 4:8, t * P:(t + 1) * P], ps[:, 7, :].rearrange("p (c t) -> p c t", c=4)).then_inc(mt_sb, 1)

            def square(n, src, scratch):
                A(scratch, src, ACT.Square, accum_out=sumsq[:, n:n + 1]).then_inc(sqd, 1)

            def h2_take(t):
                act.wait_ge(h2t_ps, t + 1)
                copy(h2T[:, 0:4, :], ps[:, 0, :].rearrange("p (c t) -> p c t", c=4)).then_inc(h2t_act, 1)

            def take_q(u):
                act.wait_ge(q_ps, u + 1)
                if u >= 2:
                    act.wait_ge(sc2_ps, u - 1)
                copy(qT[:, u % 2, :, :], ps[:, 2 + u % 2, 0:256].rearrange("p (e t) -> p e t", e=2)).then_inc(q_sb, 1)

            def gate_exp(u):
                act.wait_ge(best_set, u + 1)
                A(ebest[:, u % 2, :], best, ACT.Exp, bias=negbest[:], accum_out=gsum[:, u % 2:u % 2 + 1]).then_inc(gexp, 1)

            def gelus(u):
                with act.Fori(0, GROUPS) as i:
                    for s in range(G):
                        act.wait_ge(dotted, i * G + (u * KP + s + 1))
                        A(zact[:, s:s + 1], zdot[:, s:s + 1], ACT.Gelu).then_inc(gelued, 1)

            act.wait_ge(x1_done, 1)
            square(TILES, x[:, 0, :], h2[0])
            h2_take(0)
            take_q(0)
            gate_exp(0)
            take_q(1)
            act.wait_ge(x1_done, TILES)
            square(TILES + 1, x[:, 1, :], h2[1])
            act.wait_ge(msd, TILES + 2)
            square(TILES + 2, x[:, 2, :], h2[1])
            for u in range(UNITS):
                t, h = divmod(u, HP)
                if u + 1 < UNITS:
                    gate_exp(u + 1)
                gelus(u)
                if h == HP - 1:
                    act.wait_ge(y_read, t + 1)
                    square(2 * TILES + t, x[:, t, :], h2[t % 2])
                if u + 2 < UNITS:
                    if (u + 2) % HP == 0:
                        h2_take((u + 2) // HP)
                    take_q(u + 2)

        @block.vector
        def _(dve):
            V = nc.vector
            count = {}

            def then(ins, s=chain):
                key = s.name
                count[key] = count.get(key, 0) + 1
                ins.then_inc(s, 1)
                dve.wait_ge(s, count[key])

            def mean_square(n):
                dve.wait_ge(sqd, n + 1)
                then(V.tensor_scalar(ms[:, n:n + 1], sumsq[:, n:n + 1], 1.0 / D, EPS, ALU.mult, ALU.add), msd)

            def normed(out, n, t, gain, s):
                dve.wait_ge(rsd, n + 1)
                then(V.scalar_tensor_tensor(out, x[:, t, :], rstd[:, n:n + 1], gain, ALU.mult, ALU.mult), s)

            dve.wait_ge(g1_in, 16)
            for t in range(TILES):
                mean_square(t)
                normed(hnat[:, t % 2, :], t, t, g1b, hready)
                if t >= 1:
                    dve.wait_ge(ht_ps, t)
                    then(V.tensor_copy(hT[:, 4:8, (t - 1) * P:t * P], ps[:, 2 * ((t - 1) % 2) + 1, :].rearrange(
                        "p (c t) -> p c t", c=4)), ht_dve)
            dve.wait_ge(ht_ps, 3)
            then(V.tensor_copy(hT[:, 4:8, 2 * P:3 * P], ps[:, 1, :].rearrange("p (c t) -> p c t", c=4)), ht_dve)
            dve.wait_ge(ident_in, 32)
            then(V.tensor_copy(ident_bf[:], ident[:]))
            dve.wait_ge(kt_ps, 1)
            then(V.tensor_copy(kaT, ps[:, 0, 0:NTOK]), kt_sb)
            then(V.tensor_copy(kiwT[0:DH + HI, :], ps[0:DH + HI, 1, 0:NTOK]), kt_sb)
            dve.wait_ge(w_ps, 1)
            dve.wait_ge(wz_zero, 1)
            dve.wait_ge(small_in, 16 * 7)
            for t in range(TILES):
                then(V.tensor_tensor(
                    wz[:, t, :].rearrange("p (g s) -> p g s", s=144)[:, :, 0:STEPS],
                    ps[:, 2, t * P:(t + 1) * P].rearrange("p (g s) -> p g s", g=8),
                    m16[:].rearrange("p (a s) -> p a s", a=1).broadcast_to([P, 8, STEPS]), ALU.mult), wz_set)
            for t in range(TILES):
                k = KEYS[t]
                dve.wait_ge(combined, 8 * (t + 1))
                dve.wait_ge(bar_in, 16)
                if k > P:
                    then(V.tensor_copy(score[:, 0:k - P], psf[:, 2048:2048 + k - P]))
                then(V.tensor_tensor(score[:, k - P:k], psf[:, 2048 + k - P:2048 + k],
                                     bar[:, P * (t // 2):P * (t // 2) + P], ALU.add), scored)
                for r in range(0, TOPK[t], 8):
                    then(V.max(out=top8[:], in_=score[:, 0:k]))
                    if TOPK[t] - r < 8:
                        then(V.memset(top8[:, TOPK[t] - r:8], TAKEN))
                    then(V.match_replace(out=score[:, 0:k], in_to_replace=top8[:], in_values=score[:, 0:k],
                                         imm_value=TAKEN))
                then(V.tensor_scalar(bias[t], score[:, 0:k], -3.36e38, OFF, ALU.is_gt, ALU.mult), biased)
            for t in range(TILES):
                dve.wait_ge(proj, N_ACT + t + 1)
                src = ps[:, 6 + (N_ACT + t) % 2, :].rearrange("p (q h e d) -> p q h e d", q=2, h=HB, e=2)
                dst = rot[:, t, :, :, :].rearrange("p (q h) e d -> p q h e d", q=2)
                tmp = at(wtf, 2 * SLOT, 256).rearrange("p (q h d) -> p q h d", q=2, h=HB)
                for q in range(2):
                    def tab(i):
                        return cs[:, t, i, q:q + 1, :].broadcast_to([P, HB, DK // 2])
                    x1, x2 = src[:, q, :, 0, :], src[:, q, :, 1, :]
                    then(V.tensor_tensor(tmp[:, 0, :, :], x1, tab(0), ALU.mult))
                    then(V.tensor_tensor(tmp[:, 1, :, :], x2, tab(1), ALU.mult))
                    then(V.tensor_tensor(dst[:, q, :, 0, :], tmp[:, 0, :, :], tmp[:, 1, :, :], ALU.subtract))
                    then(V.tensor_tensor(tmp[:, 0, :, :], x1, tab(1), ALU.mult))
                    then(V.tensor_tensor(tmp[:, 1, :, :], x2, tab(0), ALU.mult))
                    ins = V.tensor_tensor(dst[:, q, :, 1, :], tmp[:, 0, :, :], tmp[:, 1, :, :], ALU.add)
                    then(ins, proj_dve if q == 1 else chain)

            dve.wait_ge(proj, len(UN))
            for b in range(2):
                then(V.tensor_copy(rotq2[:, :, b, :, :], rot[:, 2, 0:HB, :, :]), q_twice)

            dve.wait_ge(proj, len(UN))
            dve.wait_ge(s_ps, 1)
            for e in range(2):
                then(V.tensor_tensor(am0[:, e::2, :], ps[:, 4 + e, :].rearrange("p (h i) -> p h i", h=2),
                                     dmask[:, e::2, :], ALU.mult), s_masked)

            def by_parity(v):
                return v.rearrange("p (i e) n -> p e i n", e=2)

            dve.wait_ge(s_ps, 3)
            then(V.tensor_tensor(by_parity(am1), ps[:, 6:8, 0:256].rearrange("p e (i n) -> p e i n", i=2),
                                 by_parity(dmask[:, :, 0:P]), ALU.mult), s_masked)
            dve.wait_ge(dms_in, 16)
            then(V.tensor_tensor(by_parity(am2), ps[:, 6:8, 256:512].rearrange("p e (i n) -> p e i n", i=2),
                                 by_parity(dmask_s.rearrange("p (h i) -> p h i", h=HB)), ALU.mult), s_masked)
            dve.wait_ge(zeroed, 1)
            dve.wait_ge(rt_sb, 4)
            for h in range(HB):
                then(V.tensor_tensor(qz[:, h, :].rearrange("p (q n) -> p q n", q=4)[:, :, 0:2 * STEPS],
                                     qTd[:, h, :].rearrange("p (q n) -> p q n", q=4),
                                     qmask[:, h, :].rearrange("p (q n) -> p q n", q=4), ALU.mult), qz_set)
            for t in range(2):
                then(V.tensor_tensor(kdn[:, t, :, :], rot[:, t, HB:2 * HB, :, :].rearrange("p h e d -> p h (e d)"),
                                     kd[:, t * HB:(t + 1) * HB].rearrange("p (h a) -> p h a", a=1).broadcast_to([P, HB, DK]),
                                     ALU.mult), kdec)
            for b in range(STREAMS):
                col = (2 + b) * HB
                then(V.tensor_tensor(kz[:, b // 2, :, b % 2, :], rot[:, 2, HB:2 * HB, :, :].rearrange("p h e d -> p h (e d)"),
                                     kd[:, col:col + HB].rearrange("p (h a) -> p h a", a=1).broadcast_to([P, HB, DK]),
                                     ALU.mult), kdec)
            then(V.tensor_copy(selb, ident_bf[:].rearrange("p (b a t) -> p b a t", b=STREAMS, a=1).broadcast_to(
                [P, STREAMS, 8, STEPS])), sel_set)
            for k in range(KVH):
                r = slice(64 * k, 64 * k + 64)
                then(V.tensor_copy(qzb[r, :, k, :, :], qaT[r, :, 2 * P:3 * P].rearrange("p g (b t) -> p b g t", b=STREAMS)), qzb_set)
            for t in range(TILES):
                dve.wait_ge(o_ps, t + 1)
                for h in range(HB):
                    then(V.bn_stats(out=bn6[:], in_=ps[:, t, h * P:(h + 1) * P]))
                    then(V.bn_aggr(out=mv[:, h, :], in_=bn6[:]))
                then(V.tensor_scalar(veps[:], mv[:, :, 1], EPS, None, ALU.add), o_var)
                dve.wait_ge(o_rstd, t + 1)
                for h in range(HB):
                    ins = V.tensor_scalar(mixnat[:, t, h * P:(h + 1) * P], ps[:, t, h * P:(h + 1) * P],
                                          mv[:, h, 0:1], rstd4[:, h:h + 1],
                                          ALU.subtract, ALU.mult)
                    then(ins)
                then(V.tensor_tensor(mixnat[:, t, :], mixnat[:, t, :], gs[:, t, :], ALU.mult), o_norm)
            dve.wait_ge(ss_ps, 1)
            for h in range(HB):
                then(V.scalar_tensor_tensor(snew[:, :, h, :], s0[:, :, h, :], float(np.exp(STEPS * LG[h])),
                                            ps[:, 4:8, h * P:(h + 1) * P], ALU.mult, ALU.add), ss_sb)

            def att_max(n):
                t, i = ATT[n]
                c = n % 2
                dve.wait_ge(sc_ps, n + 1)
                w = 2 if t < 2 else 1
                if t < 2:
                    src = ps[:, 2 * c:2 * c + 2, 0:KEYS[t]]
                else:
                    src = psf[:, 1024 * c:1024 * c + 640]
                then(V.tensor_reduce(rowmax[:, 0:w], src, AX.X, ALU.max))
                if n >= 2:
                    dve.wait_ge(expd, n - 1)
                then(V.tensor_scalar(negmax[:, c, 0:w], rowmax[:, 0:w], -(DH ** -0.5), None, ALU.mult), smax)

            def att_scale(n):
                t, i = ATT[n]
                c = n % 2
                w = 2 if t < 2 else 1
                dve.wait_ge(expd, n + 1)
                then(V.reciprocal(resum[:, 0:w], esum[:, c, 0:w]))
                if t < 2:
                    then(V.tensor_scalar(prob[:, c, 0:KEYS[t]], prob[:, c, 0:KEYS[t]], resum[:, 0:1], None, ALU.mult))
                    then(V.tensor_scalar(prob[:, c, 256:256 + KEYS[t]], prob[:, c, 256:256 + KEYS[t]], resum[:, 1:2], None, ALU.mult), pscaled)
                else:
                    then(V.tensor_scalar(prob[:, c, :], prob[:, c, :], resum[:, 0:1], None, ALU.mult), pscaled)

            for n in range(len(ATT) + 1):
                if n < len(ATT):
                    att_max(n)
                if n >= 1:
                    att_scale(n - 1)

            def add_mix(t, bank):
                dve.wait_ge(wout, t + 1)
                then(V.tensor_tensor(x[:, t, :], psf[:, bank * 512:(bank + 2) * 512], x[:, t, :], ALU.add), x1_done)

            def h2_take(t):
                dve.wait_ge(h2t_ps, t + 1)
                then(V.tensor_copy(h2T[:, 4:8, :], ps[:, 1, :].rearrange("p (c t) -> p c t", c=4)), h2t_dve)

            def top16(u):
                dve.wait_ge(sc2_ps, u + 1)
                for e in range(2):
                    s = ps[:, 4 + u % 2, e * P:(e + 1) * P]
                    then(V.max(out=top[:, e, 0:8], in_=s))
                    then(V.match_replace(out=rest, in_to_replace=top[:, e, 0:8], in_values=s, imm_value=TAKEN))
                    then(V.max(out=top[:, e, 8:16], in_=rest))
                    then(V.max_index(topi[:, e, 0:8], top[:, e, 0:8], s))
                    then(V.max_index(topi[:, e, 8:16], top[:, e, 8:16], rest), topped if e else chain)
                then(V.tensor_copy(topf, topi))
                c4 = cand.rearrange("p (i j) -> p i j", i=KP)
                then(V.tensor_tensor(c4, top[:, 0, :].rearrange("p (i a) -> p i a", a=1).broadcast_to([P, KP, KP]),
                                     top[:, 1:2, :].broadcast_to([P, KP, KP]), ALU.add))
                if u >= 1:
                    dve.wait_ge(gexp, u)
                then(V.max(out=best[:, 0:8], in_=cand))
                then(V.match_replace(out=cand2, in_to_replace=best[:, 0:8], in_values=cand, imm_value=TAKEN))
                then(V.max(out=best[:, 8:16], in_=cand2))
                then(V.tensor_scalar(negbest[:], best[:, 0:1], -1.0, None, ALU.mult), best_set)
                then(V.max_index(besti[:, 0:8], best[:, 0:8], cand))
                then(V.max_index(besti[:, 8:16], best[:, 8:16], cand2))
                then(V.tensor_scalar(rank[:, 0, :], besti, 4, None, ALU.logical_shift_right))
                then(V.tensor_scalar(rank[:, 1, :], besti, 15, None, ALU.bitwise_and))
                then(V.tensor_copy(rankf, rank))
                for e in range(2):
                    then(V.tensor_tensor(hot[:, e, :, :], rankf[:, e, :].rearrange("p (k a) -> p k a", a=1).broadcast_to([P, KP, KP]),
                                         iota[:].rearrange("p (a r) -> p a r", a=1).broadcast_to([P, KP, KP]), ALU.is_equal))
                    then(V.tensor_tensor(hoti[:, e, :, :], hot[:, e, :, :], topf[:, e:e + 1, :].broadcast_to([P, KP, KP]), ALU.mult))
                then(V.tensor_reduce(half_id, hoti, AX.X, ALU.add))
                dve.wait_ge(gexp, u + 1)
                then(V.reciprocal(rgsum[:], gsum[:, u % 2:u % 2 + 1]))
                then(V.tensor_scalar(gates[:, u * KP:(u + 1) * KP], ebest[:, u % 2, :], rgsum[:], None, ALU.mult))
                then(V.scalar_tensor_tensor(ids[:, u * KP:(u + 1) * KP], half_id[:, 0, :], float(NK), half_id[:, 1, :],
                                            ALU.mult, ALU.add), picked)

            def picks(u):
                t = u // HP

                def scaled(n, s):
                    dve.wait_ge(gelued, n + 1)
                    V.tensor_scalar(diag[:, s, :], ident[:], zact[:, s:s + 1], gates[:, bass.ds(n, 1)],
                                    ALU.mult, ALU.mult).then_inc(diagd, 1)

                with dve.Fori(0, GROUPS) as i:
                    for s in range(G):
                        dve.wait_ge(landed[s], (i + (u * GROUPS + 1)) * 16)
                        V.tensor_tensor_reduce(rows[:, s, 0:D], rows[:, s, 0:D], h2[t % 2], 1.0, 0.0, ALU.mult, ALU.add,
                                               zdot[:, s:s + 1]).then_inc(dotted, 1)
                        if s > 0:
                            scaled(i * G + (u * KP + s - 1), s - 1)
                    scaled(i * G + (u * KP + G - 1), G - 1)

            add_mix(0, 0)
            dve.wait_ge(keys_in, 32)
            mean_square(TILES)
            normed(h2[0], TILES, 0, g2b[:], hready)
            add_mix(1, 6)
            h2_take(0)
            top16(0)
            add_mix(2, 0)
            mean_square(TILES + 1)
            mean_square(TILES + 2)
            for u in range(UNITS):
                t, h = divmod(u, HP)
                if u + 1 < UNITS:
                    top16(u + 1)
                picks(u)
                if h == HP - 4 and t + 1 < TILES:
                    normed(h2[(t + 1) % 2], TILES + t + 1, t + 1, g2b[:], hready)
                if h == 2 and t > 0:
                    dve.wait_ge(gf_in, 16)
                    normed(x[:, t - 1, :], 2 * TILES + t - 1, t - 1, gfb, y_out)
                if h == HP - 1:
                    dve.wait_ge(acc, (u + 1) * KP)
                    then(V.tensor_copy(x[:, t, :], psf[:, 6 * 512:8 * 512]), y_read)
                    mean_square(2 * TILES + t)
                if u + 2 < UNITS and (u + 2) % HP == 0:
                    h2_take((u + 2) // HP)
            normed(x[:, TILES - 1, :], 3 * TILES - 1, TILES - 1, gfb, y_out)


def kernel(x_prompt, x_sample, cache_attn_k, cache_attn_v, cache_idx_k, state_retention, ln1_g, w_in, w_out, ln2_g,
           peer_w_query, peer_keys1, peer_keys2, peer_u, peer_v, ln_final_g):
    import concourse.bacc as bacc
    from concourse.bass_utils import run_bass_kernel_spmd

    def chunked(w):
        return w.reshape(KC, P, -1).transpose(1, 0, 2).reshape(P, -1)

    w, wo, wq = (np.asarray(v)[0] for v in (w_in, w_out, peer_w_query))
    c_qa, c_kv, c_qi = 0, HA * DH, HA * DH + 2 * KVH * DH
    c_ki = c_qi + HI * DH
    c_qb = c_ki + DH + HI
    c_vb = c_qb + 2 * HB * DK
    c_gb = c_vb + HB * DV
    qcols = np.arange(HA * DH).reshape(KVH, GRP, DH).transpose(1, 0, 2).reshape(-1)
    rows_out = np.concatenate([qcols, np.arange(HA * DH, D)])
    arrays = {
        "x": np.concatenate([np.asarray(x_prompt).reshape(2, P, D), np.asarray(x_sample).reshape(1, P, D)]),
        "ln1_g": np.asarray(ln1_g)[0], "ln2_g": np.asarray(ln2_g)[0], "ln_final_g": np.asarray(ln_final_g),
        "w_kv": chunked(np.concatenate([w[:, c_kv:c_qi], w[:, c_ki:c_qb]], 1)),
        "w_qi": chunked(w[:, c_qi:c_ki]), "w_qa": chunked(w[:, qcols]),
        "w_qkb": chunked(w[:, c_qb:c_vb]), "w_vb": chunked(w[:, c_vb:c_gb]), "w_gb": chunked(w[:, c_gb:]),
        "keysT": np.stack([np.asarray(peer_keys1)[0].T, np.asarray(peer_keys2)[0].T], 1).reshape(P, -1),
        "cki": np.asarray(cache_idx_k)[0].transpose(0, 2, 1),
        "ckv": np.stack([np.asarray(cache_attn_k)[0].reshape(STREAMS, PAST, P).transpose(0, 2, 1),
                         np.asarray(cache_attn_v)[0].reshape(STREAMS, 4, P, P).transpose(0, 2, 1, 3).reshape(
                             STREAMS, P, PAST)], 1),
        "s0": np.asarray(state_retention)[0].reshape(4, 2, HB, DK, DV).transpose(1, 3, 0, 2, 4),
        "uv": np.concatenate([np.asarray(peer_u)[0], np.asarray(peer_v)[0]], 1),
    }
    for e in range(2):
        arrays[f"w_out{e}"] = chunked(wo[rows_out][:, e * 512:(e + 1) * 512])
    for j in range(4):
        arrays[f"w_q{j}"] = chunked(wq[:, j * 512:(j + 1) * 512])
    arrays.update(constants())
    arrays = {k: np.ascontiguousarray(v) for k, v in arrays.items()}

    nc = bacc.Bacc("TRN2", target_bir_lowering=False, num_devices=1)
    ins = {k: nc.dram_tensor(f"in_{k}", v.shape, mybir.dt.from_np(v.dtype), kind="ExternalInput").ap()
           for k, v in arrays.items()}
    shapes = {"y": (TILES, P, D), "k": (TILES, P, P), "v": (TILES, P, P), "ki": (TILES, P, DH),
              "state_p": (P, 2, DV), "state_s": (2, DK, 4, HB, DV)}
    outs = {k: nc.dram_tensor(f"out_{k}", s, F32, kind="ExternalOutput").ap() for k, s in shapes.items()}
    outs["kv"] = [[outs["k"][t], outs["v"][t], outs["ki"][t]] for t in range(TILES)]
    build(nc, ins, outs)
    r = run_bass_kernel_spmd(nc, [{f"in_{k}": v for k, v in arrays.items()}], core_ids=[0]).results[0]
    y, k, v, ki = (r["out_" + n] for n in ("y", "k", "v", "ki"))
    state_p = r["out_state_p"].reshape(2, DK, 2, DV).transpose(2, 0, 1, 3).reshape(1, 1, HB, DK, DV)
    state_s = r["out_state_s"].transpose(2, 0, 3, 1, 4).reshape(1, STREAMS, HB, DK, DV)
    return (y[:2].reshape(1, 2 * P, D), y[2].reshape(STREAMS, STEPS, D),
            k[:2].reshape(1, 1, 2 * P, KVH, DH), v[:2].reshape(1, 1, 2 * P, KVH, DH), ki[:2].reshape(1, 1, 2 * P, DH),
            np.ascontiguousarray(state_p),
            k[2].reshape(1, STREAMS, STEPS, KVH, DH), v[2].reshape(1, STREAMS, STEPS, KVH, DH),
            ki[2].reshape(1, STREAMS, STEPS, DH), np.ascontiguousarray(state_s))
```

```python
from contextlib import ExitStack

import numpy as np

import concourse.bass as bass
from concourse import mybir

F32 = mybir.dt.float32
BF16 = mybir.dt.bfloat16
U32 = mybir.dt.uint32
ALU = mybir.AluOpType
ACT = mybir.ActivationFunctionType
AX = mybir.AxisListType

P = 128
D = 1024
KC = D // P
TILES = 3
NTOK = TILES * P
STREAMS, STEPS, PAST = 8, 16, 512
HA, KVH, GRP, DH = 8, 2, 4, 64
HI = 8
HB, DK, DV = 4, 64, 128
CHUNK = 64
TOPK = (64, 64, 132)
KEYS = (128, 256, 640)
NKV = 2 * P + DH + HI
HP, KP, NK = 8, 16, 128
UNITS = TILES * HP
G = 8
GROUPS = KP // G
EPS = 1e-6
TAKEN = -3.39e38
BARRED = -3.0e38
OFF = -1.0e30
LG = [float(np.log(np.float32(1.0) - np.float32(2.0) ** np.float32(-5.0 - h))) for h in range(HB)]


def constants():
    t = np.arange(P)
    pos = np.stack([t, P + t, PAST + t % STEPS]).astype(np.float32)
    inv = (1.0 / (np.float32(10000.0) ** np.linspace(0.0, 1.0, DK // 2, dtype=np.float32))).astype(np.float32)
    ang = (pos[:, :, None] * inv).astype(np.float32)
    cs = np.stack([np.cos(ang), np.sin(ang)], 1)
    cs = np.stack([cs, cs * np.float32(DK ** -0.5)], 2)
    c = {"cs": cs.transpose(3, 0, 1, 2, 4).reshape(P, -1)}
    lg = np.array(LG)
    kd = np.exp((2 * P - 1 - (np.arange(2)[None, :, None] * P + t[:, None, None])) * lg)
    own = (t[:, None] // STEPS == np.arange(STREAMS)[None, :])
    kds = own[:, :, None] * np.exp((STEPS - 1 - t % STEPS)[:, None, None] * lg)
    c["kd"] = np.concatenate([kd.reshape(P, -1), kds.reshape(P, -1)], 1)
    diff = t[None, :] - t[:, None]
    near = np.where(diff[:, None, :] >= 0, np.exp(np.maximum(diff, 0)[:, None, :] * lg[None, :, None]), 0.0)
    far = np.exp((diff + P)[:, None, :] * lg[None, :, None])
    c["dmask"] = np.concatenate([near, far], 2).reshape(P, -1)
    same = (t[None, :] // STEPS == t[:, None] // STEPS)
    c["dmask_s"] = (near * same[:, None, :]).reshape(P, -1)
    half = (t // STEPS % 2)[None, :] == (t[:, None] // DK)
    c["qmask"] = (half[:, None, :] * np.exp((t % STEPS + 1)[None, None, :] * lg[None, :, None])).reshape(P, -1)
    causal = np.where(t[None, :] // CHUNK <= t[:, None] // CHUNK, 0.0, BARRED)
    c["bar"] = np.concatenate([causal, np.where(same, 0.0, BARRED)], 1)
    e8 = np.zeros((P, P))
    e8[DH:DH + HI] = (np.arange(HI)[:, None] == t[None, :] // STEPS)
    c["e8"] = e8
    c["m16"] = (t[:, None] % STEPS == np.arange(STEPS)[None, :])
    c["iota"] = np.broadcast_to(np.arange(KP), (P, KP))
    c["ident"] = np.eye(P)
    c["half"] = np.full((P, HB), -0.5)
    return {k: np.ascontiguousarray(v, dtype=np.float32) for k, v in c.items()}


def build(nc, a, o):
    with ExitStack() as ctx:
        def sb(name, shape, dt=F32):
            return ctx.enter_context(nc.sbuf_tensor(name, shape, dt))

        def sem(name):
            return ctx.enter_context(nc.semaphore(name))

        x = sb("x", [P, TILES, D])
        ident = sb("ident", [P, P])
        ident_bf = sb("ident_bf", [P, P], BF16)
        keysT = sb("keysT", [P, 2, NK])
        ids = sb("ids", [P, UNITS * KP], U32)
        gates = sb("gates", [P, UNITS * KP])
        cs = sb("cs", [P, TILES, 2, 2, DK // 2])
        kd = sb("kd", [P, 2 * HB + STREAMS * HB])
        g2b = sb("g2b", [P, D])
        dmask = sb("dmask", [P, HB, 2 * P])
        qmask = sb("qmask", [P, HB, P])
        e8 = sb("e8", [P, P])
        m16 = sb("m16", [P, STEPS])
        iota = sb("iota", [P, KP])
        half4 = sb("half4", [P, HB])
        stage = sb("stage", [P, 2, G], U32)
        zdot = sb("zdot", [P, G])
        zact = sb("zact", [P, G])
        sumsq, ms, rstd = sb("sumsq", [P, 9]), sb("ms", [P, 9]), sb("rstd", [P, 9])
        bn6, mv = sb("bn6", [P, HB, 6]), sb("mv", [P, HB, 2])
        veps, rstd4 = sb("veps", [P, HB]), sb("rstd4", [P, HB])
        rowmax, negmax = sb("rowmax", [P, 2]), sb("negmax", [P, 2, 2])
        esum, resum = sb("esum", [P, 2, 2]), sb("resum", [P, 2])
        top8 = sb("top8", [P, 8])
        negbest, gsum, rgsum = sb("negbest", [P, 1]), sb("gsum", [P, 2]), sb("rgsum", [P, 1])
        rows = sb("rows", [P, G, 2 * D])
        wt = sb("wt", [P, 6, KC * 512])
        work = sb("work", [P, 4608])
        ps = ctx.enter_context(nc.psum_tensor("ps", [P, 8, 512], F32))
        psf = ps[:, :, :].rearrange("p b n -> p (b n)")

        rowf = rows[:, :, :].rearrange("p g n -> p (g n)")
        wtf = wt[:, :, :].rearrange("p s n -> p (s n)")
        SLOT = KC * 512

        def at(region, off, n):
            return region[:, off:off + n]

        hT = at(rowf, 0, KC * NTOK).rearrange("p (c t) -> p c t", c=KC)
        hnat = at(rowf, 3072, 2 * D).rearrange("p (b n) -> p b n", b=2)
        g1b = at(rowf, 5120, D)
        qaT = at(rowf, 6144, GRP * NTOK).rearrange("p (g t) -> p g t", g=GRP)
        qiT = at(rowf, 7680, HI * NTOK).rearrange("p (g h t) -> p g h t", h=HI, t=STEPS)
        kaT = at(rowf, 10752, NTOK)
        kiwT = at(rowf, 11136, NTOK)
        biasb = at(rowf, 11520, 512).bitcast(BF16)
        bias = (biasb[:, 0:128], biasb[:, 128:384], biasb[:, 384:1024])
        rT = at(rowf, 12288, 1024).rearrange("p (t s n) -> p t s n", t=2, s=4)
        qTd = at(rowf, 13312, 512).rearrange("p (h t) -> p h t", h=HB)
        kTs = at(rowf, 13824, 256).rearrange("p (s t) -> p s t", s=2)
        am0 = at(rowf, 14080, 1024).rearrange("p (h i) -> p h i", h=HB)
        kvnat = at(rowf, 15360, TILES * NKV).rearrange("p (t n) -> p t n", t=TILES)
        qz = at(rowf, 0, HB * 640).rearrange("p (h n) -> p h n", h=HB)
        qzb = at(rowf, 2560, D).rearrange("p (b k g t) -> p b k g t", b=STREAMS, k=KVH, g=GRP)
        kdn = at(rowf, 3584, 512).rearrange("p (t h d) -> p t h d", t=2, h=HB)
        mixnat = at(rowf, 4096, TILES * 512).rearrange("p (t n) -> p t n", t=TILES)
        rotq2 = at(rowf, 5632, 512).rearrange("p (h b e d) -> p h b e d", h=HB, b=2, e=2)
        WZ = 8 * 144
        wz = at(wtf, 0, TILES * WZ).rearrange("p (t n) -> p t n", t=TILES)
        relu = at(wtf, 3456, 2 * 640).rearrange("p (b n) -> p b n", b=2)
        score = at(wtf, 4736, 640)
        cki = at(wtf, 5376, 2 * PAST).rearrange("p (b n) -> p b n", b=2)
        bar = at(wtf, 6400, 2 * P)
        prob_p = relu
        probT_p = at(wtf, 6656, 1024).rearrange("p (b n) -> p b n", b=2)
        mixT = at(wtf, 2 * SLOT, KC * NTOK).rearrange("p (c t) -> p c t", c=KC)
        am1 = at(wtf, 2 * SLOT + 3072, 512).rearrange("p (h i) -> p h i", h=HB)
        am2 = at(wtf, 2 * SLOT + 3584, 512).rearrange("p (h i) -> p h i", h=HB)
        prod = at(wtf, 3 * SLOT, 1024).rearrange("p (e i q h d) -> p e i q h d", e=2, i=2, q=2, h=HB)
        snew = at(wtf, 3 * SLOT, 2048).rearrange("p (q h v) -> p q h v", q=4, h=HB)
        prob = at(wtf, 3 * SLOT + 2048, 1280).rearrange("p (b n) -> p b n", b=2)
        selb = at(wtf, 3 * SLOT + 3328, 512).bitcast(BF16).rearrange("p (b k t) -> p b k t", b=STREAMS, k=8)
        snp = at(wtf, 3 * SLOT + 3840, 256).rearrange("p (q v) -> p q v", q=2)
        probT = at(wtf, 4 * SLOT + 2048, 1280).rearrange("p (b n) -> p b n", b=2)
        dmask_s = at(wtf, 4 * SLOT + 3328, 512)
        kz = at(wtf, 5 * SLOT, 2048).rearrange("p (q h e d) -> p q h e d", q=4, h=HB, e=2)
        s0 = at(wtf, 5 * SLOT + 2048, 2048).rearrange("p (q h v) -> p q h v", q=4, h=HB)
        ckv = [at(wtf, 4 * SLOT + b % 7 * 1024, 1024) if b in (0, 1, 7) else
               at(rowf, 12288 + (b - 2) * 1024, 1024) if b < 5 else at(rowf, (b - 5) * 1024, 1024)
               for b in range(STREAMS)]
        PLACE = (2, 3, 4, 0, 1, 5, 6, 7)
        row = [rows[:, place, :] for place in PLACE]
        diag = dmask[:, :, :].rearrange("p h (i n) -> p (h i) n", n=P)
        gfb = at(wtf, 2048, D)
        vb = at(work, 0, TILES * 512).rearrange("p (t n) -> p t n", t=TILES)
        gs = at(work, 1536, TILES * 512).rearrange("p (t n) -> p t n", t=TILES)
        rot = at(work, 3072, TILES * 512).rearrange("p (t h e d) -> p t h e d", t=TILES, h=2 * HB, e=2)
        h2 = (at(work, 0, D), at(wtf, 1024, D))
        h2T = at(work, 1024, D).rearrange("p (c t) -> p c t", c=KC)
        qT = at(work, 2048, 512).rearrange("p (b e t) -> p b e t", b=2, e=2)
        rest = (at(work, 2560, P), at(work, 4480, P))
        cand = at(work, 2688, 256)
        cand2 = at(work, 2944, 256)
        hot = at(work, 3200, 512).rearrange("p (e k r) -> p e k r", e=2, k=KP)
        hoti = at(work, 3712, 512).rearrange("p (e k r) -> p e k r", e=2, k=KP)
        top = at(work, 4224, 32).rearrange("p (e k) -> p e k", e=2)
        topi = at(work, 4256, 32).bitcast(U32).rearrange("p (e k) -> p e k", e=2)
        topf = at(work, 4288, 32).rearrange("p (e k) -> p e k", e=2)
        best = at(work, 4320, KP)
        besti = at(work, 4336, KP).bitcast(U32)
        rank = at(work, 4352, 32).bitcast(U32).rearrange("p (e k) -> p e k", e=2)
        rankf = at(work, 4384, 32).rearrange("p (e k) -> p e k", e=2)
        half_id = at(work, 4416, 32).rearrange("p (e k) -> p e k", e=2)
        ebest = at(work, 4448, 2 * KP).rearrange("p (b k) -> p b k", b=2)
        NAMES = ["kv", "qi", "qa", "vb", "gb", "qkb", "out0", "out1", "q0", "q1", "q2", "q3"]
        w_in = {n: sem("w_" + n) for n in NAMES}
        x_in = [sem(f"x_in{t}") for t in range(TILES)]
        g1_in, ident_in, small_in, bar_in, keys_in = (sem(n) for n in ("g1_in", "ident_in", "small_in", "bar_in", "keys_in"))
        gf_in, s0_in, dms_in = sem("gf_in"), sem("s0_in"), sem("dms_in")
        cki_in = [sem(f"cki_in{i}") for i in range(2)]
        ckv_in = [sem(f"ckv_in{i}") for i in range(STREAMS)]
        out_done = sem("out_done")
        sqd, msd, rsd, hready, x1_done = (sem(n) for n in ("squares", "mean_square", "rstd", "h_ready", "x1_done"))
        ht_ps, ht_act, ht_dve = sem("ht_ps"), sem("ht_act"), sem("ht_dve")
        proj, proj_act, proj_dve = sem("proj"), sem("proj_act"), sem("proj_dve")
        kt_ps, kt_sb = sem("kt_ps"), sem("kt_sb")
        w_ps, wz_zero, wz_set = sem("w_ps"), sem("wz_zero"), sem("wz_set")
        dots, relued, combined, scored, biased = (sem(n) for n in ("dots", "relued", "combined", "scored", "biased"))
        rt_ps, rt_sb, s_ps, s_masked = sem("rt_ps"), sem("rt_sb"), sem("s_ps"), sem("s_masked")
        zeroed, kdec, qz_set, qzb_set, sel_set = (sem(n) for n in ("zeroed", "kdec", "qz_set", "qzb_set", "sel_set"))
        o_ps, o_norm, o_var, o_rstd, sp_ps, sp_sb, ss_ps, ss_sb = (sem(n) for n in (
            "o_ps", "o_norm", "o_var", "o_rstd", "sp_ps", "sp_sb", "ss_ps", "ss_sb"))
        mt_ps, mt_sb, q_twice = sem("mt_ps"), sem("mt_sb"), sem("q_twice")
        sc_ps, smax, expd, pscaled, pt_ps, pt_sb, pv_ps, pv_sb = (sem(n) for n in (
            "sc_ps", "smax", "expd", "pscaled", "pt_ps", "pt_sb", "pv_ps", "pv_sb"))
        wout, h2t_ps, h2t_act, h2t_dve = sem("wout"), sem("h2t_ps"), sem("h2t_act"), sem("h2t_dve")
        q_ps, q_sb, sc2_ps, topped, best_set, gexp, picked = (sem(n) for n in (
            "q_ps", "q_sb", "sc2_ps", "topped", "best_set", "gexp", "picked"))
        staged, seen, dotted, gelued, diagd, acc, y_init, y_read, y_out = (sem(n) for n in (
            "staged", "seen", "dotted", "gelued", "diagd", "acc", "y_init", "y_read", "y_out"))
        landed = [sem(f"landed{s}") for s in range(G)]
        chain = sem("dve_chain")

        slot_of = {"kv": 0, "qi": 1, "qa": 2, "vb": 3, "gb": 4, "qkb": 5, "out0": 0, "out1": 1,
                   "q0": 5, "q1": 3, "q2": 4, "q3": 2}
        width = {"kv": NKV}

        def wv(name):
            w = width.get(name, 512)
            return wt[:, slot_of[name], 0:KC * w].rearrange("p (c n) -> p c n", c=KC)

        def load_w(eng, name):
            w = width.get(name, 512)
            eng.dma_start(wt[:, slot_of[name], 0:KC * w], a["w_" + name]).then_inc(w_in[name], 16)

        UN = ([("kv", "n", t) for t in range(TILES)] + [("qi", "t", j) for j in range(4)]
              + [("qa", "t", g) for g in range(GRP)] + [("vb", "n", t) for t in range(TILES)]
              + [("gb", "n", t) for t in range(TILES)] + [("qkb", "n", t) for t in range(TILES)])
        N_ACT = 17
        PROMPT_ATT = 2 * GRP
        ATT = [(t, g) for t in range(2) for g in range(GRP)] + [(2, b) for b in range(STREAMS)]

        def q_psum(u):
            return ps[:, 2 + u % 2, 0:256] if u else ps[:, 7, 0:256]

        def sc_psum(u):
            return ps[:, 4 + u % 2, 0:256] if u else ps[:, 7, 256:512]

        block = ctx.enter_context(nc.Block())

        @block.sync
        def _(sp):
            sp.dma_start(x[:, 0, :], a["x"][0]).then_inc(x_in[0], 16)
            sp.dma_start(g1b, a["ln1_g"].partition_broadcast(P)).then_inc(g1_in, 16)
            sp.dma_start(ident[:], a["ident"]).then_inc(ident_in, 16)
            sp.dma_start(half4[:], a["half"]).then_inc(ident_in, 16)
            for t in (1, 2):
                sp.dma_start(x[:, t, :], a["x"][t]).then_inc(x_in[t], 16)
            load_w(sp, "kv")
            load_w(sp, "qi")
            for name, dst in (("e8", e8[:]), ("m16", m16[:]), ("iota", iota[:]), ("kd", kd[:]),
                              ("cs", cs[:, :, :, :, :].rearrange("p a b c d -> p (a b c d)")),
                              ("dmask", dmask[:, :, :].rearrange("p a b -> p (a b)")),
                              ("qmask", qmask[:, :, :].rearrange("p a b -> p (a b)"))):
                sp.dma_start(dst, a[name]).then_inc(small_in, 16)
            for name in ("qa", "vb", "gb", "qkb"):
                load_w(sp, name)
            sp.dma_start(keysT[:, :, :].rearrange("p a b -> p (a b)"), a["keysT"]).then_inc(keys_in, 16)
            sp.dma_start(g2b[:], a["ln2_g"].partition_broadcast(P)).then_inc(keys_in, 16)
            sp.wait_ge(proj, 7)
            sp.dma_start(bar, a["bar"]).then_inc(bar_in, 16)
            sp.wait_ge(proj, 17)
            sp.dma_start(dmask_s, a["dmask_s"]).then_inc(dms_in, 16)
            sp.wait_ge(biased, 3)
            sp.wait_ge(pv_ps, PROMPT_ATT)
            load_w(sp, "out0")
            sp.wait_ge(proj, len(UN))
            for e in range(2):
                sp.dma_start(s0[64 * e:64 * e + 64, :, :, :], a["s0"][e]).then_inc(s0_in, 16)
            load_w(sp, "out1")
            sp.wait_ge(proj_act, 3)
            for t in range(TILES):
                for k, (c0, c1) in enumerate(((0, P), (P, 2 * P), (2 * P, 2 * P + DH))):
                    sp.dma_start(o["kv"][t][k], kvnat[:, t, c0:c1]).then_inc(out_done, 16)
            sp.wait_ge(sp_sb, 2)
            sp.dma_start(o["state_p"], snp).then_inc(out_done, 16)
            sp.wait_ge(ss_sb, HB)
            for e in range(2):
                sp.dma_start(o["state_s"][e], snew[64 * e:64 * e + 64, :, :, :]).then_inc(out_done, 16)
            load_w(sp, "q0")
            sp.wait_ge(out_done, 16 * 12)
            sp.wait_ge(pv_sb, 2 * len(ATT))
            load_w(sp, "q1")
            load_w(sp, "q2")
            sp.wait_ge(wout, TILES)
            load_w(sp, "q3")
            sp.dma_start(gfb, a["ln_final_g"].partition_broadcast(P)).then_inc(gf_in, 16)
            for t in range(TILES):
                sp.wait_ge(y_out, t + 1)
                sp.dma_start(o["y"][t], x[:, t, :]).then_inc(out_done, 16)
            sp.wait_ge(out_done, 16 * 15)

        @block.gpsimd
        def _(pool):
            def take_rstd(n):
                pool.wait_ge(msd, n + 1)
                pool.tensor_tensor(rstd[:, n:n + 1], ms[:, n:n + 1], half4[:, 0:1], ALU.pow).then_inc(rsd, 1)

            pool.wait_ge(ident_in, 32)
            for n in range(TILES):
                take_rstd(n)
            pool.wait_ge(proj, 3)
            pool.memset(at(wtf, 0, TILES * WZ), 0.0).then_inc(wz_zero, 1)
            pool.wait_ge(proj, 7)
            for b in range(STREAMS):
                if b >= 2:
                    pool.wait_ge(dots, 16 + b - 1)
                pool.dma_start(cki[0:DH, b % 2, :], a["cki"][b]).then_inc(cki_in[b % 2], 16)
            def load_ckv(b):
                for k in range(2):
                    pool.dma_start(ckv[b][:, k * PAST:(k + 1) * PAST], a["ckv"][b][k]).then_inc(ckv_in[b], 16)

            pool.wait_ge(proj, 17)
            for b in range(2):
                load_ckv(b)
            pool.wait_ge(proj, len(UN))
            pool.memset(at(rowf, 0, 3584), 0.0).then_inc(zeroed, 1)
            for t in range(TILES):
                pool.wait_ge(o_var, t + 1)
                pool.tensor_tensor(rstd4[:], veps[:], half4[:], ALU.pow).then_inc(o_rstd, 1)
            pool.wait_ge(o_ps, TILES)
            for b in range(2, STREAMS - 1):
                load_ckv(b)
            take_rstd(TILES)
            pool.wait_ge(pv_ps, PROMPT_ATT + 1)
            load_ckv(STREAMS - 1)

            def gathers(par, g, unit, first=False):
                pool.wait_ge(picked, unit + 1)
                if not first:
                    pool.sem_inc(seen)
                pool.tensor_copy(stage[:, par, :], ids[:, bass.ds(g * G, G)]).then_inc(staged, 1)
                for s in range(G):
                    if s == 0:
                        pool.wait_ge(staged, g + 1)
                        if first:
                            pool.wait_ge(mt_ps, TILES)
                            pool.wait_ge(qzb_set, 2)
                    if s == 3 and first:
                        pool.wait_ge(pv_ps, len(ATT))
                    if s == 7 and first:
                        pool.wait_ge(out_done, 16 * 12)
                    if not first:
                        pool.wait_ge(acc, (g - 1) * G + s + 1)
                    pool.sem_inc(seen)
                    pool.indirect_dma_start(row[s], None, a["uv"], bass.IndirectOffsetOnAxis(
                        ap=stage[:, par, s:s + 1], axis=0)).then_inc(landed[s], 16)

            def span(g0, g1):
                pairs = (g1 - g0) // 2
                with pool.Fori(0, pairs) as i:
                    gathers(1, i * 2 + g0, i + (g0 - 1) // 2)
                    gathers(0, i * 2 + (g0 + 1), i + (g0 + 1) // 2)
                if (g1 - g0) % 2:
                    gathers(1, g1 - 1, (g1 - 1) // 2)

            per_tile = HP * GROUPS
            gathers(0, 0, 0, first=True)
            span(1, 7)
            take_rstd(TILES + 1)
            take_rstd(TILES + 2)
            span(7, per_tile + 5)
            take_rstd(2 * TILES)
            span(per_tile + 5, 2 * per_tile + 5)
            take_rstd(2 * TILES + 1)
            span(2 * per_tile + 5, 3 * per_tile)
            take_rstd(2 * TILES + 2)

        @block.tensor
        def _(pe):
            def mm(out, lhsT, rhs, start=True, stop=True):
                return nc.tensor.matmul(out, lhsT, rhs, start=start, stop=stop)

            def tr(out, in_, k=P):
                return nc.tensor.transpose(out, in_, ident[0:k, 0:k])

            pe.wait_ge(ident_in, 32)
            for t in range(TILES):
                pe.wait_ge(hready, t + 1)
                if t == 2:
                    pe.wait_ge(ht_act, 1)
                    pe.wait_ge(ht_dve, 1)
                for c in range(KC):
                    last = tr(ps[:, 2 * (t % 2) + c // 4, (c % 4) * P:(c % 4 + 1) * P], hnat[:, t % 2, c * P:(c + 1) * P])
                last.then_inc(ht_ps, 1)

            def unit(n):
                name, kind, i = UN[n]
                if i == 0:
                    pe.wait_ge(w_in[name], 16)
                if n == 0:
                    pe.wait_ge(ht_act, TILES)
                    pe.wait_ge(ht_dve, TILES)
                if n >= 2:
                    if n - 2 < N_ACT:
                        pe.wait_ge(proj_act, n - 1)
                    else:
                        pe.wait_ge(proj_dve, n - 1 - N_ACT)
                w, bank = wv(name), 6 + n % 2
                for c in range(KC):
                    if kind == "n":
                        last = mm(ps[:, bank, 0:width.get(name, 512)], hT[:, c, i * P:(i + 1) * P], w[:, c, :],
                                  c == 0, c == KC - 1)
                    else:
                        last = mm(ps[:, bank, 0:NTOK], w[:, c, i * P:(i + 1) * P], hT[:, c, :], c == 0, c == KC - 1)
                last.then_inc(proj, 1)

            for n in range(3):
                unit(n)
            pe.wait_ge(proj_act, 3)
            for t in range(TILES):
                tr(ps[:, 0, t * P:(t + 1) * P], kvnat[:, t, 0:P])
                last = tr(ps[0:DH + HI, 1, t * P:(t + 1) * P], kvnat[:, t, 2 * P:NKV])
            last.then_inc(kt_ps, 1)
            for n in range(3, 7):
                unit(n)
            pe.wait_ge(kt_sb, 2)
            pe.wait_ge(small_in, 16 * 7)
            mm(ps[:, 2, 0:NTOK], e8[DH:DH + HI, :], kiwT[DH:DH + HI, :]).then_inc(w_ps, 1)

            def index_dots(m):
                t, g = divmod(m, 8)
                if m == 0:
                    pe.wait_ge(proj_act, 7)
                if m == 1:
                    pe.wait_ge(wz_set, TILES)
                if m >= 2:
                    pe.wait_ge(relued, m - 1)
                lhs = qiT[0:DH, m, :, :]
                b = 2 * (m % 2)
                if t < 2:
                    last = mm(ps[:, b, 0:KEYS[t]], lhs, kiwT[0:DH, 0:KEYS[t]])
                else:
                    pe.wait_ge(cki_in[g % 2], 16 * (g // 2 + 1))
                    mm(ps[:, b, :], lhs, cki[0:DH, g % 2, :])
                    last = mm(ps[:, b + 1, 0:P], lhs, kiwT[0:DH, 2 * P:3 * P])
                last.then_inc(dots, 1)

            def index_sum(m):
                t, g = divmod(m, 8)
                if m == 0:
                    pe.wait_ge(wz_set, TILES)
                if g == 0 and t > 0:
                    pe.wait_ge(scored, t)
                pe.wait_ge(relued, m + 1)
                lhs = wz[:, t, g * P:(g + 1) * P]
                if t < 2:
                    last = mm(ps[:, 4, 0:KEYS[t]], lhs, relu[:, m % 2, 0:KEYS[t]], g == 0, g == 7)
                else:
                    mm(ps[:, 4, :], lhs, relu[:, m % 2, 0:512], g == 0, g == 7)
                    last = mm(ps[:, 5, 0:P], lhs, relu[:, m % 2, 512:640], g == 0, g == 7)
                last.then_inc(combined, 1)

            for m in range(25):
                if m < 24:
                    index_dots(m)
                if m >= 1:
                    index_sum(m - 1)
            def att_scores(n):
                t, i = ATT[n]
                b = 2 * (n % 2)
                if n == 0:
                    pe.wait_ge(relued, 24)
                if n == PROMPT_ATT:
                    pe.wait_ge(mt_sb, TILES)
                    pe.wait_ge(sp_sb, 2)
                    pe.wait_ge(sel_set, 1)
                    pe.wait_ge(qzb_set, 2)
                if t < 2:
                    pe.wait_ge(proj_act, 7 + i + 1)
                if i == 0:
                    pe.wait_ge(biased, t + 1)
                if n % PROMPT_ATT >= 2:
                    pe.wait_ge(expd, n - 1)
                if t < 2:
                    for k in range(KVH):
                        r = slice(64 * k, 64 * k + 64)
                        out = ps[:, b + k, 0:KEYS[t]]
                        mm(out, qaT[r, i, t * P:(t + 1) * P], kaT[r, 0:KEYS[t]], True, False)
                        last = mm(out, ident_bf[:], bias[t], False, True)
                else:
                    pe.wait_ge(ckv_in[i], 32)
                    lhs = qzb[:, i, :, :, :]
                    mm(ps[:, b, :], lhs, ckv[i][:, 0:PAST], True, False)
                    mm(ps[:, b, :], selb[:, i, :, :], bias[2][:, 0:512], False, True)
                    mm(ps[:, b + 1, 0:P], lhs, kaT[:, 2 * P:3 * P], True, False)
                    last = mm(ps[:, b + 1, 0:P], selb[:, i, :, :], bias[2][:, 512:640], False, True)
                last.then_inc(sc_ps, 1)

            def att_out(n):
                t, i = ATT[n]
                pe.wait_ge(pscaled, n + 1)
                if n == 0:
                    pe.wait_ge(scored, 3)
                if n == PROMPT_ATT:
                    pe.wait_ge(h2t_act, 1)
                    pe.wait_ge(h2t_dve, 1)
                if n >= 1:
                    pe.wait_ge(pt_sb, n)
                if t < 2:
                    for c in range(t + 1):
                        for k in range(KVH):
                            last = tr(ps[:, 4, c * 256 + k * P:c * 256 + (k + 1) * P],
                                      prob_p[:, n % 2, k * 256 + c * P:k * 256 + (c + 1) * P])
                else:
                    for c in range(5):
                        last = tr(psf[:, 4 * 512 + c * P:4 * 512 + (c + 1) * P], prob[:, n % 2, c * P:(c + 1) * P])
                last.then_inc(pt_ps, 1)
                if n % PROMPT_ATT + 2 < PROMPT_ATT:
                    att_scores(n + 2)
                pe.wait_ge(pt_sb, n + 1)
                if n >= 1:
                    pe.wait_ge(pv_sb, 2 * n)
                if t < 2:
                    for c in range(t + 1):
                        last = mm(ps[:, 5, 0:256], kvnat[:, c, P:2 * P], probT_p[:, n % 2, c * 256:(c + 1) * 256], c == 0, c == t)
                else:
                    for c in range(5):
                        lhs = ckv[i][:, PAST + c * P:PAST + (c + 1) * P] if c < 4 else kvnat[:, 2, P:2 * P]
                        last = mm(ps[:, 6, 0:P], lhs, probT[:, n % 2, c * P:(c + 1) * P], c == 0, c == 4)
                last.then_inc(pv_ps, 1)

            for n in range(7, len(UN)):
                unit(n)
                if n in (9, 10):
                    att_scores(n - 9)
                if 11 <= n < 11 + PROMPT_ATT:
                    att_out(n - 11)


            pe.wait_ge(expd, PROMPT_ATT)
            for t in range(2):
                pe.wait_ge(proj_dve, t + 1)
                for s in range(4):
                    last = tr(ps[:, t, s * P:(s + 1) * P], rot[:, t, 2 * s:2 * s + 2, :, :])
                last.then_inc(rt_ps, 1)
            pe.wait_ge(q_twice, 2)
            for h in range(HB):
                last = tr(ps[:, 2, h * P:(h + 1) * P], rotq2[:, h, :, :, :])
            last.then_inc(rt_ps, 1)
            for s in range(2):
                last = tr(ps[:, 3, s * P:(s + 1) * P], rot[:, 2, HB + 2 * s:HB + 2 * s + 2, :, :])
            last.then_inc(rt_ps, 1)
            pe.wait_ge(rt_sb, 4)
            pe.wait_ge(pt_sb, PROMPT_ATT)
            pe.wait_ge(pv_sb, 2 * PROMPT_ATT)
            for h in range(HB):
                r = slice(64 * (h % 2), 64 * (h % 2) + 64)
                last = mm(ps[:, 4 + h % 2, (h // 2) * 256:(h // 2) * 256 + 256],
                          rT[r, 0, 2 + h // 2, :], rT[r, :, h // 2, :])
            last.then_inc(s_ps, 1)
            for h in range(HB):
                r = slice(64 * (h % 2), 64 * (h % 2) + 64)
                last = mm(ps[:, 6 + h % 2, (h // 2) * P:(h // 2 + 1) * P], rT[r, 1, 2 + h // 2, :], rT[r, 1, h // 2, :])
            last.then_inc(s_ps, 1)
            for h in range(HB):
                r = slice(64 * (h % 2), 64 * (h % 2) + 64)
                last = mm(ps[:, 6 + h % 2, (2 + h // 2) * P:(3 + h // 2) * P], kTs[r, h // 2, :], qTd[r, h, :])
            last.then_inc(s_ps, 1)
            pe.wait_ge(s_masked, 3)
            for h in range(HB):
                last = mm(ps[:, 0, h * P:(h + 1) * P], am0[:, h, 0:P], vb[:, 0, h * P:(h + 1) * P])
            last.then_inc(o_ps, 1)
            for h in range(HB):
                mm(ps[:, 1, h * P:(h + 1) * P], am0[:, h, P:2 * P], vb[:, 0, h * P:(h + 1) * P], True, False)
                last = mm(ps[:, 1, h * P:(h + 1) * P], am1[:, h, :], vb[:, 1, h * P:(h + 1) * P], False, True)
            last.then_inc(o_ps, 1)
            pe.wait_ge(s_masked, 4)
            pe.wait_ge(qz_set, HB)
            pe.wait_ge(s0_in, 32)
            for h in range(HB):
                mm(ps[:, 2, h * P:(h + 1) * P], am2[:, h, :], vb[:, 2, h * P:(h + 1) * P], True, False)
                for q in range(4):
                    last = mm(ps[:, 2, h * P:(h + 1) * P], qz[:, h, q * P:(q + 1) * P], s0[:, q, h, :], False, q == 3)
            last.then_inc(o_ps, 1)
            pe.wait_ge(kdec, 4)
            for q in range(2):
                for t in range(2):
                    last = mm(ps[:, 3, q * 256:(q + 1) * 256], kdn[:, t, 2 * q:2 * q + 2, :],
                              vb[:, t, q * 256:(q + 1) * 256], t == 0, t == 1)
            last.then_inc(sp_ps, 1)
            for q in range(4):
                for h in range(HB):
                    last = mm(ps[:, 4 + q, h * P:(h + 1) * P], kz[:, q, h, :, :], vb[:, 2, h * P:(h + 1) * P])
            last.then_inc(ss_ps, 1)

            def mix_t(t):
                pe.wait_ge(o_norm, t + 1)
                for c in range(4):
                    last = tr(ps[:, t, c * P:(c + 1) * P], mixnat[:, t, c * P:(c + 1) * P])
                last.then_inc(mt_ps, 1)

            def out_proj(t, bank):
                if t == 0:
                    pe.wait_ge(w_in["out0"], 16)
                    pe.wait_ge(w_in["out1"], 16)
                    pe.wait_ge(mt_sb, 1)
                    pe.wait_ge(ss_sb, HB)
                if t == 2:
                    pe.wait_ge(x1_done, 2)
                for e in range(2):
                    w = wv(f"out{e}")
                    for c in range(KC):
                        last = mm(ps[:, bank + e, :], mixT[:, c, t * P:(t + 1) * P], w[:, c, :], c == 0, c == KC - 1)
                last.then_inc(wout, 1)

            def h2_t(t, bank):
                pe.wait_ge(hready, TILES + t + 1)
                if t > 0:
                    pe.wait_ge(x1_done, TILES)
                    pe.wait_ge(h2t_act, t)
                    pe.wait_ge(h2t_dve, t)
                for c in range(KC):
                    last = tr(ps[:, bank + c // 4, (c % 4) * P:(c % 4 + 1) * P], h2[t % 2][:, c * P:(c + 1) * P])
                last.then_inc(h2t_ps, 1)

            def query(u):
                t, h = divmod(u, HP)
                if h == 0:
                    pe.wait_ge(h2t_act, t + 1)
                    pe.wait_ge(h2t_dve, t + 1)
                if t == 0 and h % 2 == 0:
                    pe.wait_ge(w_in[f"q{h // 2}"], 16)
                w = wv(f"q{h // 2}")
                for e in range(2):
                    col = (h % 2) * 256 + e * P
                    for c in range(KC):
                        last = mm(q_psum(u)[:, e * P:(e + 1) * P], w[:, c, col:col + P], h2T[:, c, :], c == 0, c == KC - 1)
                last.then_inc(q_ps, 1)

            def query_scores(u):
                if u >= 2:
                    pe.wait_ge(topped, u - 1)
                pe.wait_ge(q_sb, u + 1)
                for e in range(2):
                    last = mm(sc_psum(u)[:, e * P:(e + 1) * P], qT[:, u % 2, e, :], keysT[:, e, :])
                last.then_inc(sc2_ps, 1)

            def y_start(t):
                if t > 0:
                    pe.wait_ge(y_read, t)
                else:
                    pe.wait_ge(topped, 1)
                pe.wait_ge(x1_done, t + 1)
                for e in range(2):
                    last = mm(ps[:, 6 + e, :], ident[:], x[:, t, e * 512:(e + 1) * 512], True, False)
                last.then_inc(y_init, 1)

            def add_expert(n, s, stop=False):
                pe.wait_ge(diagd, n + 1)
                for e in range(2):
                    last = mm(ps[:, 6 + e, :], diag[:, s, :], row[s][:, D + e * 512:D + (e + 1) * 512], False, stop)
                last.then_inc(acc, 1)
                return last

            def picks(u):
                final = u % HP == HP - 1
                if final:
                    for s in range(G):
                        add_expert(u * KP + s, s)
                    for s in range(G):
                        add_expert(u * KP + G + s, s, s == G - 1)
                else:
                    with pe.Fori(0, GROUPS) as i:
                        for s in range(G):
                            add_expert(i * G + (u * KP + s), s)

            mix_t(0)
            out_proj(0, 6)
            mix_t(1)
            mix_t(2)
            att_scores(PROMPT_ATT)
            att_scores(PROMPT_ATT + 1)
            h2_t(0, 4)
            pe.wait_ge(keys_in, 32)
            for n in range(PROMPT_ATT, len(ATT)):
                att_out(n)
                if n == PROMPT_ATT:
                    query(0)
                if n == PROMPT_ATT + 1:
                    query_scores(0)
            pe.wait_ge(expd, len(ATT))
            pe.wait_ge(pv_sb, 2 * len(ATT))
            for u in (1, 2):
                query(u)
                query_scores(u)
            for u in range(UNITS):
                t, h = divmod(u, HP)
                if h == 0:
                    y_start(t)
                picks(u)
                if u + 3 < UNITS:
                    query(u + 3)
                    query_scores(u + 3)
                if u + 1 < TILES:
                    out_proj(u + 1, 0)
                if h == HP - 4 and t + 1 < TILES:
                    h2_t(t + 1, 0)

        @block.scalar
        def _(act):
            def A(*args, **kw):
                return nc.scalar.activation(*args, **kw)

            def copy(out, in_):
                return A(out, in_, ACT.Copy)

            def take_hT(t):
                act.wait_ge(ht_ps, t + 1)
                copy(hT[:, 0:4, t * P:(t + 1) * P], ps[:, 2 * (t % 2), :].rearrange("p (c t) -> p c t", c=4)).then_inc(ht_act, 1)

            for t in range(TILES):
                act.wait_ge(x_in[t], 16)
                if t == 2:
                    act.wait_ge(ht_ps, 1)
                A(hnat[:, t % 2, :], x[:, t, :], ACT.Square, accum_out=sumsq[:, t:t + 1]).then_inc(sqd, 1)
                if t >= 1:
                    take_hT(t - 1)
            take_hT(2)

            def take(n):
                name, kind, i = UN[n]
                act.wait_ge(proj, n + 1)
                src = ps[:, 6 + n % 2, :]
                if name == "kv":
                    copy(kvnat[:, i, :], src[:, 0:NKV]).then_inc(proj_act, 1)
                elif name == "qi":
                    for e in range(2):
                        ins = copy(qiT[0:64, :, 2 * i + e, :],
                                   src[64 * e:64 * e + 64, 0:NTOK].rearrange("p (g t) -> p g t", t=STEPS))
                    ins.then_inc(proj_act, 1)
                elif name == "qa":
                    copy(qaT[:, i, :], src[:, 0:NTOK]).then_inc(proj_act, 1)
                elif name == "vb":
                    copy(vb[:, i, :], src).then_inc(proj_act, 1)
                else:
                    A(gs[:, i, :], src, ACT.Silu).then_inc(proj_act, 1)

            for n in range(7):
                take(n)
            for m in range(24):
                t, g = divmod(m, 8)
                act.wait_ge(dots, m + 1)
                if m >= 2:
                    act.wait_ge(combined, m - 1)
                k = KEYS[t]
                A(relu[:, m % 2, 0:k], psf[:, 1024 * (m % 2):1024 * (m % 2) + k], ACT.Relu).then_inc(relued, 1)
            def att_exp(n):
                t, i = ATT[n]
                act.wait_ge(smax, n + 1)
                if n == 0:
                    act.wait_ge(combined, 24)
                if n >= 2:
                    act.wait_ge(pt_ps, n - 1)
                c = n % 2
                if t < 2:
                    for k in range(KVH):
                        ins = A(prob_p[:, c, k * 256:k * 256 + KEYS[t]], ps[:, 2 * c + k, 0:KEYS[t]], ACT.Exp,
                                bias=negmax[:, c, k:k + 1], scale=DH ** -0.5, accum_out=esum[:, c, k:k + 1])
                else:
                    ins = A(prob[:, c, :], psf[:, 1024 * c:1024 * c + 640], ACT.Exp,
                            bias=negmax[:, c, 0:1], scale=DH ** -0.5, accum_out=esum[:, c, 0:1])
                ins.then_inc(expd, 1)

            def att_take(n):
                t, i = ATT[n]
                c = n % 2
                act.wait_ge(pt_ps, n + 1)
                if n >= 2:
                    act.wait_ge(pv_ps, n - 1)
                if t < 2:
                    k = 256 * (t + 1)
                    copy(probT_p[:, c, 0:k], ps[:, 4, 0:k]).then_inc(pt_sb, 1)
                else:
                    copy(probT[:, c, :], psf[:, 2048:2048 + 640]).then_inc(pt_sb, 1)
                if n % PROMPT_ATT + 2 < PROMPT_ATT:
                    att_exp(n + 2)
                act.wait_ge(pv_ps, n + 1)
                for k in range(KVH):
                    r = slice(64 * k, 64 * k + 64)
                    if t < 2:
                        copy(mixT[r, i, t * P:(t + 1) * P], ps[r, 5, k * P:(k + 1) * P]).then_inc(pv_sb, 1)
                    else:
                        copy(mixT[r, 0:GRP, 2 * P + i * STEPS:2 * P + (i + 1) * STEPS],
                             ps[r, 6, k * 64:(k + 1) * 64].rearrange("p (g t) -> p g t", g=GRP)).then_inc(pv_sb, 1)

            for n in range(7, 11 + PROMPT_ATT):
                if n < N_ACT:
                    take(n)
                if n in (9, 10):
                    att_exp(n - 9)
                if n >= 11:
                    att_take(n - 11)

            act.wait_ge(proj, len(UN))
            for t in range(2):
                act.wait_ge(rt_ps, t + 1)
                copy(rT[:, t, :, :], ps[:, t, :].rearrange("p (s t) -> p s t", s=4)).then_inc(rt_sb, 1)
            act.wait_ge(rt_ps, 3)
            copy(qTd, ps[:, 2, :].rearrange("p (h t) -> p h t", h=HB)).then_inc(rt_sb, 1)
            act.wait_ge(rt_ps, 4)
            copy(kTs, ps[:, 3, 0:256].rearrange("p (s t) -> p s t", s=2)).then_inc(rt_sb, 1)
            act.wait_ge(sp_ps, 1)
            for e in range(2):
                copy(snp[64 * e:64 * e + 64, :, :], ps[64 * e:64 * e + 64, 3, :].rearrange(
                    "p (q e v) -> p q e v", q=2, e=2)[:, :, e, :]).then_inc(sp_sb, 1)

            def square(n, src, scratch):
                A(scratch, src, ACT.Square, accum_out=sumsq[:, n:n + 1]).then_inc(sqd, 1)

            def h2_take(t, bank):
                act.wait_ge(h2t_ps, t + 1)
                copy(h2T[:, 0:4, :], ps[:, bank, :].rearrange("p (c t) -> p c t", c=4)).then_inc(h2t_act, 1)

            def take_q(u):
                act.wait_ge(q_ps, u + 1)
                if u >= 2:
                    act.wait_ge(sc2_ps, u - 1)
                copy(qT[:, u % 2, :, :], q_psum(u).rearrange("p (e t) -> p e t", e=2)).then_inc(q_sb, 1)

            def gate_exp(u):
                act.wait_ge(best_set, u + 1)
                A(ebest[:, u % 2, :], best, ACT.Exp, bias=negbest[:], accum_out=gsum[:, u % 2:u % 2 + 1]).then_inc(gexp, 1)

            def gelus(u):
                with act.Fori(0, GROUPS) as i:
                    for s in range(G):
                        act.wait_ge(dotted, i * G + (u * KP + s + 1))
                        A(zact[:, s:s + 1], zdot[:, s:s + 1], ACT.Gelu).then_inc(gelued, 1)

            def mix_take(t):
                act.wait_ge(mt_ps, t + 1)
                copy(mixT[:, 4:8, t * P:(t + 1) * P], ps[:, t, :].rearrange("p (c t) -> p c t", c=4)).then_inc(mt_sb, 1)

            mix_take(0)
            mix_take(1)
            mix_take(2)
            act.wait_ge(x1_done, 1)
            square(TILES, x[:, 0, :], h2[0])
            att_exp(PROMPT_ATT)
            att_exp(PROMPT_ATT + 1)
            h2_take(0, 4)
            for n in range(PROMPT_ATT, len(ATT)):
                att_take(n)
                if n == PROMPT_ATT:
                    take_q(0)
                if n == PROMPT_ATT + 3:
                    gate_exp(0)
            take_q(1)
            take_q(2)
            gate_exp(1)
            for u in range(UNITS):
                t, h = divmod(u, HP)
                gelus(u)
                if h == HP - 1:
                    act.wait_ge(y_read, t + 1)
                    square(2 * TILES + t, x[:, t, :], h2[t % 2])
                if u + 2 < UNITS:
                    gate_exp(u + 2)
                if u + 3 < UNITS:
                    take_q(u + 3)
                if u == 2:
                    act.wait_ge(x1_done, TILES)
                    square(TILES + 1, x[:, 1, :], h2[1])
                    act.wait_ge(msd, TILES + 2)
                    square(TILES + 2, x[:, 2, :], h2[1])
                if h == HP - 4 and t + 1 < TILES:
                    h2_take(t + 1, 0)

        @block.vector
        def _(dve):
            V = nc.vector
            count = {}

            def then(ins, s=chain):
                key = s.name
                count[key] = count.get(key, 0) + 1
                ins.then_inc(s, 1)
                dve.wait_ge(s, count[key])

            def mean_square(n):
                dve.wait_ge(sqd, n + 1)
                then(V.tensor_scalar(ms[:, n:n + 1], sumsq[:, n:n + 1], 1.0 / D, EPS, ALU.mult, ALU.add), msd)

            def normed(out, n, t, gain, s):
                dve.wait_ge(rsd, n + 1)
                then(V.scalar_tensor_tensor(out, x[:, t, :], rstd[:, n:n + 1], gain, ALU.mult, ALU.mult), s)

            dve.wait_ge(g1_in, 16)
            for t in range(TILES):
                mean_square(t)
                normed(hnat[:, t % 2, :], t, t, g1b, hready)
                if t >= 1:
                    dve.wait_ge(ht_ps, t)
                    then(V.tensor_copy(hT[:, 4:8, (t - 1) * P:t * P], ps[:, 2 * ((t - 1) % 2) + 1, :].rearrange(
                        "p (c t) -> p c t", c=4)), ht_dve)
            dve.wait_ge(ht_ps, 3)
            then(V.tensor_copy(hT[:, 4:8, 2 * P:3 * P], ps[:, 1, :].rearrange("p (c t) -> p c t", c=4)), ht_dve)
            dve.wait_ge(ident_in, 32)
            then(V.tensor_copy(ident_bf[:], ident[:]))
            dve.wait_ge(kt_ps, 1)
            then(V.tensor_copy(kaT, ps[:, 0, 0:NTOK]), kt_sb)
            then(V.tensor_copy(kiwT[0:DH + HI, :], ps[0:DH + HI, 1, 0:NTOK]), kt_sb)
            dve.wait_ge(w_ps, 1)
            dve.wait_ge(wz_zero, 1)
            dve.wait_ge(small_in, 16 * 7)
            for t in range(TILES):
                then(V.tensor_tensor(
                    wz[:, t, :].rearrange("p (g s) -> p g s", s=144)[:, :, 0:STEPS],
                    ps[:, 2, t * P:(t + 1) * P].rearrange("p (g s) -> p g s", g=8),
                    m16[:].rearrange("p (a s) -> p a s", a=1).broadcast_to([P, 8, STEPS]), ALU.mult), wz_set)
            def att_max(n):
                t, i = ATT[n]
                c = n % 2
                dve.wait_ge(sc_ps, n + 1)
                w = 2 if t < 2 else 1
                if t < 2:
                    src = ps[:, 2 * c:2 * c + 2, 0:KEYS[t]]
                else:
                    src = psf[:, 1024 * c:1024 * c + 640]
                then(V.tensor_reduce(rowmax[:, 0:w], src, AX.X, ALU.max))
                if n >= 2:
                    dve.wait_ge(expd, n - 1)
                then(V.tensor_scalar(negmax[:, c, 0:w], rowmax[:, 0:w], -(DH ** -0.5), None, ALU.mult), smax)

            def att_scale(n):
                t, i = ATT[n]
                c = n % 2
                w = 2 if t < 2 else 1
                dve.wait_ge(expd, n + 1)
                then(V.reciprocal(resum[:, 0:w], esum[:, c, 0:w]))
                if t < 2:
                    then(V.tensor_scalar(prob_p[:, c, 0:KEYS[t]], prob_p[:, c, 0:KEYS[t]], resum[:, 0:1], None, ALU.mult))
                    then(V.tensor_scalar(prob_p[:, c, 256:256 + KEYS[t]], prob_p[:, c, 256:256 + KEYS[t]], resum[:, 1:2], None, ALU.mult), pscaled)
                else:
                    then(V.tensor_scalar(prob[:, c, :], prob[:, c, :], resum[:, 0:1], None, ALU.mult), pscaled)

            def att_step(n):
                if n % PROMPT_ATT + 1 < PROMPT_ATT:
                    att_scale(n + 1)
                if n % PROMPT_ATT + 2 < PROMPT_ATT:
                    att_max(n + 2)

            def between(r):
                if r == 7:
                    att_max(0)
                if r == 9:
                    att_max(1)
                    att_scale(0)
                if r in (11, 13, 15):
                    att_step((r - 11) // 2)

            for t in range(TILES):
                k = KEYS[t]
                dve.wait_ge(combined, 8 * (t + 1))
                dve.wait_ge(bar_in, 16)
                if k > P:
                    then(V.tensor_copy(score[:, 0:k - P], psf[:, 2048:2048 + k - P]))
                then(V.tensor_tensor(score[:, k - P:k], psf[:, 2048 + k - P:2048 + k],
                                     bar[:, P * (t // 2):P * (t // 2) + P], ALU.add), scored)
                for r in range(0, TOPK[t], 8):
                    then(V.max(out=top8[:], in_=score[:, 0:k]))
                    if TOPK[t] - r < 8:
                        then(V.memset(top8[:, TOPK[t] - r:8], TAKEN))
                    then(V.match_replace(out=score[:, 0:k], in_to_replace=top8[:], in_values=score[:, 0:k],
                                         imm_value=TAKEN))
                    if t == 2:
                        between(r // 8)
                then(V.tensor_scalar(bias[t], score[:, 0:k], -3.36e38, OFF, ALU.is_gt, ALU.mult), biased)

            def rotate(t):
                dve.wait_ge(proj, N_ACT + t + 1)
                src = ps[:, 6 + (N_ACT + t) % 2, :].rearrange("p (q h e d) -> p q h e d", q=2, h=HB, e=2)
                dst = rot[:, t, :, :, :].rearrange("p (q h) e d -> p q h e d", q=2)
                for e in range(2):
                    for i in range(2):
                        tab = cs[:, t, i, :, :].rearrange("p q (a d) -> p q a d", a=1).broadcast_to([P, 2, HB, DK // 2])
                        ins = V.tensor_tensor(prod[:, e, i, :, :, :], src[:, :, :, e, :], tab, ALU.mult)
                then(ins)
                V.tensor_tensor(dst[:, :, :, 0, :], prod[:, 0, 0, :, :, :], prod[:, 1, 1, :, :, :], ALU.subtract)
                then(V.tensor_tensor(dst[:, :, :, 1, :], prod[:, 0, 1, :, :, :], prod[:, 1, 0, :, :, :], ALU.add), proj_dve)

            for n in range(3, 6):
                att_step(n)
            rotate(0)
            att_step(6)
            rotate(1)
            rotate(2)

            dve.wait_ge(proj, len(UN))
            for b in range(2):
                then(V.tensor_copy(rotq2[:, :, b, :, :], rot[:, 2, 0:HB, :, :]), q_twice)

            dve.wait_ge(proj, len(UN))
            dve.wait_ge(s_ps, 1)
            for e in range(2):
                then(V.tensor_tensor(am0[:, e::2, :], ps[:, 4 + e, :].rearrange("p (h i) -> p h i", h=2),
                                     dmask[:, e::2, :], ALU.mult), s_masked)

            def by_parity(v):
                return v.rearrange("p (i e) n -> p e i n", e=2)

            dve.wait_ge(s_ps, 3)
            then(V.tensor_tensor(by_parity(am1), ps[:, 6:8, 0:256].rearrange("p e (i n) -> p e i n", i=2),
                                 by_parity(dmask[:, :, 0:P]), ALU.mult), s_masked)
            dve.wait_ge(dms_in, 16)
            then(V.tensor_tensor(by_parity(am2), ps[:, 6:8, 256:512].rearrange("p e (i n) -> p e i n", i=2),
                                 by_parity(dmask_s.rearrange("p (h i) -> p h i", h=HB)), ALU.mult), s_masked)
            dve.wait_ge(zeroed, 1)
            dve.wait_ge(rt_sb, 4)
            for h in range(HB):
                then(V.tensor_tensor(qz[:, h, :].rearrange("p (q n) -> p q n", q=4)[:, :, 0:2 * STEPS],
                                     qTd[:, h, :].rearrange("p (q n) -> p q n", q=4),
                                     qmask[:, h, :].rearrange("p (q n) -> p q n", q=4), ALU.mult), qz_set)
            for t in range(2):
                then(V.tensor_tensor(kdn[:, t, :, :], rot[:, t, HB:2 * HB, :, :].rearrange("p h e d -> p h (e d)"),
                                     kd[:, t * HB:(t + 1) * HB].rearrange("p (h a) -> p h a", a=1).broadcast_to([P, HB, DK]),
                                     ALU.mult), kdec)
            for e in range(2):
                decay = kd[:, 2 * HB:].rearrange("p (q e h a) -> p q e h a", q=4, e=2, a=1)[:, :, e, :, :]
                then(V.tensor_tensor(kz[:, :, :, e, :], rot[:, 2:3, HB:2 * HB, :, :].rearrange(
                    "p q h e d -> p q h (e d)").broadcast_to([P, 4, HB, DK]), decay.broadcast_to([P, 4, HB, DK]), ALU.mult), kdec)
            then(V.tensor_copy(selb, ident_bf[:].rearrange("p (b a t) -> p b a t", b=STREAMS, a=1).broadcast_to(
                [P, STREAMS, 8, STEPS])), sel_set)
            for k in range(KVH):
                r = slice(64 * k, 64 * k + 64)
                then(V.tensor_copy(qzb[r, :, k, :, :], qaT[r, :, 2 * P:3 * P].rearrange("p g (b t) -> p b g t", b=STREAMS)), qzb_set)
            def group_norm(t):
                dve.wait_ge(o_ps, t + 1)
                for h in range(HB):
                    ins = V.bn_stats(out=bn6[:, h, :], in_=ps[:, t, h * P:(h + 1) * P])
                then(ins)
                for h in range(HB):
                    ins = V.bn_aggr(out=mv[:, h, :], in_=bn6[:, h, :])
                then(ins)
                then(V.tensor_scalar(veps[:], mv[:, :, 1], EPS, None, ALU.add), o_var)
                dve.wait_ge(o_rstd, t + 1)
                for h in range(HB):
                    ins = V.tensor_scalar(mixnat[:, t, h * P:(h + 1) * P], ps[:, t, h * P:(h + 1) * P],
                                          mv[:, h, 0:1], rstd4[:, h:h + 1],
                                          ALU.subtract, ALU.mult)
                then(ins)
                then(V.tensor_tensor(mixnat[:, t, :], mixnat[:, t, :], gs[:, t, :], ALU.mult), o_norm)
            group_norm(0)
            dve.wait_ge(ss_ps, 1)
            for h in range(HB):
                then(V.scalar_tensor_tensor(snew[:, :, h, :], s0[:, :, h, :], float(np.exp(STEPS * LG[h])),
                                            ps[:, 4:8, h * P:(h + 1) * P], ALU.mult, ALU.add), ss_sb)
            group_norm(1)
            group_norm(2)

            def add_mix(t, bank):
                dve.wait_ge(wout, t + 1)
                then(V.tensor_tensor(x[:, t, :], psf[:, bank * 512:(bank + 2) * 512], x[:, t, :], ALU.add), x1_done)

            def h2_take(t, bank):
                dve.wait_ge(h2t_ps, t + 1)
                then(V.tensor_copy(h2T[:, 4:8, :], ps[:, bank + 1, :].rearrange("p (c t) -> p c t", c=4)), h2t_dve)

            def top16_halves(u):
                dve.wait_ge(sc2_ps, u + 1)
                s = [sc_psum(u)[:, e * P:(e + 1) * P] for e in range(2)]
                for e in range(2):
                    ins = V.max(out=top[:, e, 0:8], in_=s[e])
                then(ins)
                for e in range(2):
                    ins = V.match_replace(out=rest[e], in_to_replace=top[:, e, 0:8], in_values=s[e], imm_value=TAKEN)
                then(ins)
                for e in range(2):
                    ins = V.max(out=top[:, e, 8:16], in_=rest[e])
                for e in range(2):
                    ins = V.max_index(topi[:, e, 0:8], top[:, e, 0:8], s[e])
                then(ins, topped)
                for e in range(2):
                    ins = V.max_index(topi[:, e, 8:16], top[:, e, 8:16], rest[e])
                then(ins)
                then(V.tensor_copy(topf, topi))

            def top16_pairs(u):
                c4 = cand.rearrange("p (i j) -> p i j", i=KP)
                then(V.tensor_tensor(c4, top[:, 0, :].rearrange("p (i a) -> p i a", a=1).broadcast_to([P, KP, KP]),
                                     top[:, 1:2, :].broadcast_to([P, KP, KP]), ALU.add))
                if u >= 1:
                    dve.wait_ge(gexp, u)
                then(V.max(out=best[:, 0:8], in_=cand))
                then(V.match_replace(out=cand2, in_to_replace=best[:, 0:8], in_values=cand, imm_value=TAKEN))
                then(V.max(out=best[:, 8:16], in_=cand2))
                then(V.tensor_scalar(negbest[:], best[:, 0:1], -1.0, None, ALU.mult), best_set)
                V.max_index(besti[:, 0:8], best[:, 0:8], cand)
                then(V.max_index(besti[:, 8:16], best[:, 8:16], cand2))

            def top16_ids(u):
                V.tensor_scalar(rank[:, 0, :], besti, 4, None, ALU.logical_shift_right)
                then(V.tensor_scalar(rank[:, 1, :], besti, 15, None, ALU.bitwise_and))
                then(V.tensor_copy(rankf, rank))
                for e in range(2):
                    ins = (V.tensor_tensor(hot[:, e, :, :], rankf[:, e, :].rearrange("p (k a) -> p k a", a=1).broadcast_to([P, KP, KP]),
                                         iota[:].rearrange("p (a r) -> p a r", a=1).broadcast_to([P, KP, KP]), ALU.is_equal))
                then(ins)
                for e in range(2):
                    ins = (V.tensor_tensor(hoti[:, e, :, :], hot[:, e, :, :], topf[:, e:e + 1, :].broadcast_to([P, KP, KP]), ALU.mult))
                then(ins)
                then(V.tensor_reduce(half_id, hoti, AX.X, ALU.add))
                dve.wait_ge(gexp, u + 1)
                then(V.reciprocal(rgsum[:], gsum[:, u % 2:u % 2 + 1]))
                then(V.tensor_scalar(gates[:, u * KP:(u + 1) * KP], ebest[:, u % 2, :], rgsum[:], None, ALU.mult))
                then(V.scalar_tensor_tensor(ids[:, u * KP:(u + 1) * KP], half_id[:, 0, :], float(NK), half_id[:, 1, :],
                                            ALU.mult, ALU.add), picked)

            def top16(u):
                top16_halves(u)
                top16_pairs(u)
                top16_ids(u)

            def picks(u):
                t = u // HP

                def scaled(n, s):
                    dve.wait_ge(gelued, n + 1)
                    V.tensor_scalar(diag[:, s, :], ident[:], zact[:, s:s + 1], gates[:, bass.ds(n, 1)],
                                    ALU.mult, ALU.mult).then_inc(diagd, 1)

                with dve.Fori(0, GROUPS) as i:
                    for s in range(G):
                        dve.wait_ge(landed[s], (i + (u * GROUPS + 1)) * 16)
                        V.tensor_tensor_reduce(row[s][:, 0:D], row[s][:, 0:D], h2[t % 2], 1.0, 0.0, ALU.mult, ALU.add,
                                               zdot[:, s:s + 1]).then_inc(dotted, 1)
                        if s > 0:
                            scaled(i * G + (u * KP + s - 1), s - 1)
                    scaled(i * G + (u * KP + G - 1), G - 1)

            add_mix(0, 6)
            dve.wait_ge(keys_in, 32)
            mean_square(TILES)
            normed(h2[0], TILES, 0, g2b[:], hready)
            att_max(PROMPT_ATT)
            att_max(PROMPT_ATT + 1)
            h2_take(0, 4)
            att_scale(PROMPT_ATT)
            for n in range(PROMPT_ATT, len(ATT)):
                att_step(n)
                if n == PROMPT_ATT + 1:
                    top16_halves(0)
                if n == PROMPT_ATT + 2:
                    top16_pairs(0)
                if n == PROMPT_ATT + 3:
                    top16_ids(0)
            top16(1)
            for u in range(UNITS):
                t, h = divmod(u, HP)
                picks(u)
                if h == HP - 1:
                    dve.wait_ge(acc, (u + 1) * KP)
                    then(V.tensor_copy(x[:, t, :], psf[:, 6 * 512:8 * 512]), y_read)
                if u in (1, 2):
                    add_mix(u, 0)
                if u + 2 < UNITS:
                    top16(u + 2)
                if u == 2:
                    mean_square(TILES + 1)
                    mean_square(TILES + 2)
                if h == HP - 5 and t + 1 < TILES:
                    normed(h2[(t + 1) % 2], TILES + t + 1, t + 1, g2b[:], hready)
                if h == 2 and t > 0:
                    dve.wait_ge(gf_in, 16)
                    normed(x[:, t - 1, :], 2 * TILES + t - 1, t - 1, gfb, y_out)
                if h == HP - 1:
                    mean_square(2 * TILES + t)
                if h == HP - 4 and t + 1 < TILES:
                    h2_take(t + 1, 0)
            normed(x[:, TILES - 1, :], 3 * TILES - 1, TILES - 1, gfb, y_out)


def kernel(x_prompt, x_sample, cache_attn_k, cache_attn_v, cache_idx_k, state_retention, ln1_g, w_in, w_out, ln2_g,
           peer_w_query, peer_keys1, peer_keys2, peer_u, peer_v, ln_final_g):
    import concourse.bacc as bacc
    from concourse.bass_utils import run_bass_kernel_spmd

    def chunked(w):
        return w.reshape(KC, P, -1).transpose(1, 0, 2).reshape(P, -1)

    w, wo, wq = (np.asarray(v)[0] for v in (w_in, w_out, peer_w_query))
    c_qa, c_kv, c_qi = 0, HA * DH, HA * DH + 2 * KVH * DH
    c_ki = c_qi + HI * DH
    c_qb = c_ki + DH + HI
    c_vb = c_qb + 2 * HB * DK
    c_gb = c_vb + HB * DV
    qcols = np.arange(HA * DH).reshape(KVH, GRP, DH).transpose(1, 0, 2).reshape(-1)
    rows_out = np.concatenate([qcols, np.arange(HA * DH, D)])
    arrays = {
        "x": np.concatenate([np.asarray(x_prompt).reshape(2, P, D), np.asarray(x_sample).reshape(1, P, D)]),
        "ln1_g": np.asarray(ln1_g)[0], "ln2_g": np.asarray(ln2_g)[0], "ln_final_g": np.asarray(ln_final_g),
        "w_kv": chunked(np.concatenate([w[:, c_kv:c_qi], w[:, c_ki:c_qb]], 1)),
        "w_qi": chunked(w[:, c_qi:c_ki]), "w_qa": chunked(w[:, qcols]),
        "w_qkb": chunked(w[:, c_qb:c_vb]), "w_vb": chunked(w[:, c_vb:c_gb]), "w_gb": chunked(w[:, c_gb:]),
        "keysT": np.stack([np.asarray(peer_keys1)[0].T, np.asarray(peer_keys2)[0].T], 1).reshape(P, -1),
        "cki": np.asarray(cache_idx_k)[0].transpose(0, 2, 1),
        "ckv": np.stack([np.asarray(cache_attn_k)[0].reshape(STREAMS, PAST, P).transpose(0, 2, 1),
                         np.asarray(cache_attn_v)[0].reshape(STREAMS, 4, P, P).transpose(0, 2, 1, 3).reshape(
                             STREAMS, P, PAST)], 1),
        "s0": np.asarray(state_retention)[0].reshape(4, 2, HB, DK, DV).transpose(1, 3, 0, 2, 4),
        "uv": np.concatenate([np.asarray(peer_u)[0], np.asarray(peer_v)[0]], 1),
    }
    for e in range(2):
        arrays[f"w_out{e}"] = chunked(wo[rows_out][:, e * 512:(e + 1) * 512])
    for j in range(4):
        arrays[f"w_q{j}"] = chunked(wq[:, j * 512:(j + 1) * 512])
    arrays.update(constants())
    arrays = {k: np.ascontiguousarray(v) for k, v in arrays.items()}

    nc = bacc.Bacc("TRN2", target_bir_lowering=False, num_devices=1)
    ins = {k: nc.dram_tensor(f"in_{k}", v.shape, mybir.dt.from_np(v.dtype), kind="ExternalInput").ap()
           for k, v in arrays.items()}
    shapes = {"y": (TILES, P, D), "k": (TILES, P, P), "v": (TILES, P, P), "ki": (TILES, P, DH),
              "state_p": (P, 2, DV), "state_s": (2, DK, 4, HB, DV)}
    outs = {k: nc.dram_tensor(f"out_{k}", s, F32, kind="ExternalOutput").ap() for k, s in shapes.items()}
    outs["kv"] = [[outs["k"][t], outs["v"][t], outs["ki"][t]] for t in range(TILES)]
    build(nc, ins, outs)
    r = run_bass_kernel_spmd(nc, [{f"in_{k}": v for k, v in arrays.items()}], core_ids=[0]).results[0]
    y, k, v, ki = (r["out_" + n] for n in ("y", "k", "v", "ki"))
    state_p = r["out_state_p"].reshape(2, DK, 2, DV).transpose(2, 0, 1, 3).reshape(1, 1, HB, DK, DV)
    state_s = r["out_state_s"].transpose(2, 0, 3, 1, 4).reshape(1, STREAMS, HB, DK, DV)
    return (y[:2].reshape(1, 2 * P, D), y[2].reshape(STREAMS, STEPS, D),
            k[:2].reshape(1, 1, 2 * P, KVH, DH), v[:2].reshape(1, 1, 2 * P, KVH, DH), ki[:2].reshape(1, 1, 2 * P, DH),
            np.ascontiguousarray(state_p),
            k[2].reshape(1, STREAMS, STEPS, KVH, DH), v[2].reshape(1, STREAMS, STEPS, KVH, DH),
            ki[2].reshape(1, STREAMS, STEPS, DH), np.ascontiguousarray(state_s))
```

```python
from contextlib import ExitStack

import numpy as np

import concourse.bass as bass
from concourse import mybir

F32 = mybir.dt.float32
BF16 = mybir.dt.bfloat16
U32 = mybir.dt.uint32
ALU = mybir.AluOpType
ACT = mybir.ActivationFunctionType
AX = mybir.AxisListType

P = 128
D = 1024
KC = D // P
TILES = 3
NTOK = TILES * P
STREAMS, STEPS, PAST = 8, 16, 512
HA, KVH, GRP, DH = 8, 2, 4, 64
HI = 8
HB, DK, DV = 4, 64, 128
CHUNK = 64
TOPK = (64, 64, 132)
KEYS = (128, 256, 640)
NKV = 2 * P + DH + HI
HP, KP, NK = 8, 16, 128
UNITS = TILES * HP
G = 8
GROUPS = KP // G
EPS = 1e-6
TAKEN = -3.39e38
BARRED = -3.0e38
OFF = -1.0e30
LG = [float(np.log(np.float32(1.0) - np.float32(2.0) ** np.float32(-5.0 - h))) for h in range(HB)]


def constants():
    t = np.arange(P)
    pos = np.stack([t, P + t, PAST + t % STEPS]).astype(np.float32)
    inv = (1.0 / (np.float32(10000.0) ** np.linspace(0.0, 1.0, DK // 2, dtype=np.float32))).astype(np.float32)
    ang = (pos[:, :, None] * inv).astype(np.float32)
    cs = np.stack([np.cos(ang), np.sin(ang)], 1)
    cs = np.stack([cs, cs * np.float32(DK ** -0.5)], 2)
    c = {"cs": cs.transpose(3, 0, 1, 2, 4).reshape(P, -1)}
    lg = np.array(LG)
    kd = np.exp((2 * P - 1 - (np.arange(2)[None, :, None] * P + t[:, None, None])) * lg)
    own = (t[:, None] // STEPS == np.arange(STREAMS)[None, :])
    kds = own[:, :, None] * np.exp((STEPS - 1 - t % STEPS)[:, None, None] * lg)
    c["kd"] = np.concatenate([kd.reshape(P, -1), kds.reshape(P, -1)], 1)
    diff = t[None, :] - t[:, None]
    near = np.where(diff[:, None, :] >= 0, np.exp(np.maximum(diff, 0)[:, None, :] * lg[None, :, None]), 0.0)
    far = np.exp((diff + P)[:, None, :] * lg[None, :, None])
    c["dmask"] = np.concatenate([near, far], 2).reshape(P, -1)
    same = (t[None, :] // STEPS == t[:, None] // STEPS)
    c["dmask_s"] = (near * same[:, None, :]).reshape(P, -1)
    half = (t // STEPS % 2)[None, :] == (t[:, None] // DK)
    c["qmask"] = (half[:, None, :] * np.exp((t % STEPS + 1)[None, None, :] * lg[None, :, None])).reshape(P, -1)
    causal = np.where(t[None, :] // CHUNK <= t[:, None] // CHUNK, 0.0, BARRED)
    c["bar"] = np.concatenate([causal, np.where(same, 0.0, BARRED)], 1)
    e8 = np.zeros((P, P))
    e8[DH:DH + HI] = (np.arange(HI)[:, None] == t[None, :] // STEPS)
    c["e8"] = e8
    c["m16"] = (t[:, None] % STEPS == np.arange(STEPS)[None, :])
    c["iota"] = np.broadcast_to(np.arange(KP), (P, KP))
    c["ident"] = np.eye(P)
    c["half"] = np.full((P, HB), -0.5)
    return {k: np.ascontiguousarray(v, dtype=np.float32) for k, v in c.items()}


def build(nc, a, o):
    with ExitStack() as ctx:
        def sb(name, shape, dt=F32):
            return ctx.enter_context(nc.sbuf_tensor(name, shape, dt))

        def sem(name):
            return ctx.enter_context(nc.semaphore(name))

        x = sb("x", [P, TILES, D])
        ident = sb("ident", [P, P])
        ident_bf = sb("ident_bf", [P, P], BF16)
        keysT = sb("keysT", [P, 2, NK])
        ids = sb("ids", [P, UNITS * KP], U32)
        gates = sb("gates", [P, UNITS * KP])
        cs = sb("cs", [P, TILES, 2, 2, DK // 2])
        kd = sb("kd", [P, 2 * HB + STREAMS * HB])
        g2b = sb("g2b", [P, D])
        dmask = sb("dmask", [P, HB, 2 * P])
        qmask = sb("qmask", [P, HB, P])
        e8 = sb("e8", [P, P])
        m16 = sb("m16", [P, STEPS])
        iota = sb("iota", [P, KP])
        neg_half = sb("neg_half", [P, HB])
        stage = sb("stage", [P, 2, G], U32)
        zdot = sb("zdot", [P, G])
        zact = sb("zact", [P, G])
        sumsq, ms, rstd = sb("sumsq", [P, 9]), sb("ms", [P, 9]), sb("rstd", [P, 9])
        bn6, mv = sb("bn6", [P, HB, 6]), sb("mv", [P, HB, 2])
        veps, rstd4 = sb("veps", [P, HB]), sb("rstd4", [P, HB])
        rowmax, negmax = sb("rowmax", [P, 2]), sb("negmax", [P, 2, 2])
        esum, resum = sb("esum", [P, 2, 2]), sb("resum", [P, 2])
        top8 = sb("top8", [P, 8])
        negbest, gsum, rgsum = sb("negbest", [P, 1]), sb("gsum", [P, 2]), sb("rgsum", [P, 1])
        rows = sb("rows", [P, G, 2 * D])
        wt = sb("wt", [P, 6, KC * 512])
        work = sb("work", [P, 4608])
        ps = ctx.enter_context(nc.psum_tensor("ps", [P, 8, 512], F32))
        psf = ps[:, :, :].rearrange("p b n -> p (b n)")

        rowf = rows[:, :, :].rearrange("p g n -> p (g n)")
        wtf = wt[:, :, :].rearrange("p s n -> p (s n)")
        SLOT = KC * 512

        def at(region, off, n):
            return region[:, off:off + n]

        hT = at(rowf, 0, KC * NTOK).rearrange("p (c t) -> p c t", c=KC)
        hnat = at(rowf, 3072, 2 * D).rearrange("p (b n) -> p b n", b=2)
        g1b = at(rowf, 5120, D)
        qaT = at(rowf, 6144, GRP * NTOK).rearrange("p (g t) -> p g t", g=GRP)
        qiT = at(rowf, 7680, HI * NTOK).rearrange("p (g h t) -> p g h t", h=HI, t=STEPS)
        kaT = at(rowf, 10752, NTOK)
        kiwT = at(rowf, 11136, NTOK)
        biasb = at(rowf, 11520, 512).bitcast(BF16)
        bias = (biasb[:, 0:128], biasb[:, 128:384], biasb[:, 384:1024])
        rT = at(rowf, 12288, 1024).rearrange("p (t s n) -> p t s n", t=2, s=4)
        qTd = at(rowf, 13312, 512).rearrange("p (h t) -> p h t", h=HB)
        kTs = at(rowf, 13824, 256).rearrange("p (s t) -> p s t", s=2)
        am0 = at(rowf, 14080, 1024).rearrange("p (h i) -> p h i", h=HB)
        kvnat = at(rowf, 15360, TILES * NKV).rearrange("p (t n) -> p t n", t=TILES)
        vb = at(rowf, 7680, TILES * 512).rearrange("p (t n) -> p t n", t=TILES)
        gs = at(rowf, 9216, TILES * 512).rearrange("p (t n) -> p t n", t=TILES)
        qz = at(rowf, 0, HB * 640).rearrange("p (h n) -> p h n", h=HB)
        qzb = at(rowf, 2560, D).rearrange("p (b k g t) -> p b k g t", b=STREAMS, k=KVH, g=GRP)
        kdn = at(rowf, 3584, 512).rearrange("p (t h d) -> p t h d", t=2, h=HB)
        mixnat = at(rowf, 4096, TILES * 512).rearrange("p (t n) -> p t n", t=TILES)
        rotq2 = at(rowf, 5632, 512).rearrange("p (h b e d) -> p h b e d", h=HB, b=2, e=2)
        WZ = 8 * 144
        wz = at(wtf, 0, TILES * WZ).rearrange("p (t n) -> p t n", t=TILES)
        relu = at(wtf, 3456, 2 * 640).rearrange("p (b n) -> p b n", b=2)
        score = at(wtf, 4736, 640)
        cki = at(wtf, 5376, 2 * PAST).rearrange("p (b n) -> p b n", b=2)
        bar = at(wtf, 6400, 2 * P)
        prob_p = relu
        probT_p = at(wtf, 6656, 1024).rearrange("p (b n) -> p b n", b=2)
        mixT = at(wtf, 2 * SLOT, KC * NTOK).rearrange("p (c t) -> p c t", c=KC)
        am1 = at(wtf, 2 * SLOT + 3072, 512).rearrange("p (h i) -> p h i", h=HB)
        am2 = at(wtf, 2 * SLOT + 3584, 512).rearrange("p (h i) -> p h i", h=HB)
        prod = at(wtf, 3 * SLOT, 1024).rearrange("p (e i q h d) -> p e i q h d", e=2, i=2, q=2, h=HB)
        s0 = at(wtf, 3 * SLOT, 2048).rearrange("p (q h v) -> p q h v", q=4, h=HB)
        prob = at(wtf, 3 * SLOT + 2048, 1280).rearrange("p (b n) -> p b n", b=2)
        selb = at(wtf, 3 * SLOT + 3328, 512).bitcast(BF16).rearrange("p (b k t) -> p b k t", b=STREAMS, k=8)
        snp = at(wtf, 3 * SLOT + 3840, 256).rearrange("p (q v) -> p q v", q=2)
        probT = at(wtf, 4 * SLOT + 2048, 1280).rearrange("p (b n) -> p b n", b=2)
        dmask_s = at(wtf, 3 * SLOT + 2048, 512)
        kz = at(wtf, 4 * SLOT + 2048, 2048).rearrange("p (q h e d) -> p q h e d", q=4, h=HB, e=2)
        ckv = [at(wtf, 4 * SLOT + b % 7 * 1024, 1024) if b in (0, 1, 7) else
               at(rowf, 12288 + (b - 2) * 1024, 1024) if b < 5 else at(rowf, (b - 5) * 1024, 1024)
               for b in range(STREAMS)]
        PLACE = (2, 3, 4, 6, 5, 1, 0, 7)
        row = [rows[:, place, :] for place in PLACE]
        diag = dmask[:, :, :].rearrange("p h (i n) -> p (h i) n", n=P)
        gfb = at(wtf, 2048, D)
        sq = at(wtf, 3072, D)
        rot = at(work, 3072, TILES * 512).rearrange("p (t h e d) -> p t h e d", t=TILES, h=2 * HB, e=2)
        h2 = (at(work, 0, D), at(wtf, 1024, D))
        h2T = at(work, 1024, D).rearrange("p (c t) -> p c t", c=KC)
        qT = at(work, 2048, 512).rearrange("p (b e t) -> p b e t", b=2, e=2)
        rest = (at(work, 2560, P), at(work, 4480, P))
        cand = at(work, 2688, 256)
        cand2 = at(work, 2944, 256)
        hot = at(work, 3200, 512).rearrange("p (e k r) -> p e k r", e=2, k=KP)
        hoti = at(work, 3712, 512).rearrange("p (e k r) -> p e k r", e=2, k=KP)
        top = at(work, 4224, 32).rearrange("p (e k) -> p e k", e=2)
        topi = at(work, 4256, 32).bitcast(U32).rearrange("p (e k) -> p e k", e=2)
        topf = at(work, 4288, 32).rearrange("p (e k) -> p e k", e=2)
        best = at(work, 4320, KP)
        besti = at(work, 4336, KP).bitcast(U32)
        rank = at(work, 4352, 32).bitcast(U32).rearrange("p (e k) -> p e k", e=2)
        rankf = at(work, 4384, 32).rearrange("p (e k) -> p e k", e=2)
        half_id = at(work, 4416, 32).rearrange("p (e k) -> p e k", e=2)
        ebest = at(work, 4448, 2 * KP).rearrange("p (b k) -> p b k", b=2)
        NAMES = ["kv", "qi", "qa", "vb", "gb", "qkb", "out0", "out1", "q0", "q1", "q2", "q3"]
        w_in = {n: sem("w_" + n) for n in NAMES}
        x_in = [sem(f"x_in{t}") for t in range(TILES)]
        g1_in, ident_in, small_in, bar_in, keys_in = (sem(n) for n in ("g1_in", "ident_in", "small_in", "bar_in", "keys_in"))
        gf_in, s0_in, dms_in = sem("gf_in"), sem("s0_in"), sem("dms_in")
        cki_in = [sem(f"cki_in{i}") for i in range(2)]
        ckv_in = [sem(f"ckv_in{i}") for i in range(STREAMS)]
        out_done = sem("out_done")
        sqd, msd, rsd, hready, x1_done = (sem(n) for n in ("squares", "mean_square", "rstd", "h_ready", "x1_done"))
        ht_ps, ht_act, ht_dve = sem("ht_ps"), sem("ht_act"), sem("ht_dve")
        proj, proj_act, proj_dve = sem("proj"), sem("proj_act"), sem("proj_dve")
        kt_ps, kt_sb = sem("kt_ps"), sem("kt_sb")
        w_ps, wz_zero, wz_set = sem("w_ps"), sem("wz_zero"), sem("wz_set")
        dots, relued, combined, scored, biased = (sem(n) for n in ("dots", "relued", "combined", "scored", "biased"))
        rt_ps, rt_sb, s_ps, s_masked = sem("rt_ps"), sem("rt_sb"), sem("s_ps"), sem("s_masked")
        zeroed, kdec, qz_set, qzb_set, sel_set = (sem(n) for n in ("zeroed", "kdec", "qz_set", "qzb_set", "sel_set"))
        o_ps, o_norm, o_var, o_rstd, sp_ps, sp_sb, ss_ps, ss_sb = (sem(n) for n in (
            "o_ps", "o_norm", "o_var", "o_rstd", "sp_ps", "sp_sb", "ss_ps", "ss_sb"))
        mt_ps, mt_sb, q_twice = sem("mt_ps"), sem("mt_sb"), sem("q_twice")
        sc_ps, smax, expd, pscaled, pt_ps, pt_sb, pv_ps, pv_sb = (sem(n) for n in (
            "sc_ps", "smax", "expd", "pscaled", "pt_ps", "pt_sb", "pv_ps", "pv_sb"))
        wout, h2t_ps, h2t_act, h2t_dve = sem("wout"), sem("h2t_ps"), sem("h2t_act"), sem("h2t_dve")
        q_ps, q_sb, sc2_ps, topped, best_set, gexp, picked = (sem(n) for n in (
            "q_ps", "q_sb", "sc2_ps", "topped", "best_set", "gexp", "picked"))
        staged, seen, dotted, gelued, diagd, acc, y_init, y_read, y_out = (sem(n) for n in (
            "staged", "seen", "dotted", "gelued", "diagd", "acc", "y_init", "y_read", "y_out"))
        landed = [sem(f"landed{s}") for s in range(G)]
        chain = sem("dve_chain")

        slot_of = {"kv": 0, "qi": 1, "qa": 2, "vb": 3, "gb": 4, "qkb": 5, "out0": 0, "out1": 1,
                   "q0": 5, "q1": 3, "q2": 4, "q3": 2}
        width = {"kv": NKV}

        def wv(name):
            w = width.get(name, 512)
            return wt[:, slot_of[name], 0:KC * w].rearrange("p (c n) -> p c n", c=KC)

        def load_w(eng, name):
            w = width.get(name, 512)
            eng.dma_start(wt[:, slot_of[name], 0:KC * w], a["w_" + name]).then_inc(w_in[name], 16)

        def load_ckv(eng, b):
            for k in range(2):
                eng.dma_start(ckv[b][:, k * PAST:(k + 1) * PAST], a["ckv"][b][k]).then_inc(ckv_in[b], 16)

        UN = ([("kv", "n", t) for t in range(TILES)] + [("qi", "t", j) for j in range(4)]
              + [("qa", "t", g) for g in range(GRP)] + [("vb", "n", t) for t in range(TILES)]
              + [("qkb", "n", t) for t in range(TILES)] + [("gb", "n", t) for t in range(TILES)])
        QKB = 14

        def taken(n):
            if QKB <= n < QKB + TILES:
                return proj_dve, n - QKB + 1
            return proj_act, n + 1 - (TILES if n > QKB else 0)

        PROMPT_ATT = 2 * GRP
        ATT = [(t, g) for t in range(2) for g in range(GRP)] + [(2, b) for b in range(STREAMS)]

        def q_psum(u):
            return ps[:, 2 + u % 2, 0:256] if u else ps[:, 7, 0:256]

        def sc_psum(u):
            return ps[:, 4 + u % 2, 0:256] if u else ps[:, 7, 256:512]

        LATER_OUT = {0: ((1, 0),), 1: ((1, 1),), 2: ((2, 0), (2, 1))}
        PROMPT_AFTER = {11: (0,), 12: (1,), 13: (2,), 14: (3, 4), 15: (5, 6), 16: (7,)}

        block = ctx.enter_context(nc.Block())

        @block.sync
        def _(sp):
            sp.dma_start(x[:, 0, :], a["x"][0]).then_inc(x_in[0], 16)
            sp.dma_start(g1b, a["ln1_g"].partition_broadcast(P)).then_inc(g1_in, 16)
            sp.dma_start(ident[:], a["ident"]).then_inc(ident_in, 16)
            sp.dma_start(neg_half[:], a["half"]).then_inc(ident_in, 16)
            load_w(sp, "kv")
            for t in (1, 2):
                sp.dma_start(x[:, t, :], a["x"][t]).then_inc(x_in[t], 16)
            load_w(sp, "qi")
            for name, dst in (("e8", e8[:]), ("m16", m16[:]), ("iota", iota[:]), ("kd", kd[:]),
                              ("cs", cs[:, :, :, :, :].rearrange("p a b c d -> p (a b c d)")),
                              ("dmask", dmask[:, :, :].rearrange("p a b -> p (a b)")),
                              ("qmask", qmask[:, :, :].rearrange("p a b -> p (a b)"))):
                sp.dma_start(dst, a[name]).then_inc(small_in, 16)
            for name in ("qa", "vb", "qkb", "gb"):
                load_w(sp, name)
            sp.dma_start(keysT[:, :, :].rearrange("p a b -> p (a b)"), a["keysT"]).then_inc(keys_in, 16)
            sp.dma_start(g2b[:], a["ln2_g"].partition_broadcast(P)).then_inc(keys_in, 16)
            sp.wait_ge(proj, 7)
            sp.dma_start(bar, a["bar"]).then_inc(bar_in, 16)
            sp.wait_ge(proj, 14)
            sp.dma_start(dmask_s, a["dmask_s"]).then_inc(dms_in, 16)
            sp.wait_ge(proj, 17)
            load_w(sp, "q0")
            sp.wait_ge(proj_dve, TILES)
            for e in range(2):
                sp.dma_start(s0[64 * e:64 * e + 64, :, :, :], a["s0"][e]).then_inc(s0_in, 16)
            sp.wait_ge(biased, 3)
            sp.wait_ge(pv_ps, PROMPT_ATT)
            load_w(sp, "out0")
            load_w(sp, "out1")
            sp.wait_ge(proj_act, 3)
            for t in range(TILES):
                for k, (c0, c1) in enumerate(((0, P), (P, 2 * P), (2 * P, 2 * P + DH))):
                    sp.dma_start(o["kv"][t][k], kvnat[:, t, c0:c1]).then_inc(out_done, 16)
            sp.wait_ge(sp_sb, 2)
            sp.dma_start(o["state_p"], snp).then_inc(out_done, 16)
            sp.wait_ge(ss_sb, HB)
            for e in range(2):
                sp.dma_start(o["state_s"][e], s0[64 * e:64 * e + 64, :, :, :]).then_inc(out_done, 16)
            sp.wait_ge(out_done, 16 * 12)
            sp.wait_ge(pv_ps, PROMPT_ATT + 1)
            load_ckv(sp, STREAMS - 1)
            sp.wait_ge(pv_sb, 2 * len(ATT))
            load_w(sp, "q1")
            load_w(sp, "q2")
            sp.wait_ge(wout, 2 * TILES)
            load_w(sp, "q3")
            sp.dma_start(gfb, a["ln_final_g"].partition_broadcast(P)).then_inc(gf_in, 16)
            for t in range(TILES):
                sp.wait_ge(y_out, t + 1)
                sp.dma_start(o["y"][t], x[:, t, :]).then_inc(out_done, 16)
            sp.wait_ge(out_done, 16 * 15)

        @block.gpsimd
        def _(pool):
            def take_rstd(n):
                pool.wait_ge(msd, n + 1)
                pool.tensor_tensor(rstd[:, n:n + 1], ms[:, n:n + 1], neg_half[:, 0:1], ALU.pow).then_inc(rsd, 1)

            pool.wait_ge(ident_in, 32)
            for n in range(TILES):
                take_rstd(n)
            pool.wait_ge(proj, 3)
            pool.memset(at(wtf, 0, TILES * WZ), 0.0).then_inc(wz_zero, 1)
            pool.wait_ge(proj, 7)
            for b in range(STREAMS):
                if b >= 2:
                    pool.wait_ge(dots, 16 + b - 1)
                pool.dma_start(cki[0:DH, b % 2, :], a["cki"][b]).then_inc(cki_in[b % 2], 16)

            def group_rstd(t):
                pool.wait_ge(o_var, t + 1)
                pool.tensor_tensor(rstd4[:], veps[:], neg_half[:], ALU.pow).then_inc(o_rstd, 1)

            group_rstd(0)
            pool.wait_ge(proj, len(UN))
            pool.memset(at(rowf, 0, 3584), 0.0).then_inc(zeroed, 1)
            for b in range(2):
                load_ckv(pool, b)
            take_rstd(TILES)
            group_rstd(1)
            group_rstd(2)
            pool.wait_ge(o_ps, TILES)
            for b in range(2, STREAMS - 1):
                load_ckv(pool, b)

            def gathers(par, g, unit, first=False):
                pool.wait_ge(picked, unit + 1)
                if not first:
                    pool.sem_inc(seen)
                pool.tensor_copy(stage[:, par, :], ids[:, bass.ds(g * G, G)]).then_inc(staged, 1)
                for s in range(G):
                    if s == 0:
                        pool.wait_ge(staged, g + 1)
                        if first:
                            pool.wait_ge(mt_ps, TILES)
                            pool.wait_ge(qzb_set, 2)
                    if s == 3 and first:
                        pool.wait_ge(pv_ps, PROMPT_ATT + 4)
                    if s == 4 and first:
                        pool.wait_ge(sc_ps, len(ATT))
                    if s == 6 and first:
                        pool.wait_ge(pv_ps, PROMPT_ATT + 7)
                    if s == 7 and first:
                        pool.wait_ge(pv_ps, len(ATT))
                        pool.wait_ge(out_done, 16 * 12)
                    if not first:
                        pool.wait_ge(acc, (g - 1) * G + s + 1)
                    pool.sem_inc(seen)
                    pool.indirect_dma_start(row[s], None, a["uv"], bass.IndirectOffsetOnAxis(
                        ap=stage[:, par, s:s + 1], axis=0)).then_inc(landed[s], 16)

            def span(g0, g1):
                pairs = (g1 - g0) // 2
                with pool.Fori(0, pairs) as i:
                    gathers(1, i * 2 + g0, i + (g0 - 1) // 2)
                    gathers(0, i * 2 + (g0 + 1), i + (g0 + 1) // 2)
                if (g1 - g0) % 2:
                    gathers(1, g1 - 1, (g1 - 1) // 2)

            per_tile = HP * GROUPS
            gathers(0, 0, 0, first=True)
            span(1, 9)
            take_rstd(TILES + 1)
            take_rstd(TILES + 2)
            span(9, per_tile + 5)
            take_rstd(2 * TILES)
            span(per_tile + 5, 2 * per_tile + 5)
            take_rstd(2 * TILES + 1)
            span(2 * per_tile + 5, 3 * per_tile)
            take_rstd(2 * TILES + 2)

        @block.tensor
        def _(pe):
            def mm(out, lhsT, rhs, start=True, stop=True):
                return nc.tensor.matmul(out, lhsT, rhs, start=start, stop=stop)

            def tr(out, in_, k=P):
                return nc.tensor.transpose(out, in_, ident[0:k, 0:k])

            pe.wait_ge(ident_in, 32)

            def norm_t(t):
                pe.wait_ge(hready, t + 1)
                if t == 2:
                    pe.wait_ge(ht_act, 1)
                    pe.wait_ge(ht_dve, 1)
                for c in range(KC):
                    last = tr(ps[:, 2 * (t % 2) + c // 4, (c % 4) * P:(c % 4 + 1) * P], hnat[:, t % 2, c * P:(c + 1) * P])
                last.then_inc(ht_ps, 1)

            def unit(n):
                name, kind, i = UN[n]
                if i == 0:
                    pe.wait_ge(w_in[name], 16)
                if name == "kv":
                    pe.wait_ge(ht_act, i + 1)
                    pe.wait_ge(ht_dve, i + 1)
                if n >= 2:
                    pe.wait_ge(*taken(n - 2))
                w, bank = wv(name), 6 + n % 2
                for c in range(KC):
                    if kind == "n":
                        last = mm(ps[:, bank, 0:width.get(name, 512)], hT[:, c, i * P:(i + 1) * P], w[:, c, :],
                                  c == 0, c == KC - 1)
                    else:
                        last = mm(ps[:, bank, 0:NTOK], w[:, c, i * P:(i + 1) * P], hT[:, c, :], c == 0, c == KC - 1)
                last.then_inc(proj, 1)

            for n in range(TILES):
                norm_t(n)
                unit(n)
            pe.wait_ge(proj_act, 3)
            for t in range(TILES):
                tr(ps[:, 0, t * P:(t + 1) * P], kvnat[:, t, 0:P])
                last = tr(ps[0:DH + HI, 1, t * P:(t + 1) * P], kvnat[:, t, 2 * P:NKV])
            last.then_inc(kt_ps, 1)
            for n in range(3, 7):
                unit(n)
            pe.wait_ge(kt_sb, 2)
            pe.wait_ge(small_in, 16 * 7)
            mm(ps[:, 2, 0:NTOK], e8[DH:DH + HI, :], kiwT[DH:DH + HI, :]).then_inc(w_ps, 1)

            def index_dots(m):
                t, g = divmod(m, 8)
                if m == 0:
                    pe.wait_ge(proj_act, 7)
                if m == 1:
                    pe.wait_ge(wz_set, TILES)
                if m >= 2:
                    pe.wait_ge(relued, m - 1)
                lhs = qiT[0:DH, m, :, :]
                b = 2 * (m % 2)
                if t < 2:
                    last = mm(ps[:, b, 0:KEYS[t]], lhs, kiwT[0:DH, 0:KEYS[t]])
                else:
                    pe.wait_ge(cki_in[g % 2], 16 * (g // 2 + 1))
                    mm(ps[:, b, :], lhs, cki[0:DH, g % 2, :])
                    last = mm(ps[:, b + 1, 0:P], lhs, kiwT[0:DH, 2 * P:3 * P])
                last.then_inc(dots, 1)

            def index_sum(m):
                t, g = divmod(m, 8)
                if m == 0:
                    pe.wait_ge(wz_set, TILES)
                if g == 0 and t > 0:
                    pe.wait_ge(scored, t)
                pe.wait_ge(relued, m + 1)
                lhs = wz[:, t, g * P:(g + 1) * P]
                if t < 2:
                    last = mm(ps[:, 4, 0:KEYS[t]], lhs, relu[:, m % 2, 0:KEYS[t]], g == 0, g == 7)
                else:
                    mm(ps[:, 4, :], lhs, relu[:, m % 2, 0:512], g == 0, g == 7)
                    last = mm(ps[:, 5, 0:P], lhs, relu[:, m % 2, 512:640], g == 0, g == 7)
                last.then_inc(combined, 1)

            for m in range(25):
                if m < 24:
                    index_dots(m)
                if m >= 1:
                    index_sum(m - 1)
            def att_scores(n):
                t, i = ATT[n]
                b = 2 * (n % 2)
                if n == 0:
                    pe.wait_ge(relued, 24)
                if n == PROMPT_ATT:
                    pe.wait_ge(mt_sb, TILES)
                    pe.wait_ge(sp_sb, 2)
                    pe.wait_ge(sel_set, 1)
                    pe.wait_ge(qzb_set, 2)
                if t < 2:
                    pe.wait_ge(proj_act, 7 + i + 1)
                if i == 0:
                    pe.wait_ge(biased, t + 1)
                if n % PROMPT_ATT >= 2:
                    pe.wait_ge(expd, n - 1)
                if t < 2:
                    for k in range(KVH):
                        r = slice(64 * k, 64 * k + 64)
                        out = ps[:, b + k, 0:KEYS[t]]
                        mm(out, qaT[r, i, t * P:(t + 1) * P], kaT[r, 0:KEYS[t]], True, False)
                        last = mm(out, ident_bf[:], bias[t], False, True)
                else:
                    pe.wait_ge(ckv_in[i], 32)
                    lhs = qzb[:, i, :, :, :]
                    mm(ps[:, b, :], lhs, ckv[i][:, 0:PAST], True, False)
                    mm(ps[:, b, :], selb[:, i, :, :], bias[2][:, 0:512], False, True)
                    mm(ps[:, b + 1, 0:P], lhs, kaT[:, 2 * P:3 * P], True, False)
                    last = mm(ps[:, b + 1, 0:P], selb[:, i, :, :], bias[2][:, 512:640], False, True)
                last.then_inc(sc_ps, 1)

            def att_out(n):
                t, i = ATT[n]
                pe.wait_ge(pscaled, n + 1)
                if n == 0:
                    pe.wait_ge(scored, 3)
                if n >= 1:
                    pe.wait_ge(pt_sb, n)
                if t < 2:
                    for c in range(t + 1):
                        for k in range(KVH):
                            last = tr(ps[:, 4, c * 256 + k * P:c * 256 + (k + 1) * P],
                                      prob_p[:, n % 2, k * 256 + c * P:k * 256 + (c + 1) * P])
                else:
                    for c in range(5):
                        last = tr(psf[:, 4 * 512 + c * P:4 * 512 + (c + 1) * P], prob[:, n % 2, c * P:(c + 1) * P])
                last.then_inc(pt_ps, 1)
                if n % PROMPT_ATT + 2 < PROMPT_ATT:
                    att_scores(n + 2)
                pe.wait_ge(pt_sb, n + 1)
                if n >= 1:
                    pe.wait_ge(pv_sb, 2 * n)
                if t < 2:
                    for c in range(t + 1):
                        last = mm(ps[:, 5, 0:256], kvnat[:, c, P:2 * P], probT_p[:, n % 2, c * 256:(c + 1) * 256], c == 0, c == t)
                else:
                    for c in range(5):
                        lhs = ckv[i][:, PAST + c * P:PAST + (c + 1) * P] if c < 4 else kvnat[:, 2, P:2 * P]
                        last = mm(ps[:, 6, 0:P], lhs, probT[:, n % 2, c * P:(c + 1) * P], c == 0, c == 4)
                last.then_inc(pv_ps, 1)

            for n in range(7, QKB + TILES):
                unit(n)
                if n in (9, 10):
                    att_scores(n - 9)
                for m in PROMPT_AFTER.get(n, ()):
                    att_out(m)

            pe.wait_ge(expd, PROMPT_ATT)
            for t in range(2):
                pe.wait_ge(proj_dve, t + 1)
                for s in range(4):
                    last = tr(ps[:, t, s * P:(s + 1) * P], rot[:, t, 2 * s:2 * s + 2, :, :])
                last.then_inc(rt_ps, 1)
            unit(QKB + TILES)
            pe.wait_ge(q_twice, 2)
            for h in range(HB):
                last = tr(ps[:, 2, h * P:(h + 1) * P], rotq2[:, h, :, :, :])
            last.then_inc(rt_ps, 1)
            for s in range(2):
                last = tr(ps[:, 3, s * P:(s + 1) * P], rot[:, 2, HB + 2 * s:HB + 2 * s + 2, :, :])
            last.then_inc(rt_ps, 1)
            pe.wait_ge(rt_sb, 2)
            pe.wait_ge(pt_sb, PROMPT_ATT)
            pe.wait_ge(pv_sb, 2 * PROMPT_ATT)
            for h in range(HB):
                r = slice(64 * (h % 2), 64 * (h % 2) + 64)
                last = mm(ps[:, 4 + h % 2, (h // 2) * 256:(h // 2) * 256 + 256],
                          rT[r, 0, 2 + h // 2, :], rT[r, :, h // 2, :])
            last.then_inc(s_ps, 1)
            unit(QKB + TILES + 1)
            pe.wait_ge(rt_sb, 4)
            pe.wait_ge(s_masked, 2)
            for h in range(HB):
                r = slice(64 * (h % 2), 64 * (h % 2) + 64)
                mm(ps[:, 4 + h % 2, (h // 2) * P:(h // 2 + 1) * P], rT[r, 1, 2 + h // 2, :], rT[r, 1, h // 2, :])
                last = mm(ps[:, 4 + h % 2, (2 + h // 2) * P:(3 + h // 2) * P], kTs[r, h // 2, :], qTd[r, h, :])
            last.then_inc(s_ps, 1)
            for h in range(HB):
                last = mm(ps[:, 0, h * P:(h + 1) * P], am0[:, h, 0:P], vb[:, 0, h * P:(h + 1) * P])
            last.then_inc(o_ps, 1)
            unit(QKB + TILES + 2)

            def retained_1():
                pe.wait_ge(s_masked, 3)
                for h in range(HB):
                    mm(ps[:, 1, h * P:(h + 1) * P], am0[:, h, P:2 * P], vb[:, 0, h * P:(h + 1) * P], True, False)
                    last = mm(ps[:, 1, h * P:(h + 1) * P], am1[:, h, :], vb[:, 1, h * P:(h + 1) * P], False, True)
                last.then_inc(o_ps, 1)

            def states_s():
                pe.wait_ge(kdec, 4)
                pe.wait_ge(s_masked, 4)
                pe.wait_ge(*taken(len(UN) - 1))
                for q in range(4):
                    for h in range(HB):
                        last = mm(ps[:, 4 + q, h * P:(h + 1) * P], kz[:, q, h, :, :], vb[:, 2, h * P:(h + 1) * P])
                last.then_inc(ss_ps, 1)

            def retained_2():
                pe.wait_ge(x1_done, 2)
                pe.wait_ge(qz_set, HB)
                pe.wait_ge(s0_in, 32)
                for h in range(HB):
                    mm(ps[:, 2, h * P:(h + 1) * P], am2[:, h, :], vb[:, 2, h * P:(h + 1) * P], True, False)
                    for q in range(4):
                        last = mm(ps[:, 2, h * P:(h + 1) * P], qz[:, h, q * P:(q + 1) * P], s0[:, q, h, :], False, q == 3)
                last.then_inc(o_ps, 1)

            def state_p():
                for q in range(2):
                    for t in range(2):
                        last = mm(ps[:, 3, q * 256:(q + 1) * 256], kdn[:, t, 2 * q:2 * q + 2, :],
                                  vb[:, t, q * 256:(q + 1) * 256], t == 0, t == 1)
                last.then_inc(sp_ps, 1)

            def mix_t(t):
                pe.wait_ge(o_norm, t + 1)
                for c in range(4):
                    last = tr(ps[:, t, c * P:(c + 1) * P], mixnat[:, t, c * P:(c + 1) * P])
                last.then_inc(mt_ps, 1)

            def out_proj(t, bank, e):
                if t == 0 and e == 0:
                    pe.wait_ge(w_in["out0"], 16)
                    pe.wait_ge(w_in["out1"], 16)
                    pe.wait_ge(mt_sb, 1)
                if t == 2:
                    pe.wait_ge(x1_done, 2 + e + 1)
                w = wv(f"out{e}")
                for c in range(KC):
                    last = mm(ps[:, bank + e, :], mixT[:, c, t * P:(t + 1) * P], w[:, c, :], c == 0, c == KC - 1)
                last.then_inc(wout, 1)

            def h2_t(t):
                pe.wait_ge(hready, TILES + t + 1)
                if t == 0:
                    pe.wait_ge(o_norm, 2)
                else:
                    pe.wait_ge(x1_done, 2 * TILES)
                    pe.wait_ge(h2t_act, t)
                    pe.wait_ge(h2t_dve, t)
                for c in range(KC):
                    last = tr(ps[:, c // 4, (c % 4) * P:(c % 4 + 1) * P], h2[t % 2][:, c * P:(c + 1) * P])
                last.then_inc(h2t_ps, 1)

            def query(u):
                t, h = divmod(u, HP)
                if h == 0:
                    pe.wait_ge(h2t_act, t + 1)
                    pe.wait_ge(h2t_dve, t + 1)
                if t == 0 and h % 2 == 0:
                    pe.wait_ge(w_in[f"q{h // 2}"], 16)
                w = wv(f"q{h // 2}")
                for e in range(2):
                    col = (h % 2) * 256 + e * P
                    for c in range(KC):
                        last = mm(q_psum(u)[:, e * P:(e + 1) * P], w[:, c, col:col + P], h2T[:, c, :], c == 0, c == KC - 1)
                last.then_inc(q_ps, 1)

            def query_scores(u):
                if u >= 2:
                    pe.wait_ge(topped, u - 1)
                pe.wait_ge(q_sb, u + 1)
                for e in range(2):
                    last = mm(sc_psum(u)[:, e * P:(e + 1) * P], qT[:, u % 2, e, :], keysT[:, e, :])
                last.then_inc(sc2_ps, 1)

            def y_start(t):
                if t > 0:
                    pe.wait_ge(y_read, t)
                else:
                    pe.wait_ge(topped, 1)
                pe.wait_ge(x1_done, 2 * t + 2)
                for e in range(2):
                    last = mm(ps[:, 6 + e, :], ident[:], x[:, t, e * 512:(e + 1) * 512], True, False)
                last.then_inc(y_init, 1)

            def add_expert(n, s, stop=False):
                pe.wait_ge(diagd, n + 1)
                for e in range(2):
                    last = mm(ps[:, 6 + e, :], diag[:, s, :], row[s][:, D + e * 512:D + (e + 1) * 512], False, stop)
                last.then_inc(acc, 1)
                return last

            def picks(u):
                final = u % HP == HP - 1
                if u == 0:
                    for s in range(G):
                        add_expert(s, s)
                    for early in (1, 2):
                        query(early)
                        query_scores(early)
                    for s in range(G):
                        add_expert(G + s, s)
                elif final:
                    for s in range(G):
                        add_expert(u * KP + s, s)
                    for s in range(G):
                        add_expert(u * KP + G + s, s, s == G - 1)
                else:
                    with pe.Fori(0, GROUPS) as i:
                        for s in range(G):
                            add_expert(i * G + (u * KP + s), s)

            mix_t(0)
            out_proj(0, 2, 0)
            out_proj(0, 2, 1)
            retained_1()
            retained_2()
            states_s()
            state_p()
            h2_t(0)
            pe.wait_ge(keys_in, 32)
            pe.wait_ge(ss_sb, HB)
            query(0)
            query_scores(0)
            mix_t(1)
            mix_t(2)
            att_scores(PROMPT_ATT)
            att_scores(PROMPT_ATT + 1)
            for n in range(PROMPT_ATT, len(ATT)):
                att_out(n)
            pe.wait_ge(expd, len(ATT))
            pe.wait_ge(pv_sb, 2 * len(ATT))
            for u in range(UNITS):
                t, h = divmod(u, HP)
                if h == 0:
                    y_start(t)
                picks(u)
                if u + 3 < UNITS:
                    query(u + 3)
                    query_scores(u + 3)
                for tile, e in LATER_OUT.get(u, ()):
                    out_proj(tile, 0, e)
                if h == HP - 4 and t + 1 < TILES:
                    h2_t(t + 1)

        @block.scalar
        def _(act):
            def A(*args, **kw):
                return nc.scalar.activation(*args, **kw)

            def copy(out, in_):
                return A(out, in_, ACT.Copy)

            def take_hT(t):
                act.wait_ge(ht_ps, t + 1)
                copy(hT[:, 0:4, t * P:(t + 1) * P], ps[:, 2 * (t % 2), :].rearrange("p (c t) -> p c t", c=4)).then_inc(ht_act, 1)

            for t in range(TILES):
                act.wait_ge(x_in[t], 16)
                A(hnat[:, t % 2, :], x[:, t, :], ACT.Square, accum_out=sumsq[:, t:t + 1]).then_inc(sqd, 1)
                take_hT(t)

            def take(n):
                name, kind, i = UN[n]
                act.wait_ge(proj, n + 1)
                src = ps[:, 6 + n % 2, :]
                if name == "kv":
                    copy(kvnat[:, i, :], src[:, 0:NKV]).then_inc(proj_act, 1)
                elif name == "qi":
                    for e in range(2):
                        ins = copy(qiT[0:64, :, 2 * i + e, :],
                                   src[64 * e:64 * e + 64, 0:NTOK].rearrange("p (g t) -> p g t", t=STEPS))
                    ins.then_inc(proj_act, 1)
                elif name == "qa":
                    copy(qaT[:, i, :], src[:, 0:NTOK]).then_inc(proj_act, 1)
                elif name == "vb":
                    copy(vb[:, i, :], src).then_inc(proj_act, 1)
                else:
                    A(gs[:, i, :], src, ACT.Silu).then_inc(proj_act, 1)

            for n in range(7):
                take(n)
            for m in range(24):
                t, g = divmod(m, 8)
                act.wait_ge(dots, m + 1)
                if m >= 2:
                    act.wait_ge(combined, m - 1)
                k = KEYS[t]
                A(relu[:, m % 2, 0:k], psf[:, 1024 * (m % 2):1024 * (m % 2) + k], ACT.Relu).then_inc(relued, 1)
            def att_exp(n):
                t, i = ATT[n]
                act.wait_ge(smax, n + 1)
                if n == 0:
                    act.wait_ge(combined, 24)
                if n >= 2:
                    act.wait_ge(pt_ps, n - 1)
                c = n % 2
                if t < 2:
                    for k in range(KVH):
                        ins = A(prob_p[:, c, k * 256:k * 256 + KEYS[t]], ps[:, 2 * c + k, 0:KEYS[t]], ACT.Exp,
                                bias=negmax[:, c, k:k + 1], scale=DH ** -0.5, accum_out=esum[:, c, k:k + 1])
                else:
                    ins = A(prob[:, c, :], psf[:, 1024 * c:1024 * c + 640], ACT.Exp,
                            bias=negmax[:, c, 0:1], scale=DH ** -0.5, accum_out=esum[:, c, 0:1])
                ins.then_inc(expd, 1)

            def att_take(n):
                t, i = ATT[n]
                c = n % 2
                act.wait_ge(pt_ps, n + 1)
                if n >= 2:
                    act.wait_ge(pv_ps, n - 1)
                if t < 2:
                    k = 256 * (t + 1)
                    copy(probT_p[:, c, 0:k], ps[:, 4, 0:k]).then_inc(pt_sb, 1)
                else:
                    copy(probT[:, c, :], psf[:, 2048:2048 + 640]).then_inc(pt_sb, 1)
                if n % PROMPT_ATT + 2 < PROMPT_ATT:
                    att_exp(n + 2)
                act.wait_ge(pv_ps, n + 1)
                for k in range(KVH):
                    r = slice(64 * k, 64 * k + 64)
                    if t < 2:
                        copy(mixT[r, i, t * P:(t + 1) * P], ps[r, 5, k * P:(k + 1) * P]).then_inc(pv_sb, 1)
                    else:
                        copy(mixT[r, 0:GRP, 2 * P + i * STEPS:2 * P + (i + 1) * STEPS],
                             ps[r, 6, k * 64:(k + 1) * 64].rearrange("p (g t) -> p g t", g=GRP)).then_inc(pv_sb, 1)

            for n in range(7, QKB + TILES):
                if n < QKB:
                    take(n)
                if n in (9, 10):
                    att_exp(n - 9)
                for m in PROMPT_AFTER.get(n, ()):
                    att_take(m)

            for t in range(2):
                act.wait_ge(rt_ps, t + 1)
                copy(rT[:, t, :, :], ps[:, t, :].rearrange("p (s t) -> p s t", s=4)).then_inc(rt_sb, 1)
            take(QKB + TILES)
            act.wait_ge(rt_ps, 3)
            copy(qTd, ps[:, 2, :].rearrange("p (h t) -> p h t", h=HB)).then_inc(rt_sb, 1)
            act.wait_ge(rt_ps, 4)
            copy(kTs, ps[:, 3, 0:256].rearrange("p (s t) -> p s t", s=2)).then_inc(rt_sb, 1)
            take(QKB + TILES + 1)
            take(QKB + TILES + 2)

            def square(n, src, scratch):
                A(scratch, src, ACT.Square, accum_out=sumsq[:, n:n + 1]).then_inc(sqd, 1)

            def h2_take(t):
                act.wait_ge(h2t_ps, t + 1)
                copy(h2T[:, 0:4, :], ps[:, 0, :].rearrange("p (c t) -> p c t", c=4)).then_inc(h2t_act, 1)

            def take_q(u):
                act.wait_ge(q_ps, u + 1)
                if u >= 2:
                    act.wait_ge(sc2_ps, u - 1)
                copy(qT[:, u % 2, :, :], q_psum(u).rearrange("p (e t) -> p e t", e=2)).then_inc(q_sb, 1)

            def gate_exp(u):
                act.wait_ge(best_set, u + 1)
                A(ebest[:, u % 2, :], best, ACT.Exp, bias=negbest[:], accum_out=gsum[:, u % 2:u % 2 + 1]).then_inc(gexp, 1)

            def gelus(u):
                def group(n):
                    for s in range(G):
                        act.wait_ge(dotted, n + (s + 1))
                        A(zact[:, s:s + 1], zdot[:, s:s + 1], ACT.Gelu).then_inc(gelued, 1)

                if u == 0:
                    group(0)
                    take_q(1)
                    take_q(2)
                    gate_exp(1)
                    group(G)
                else:
                    with act.Fori(0, GROUPS) as i:
                        group(i * G + u * KP)

            def mix_take(t):
                act.wait_ge(mt_ps, t + 1)
                copy(mixT[:, 4:8, t * P:(t + 1) * P], ps[:, t, :].rearrange("p (c t) -> p c t", c=4)).then_inc(mt_sb, 1)

            mix_take(0)
            act.wait_ge(x1_done, 2)
            square(TILES, x[:, 0, :], h2[0])
            act.wait_ge(sp_ps, 1)
            for e in range(2):
                copy(snp[64 * e:64 * e + 64, :, :], ps[64 * e:64 * e + 64, 3, :].rearrange(
                    "p (q e v) -> p q e v", q=2, e=2)[:, :, e, :]).then_inc(sp_sb, 1)
            h2_take(0)
            take_q(0)
            mix_take(1)
            mix_take(2)
            att_exp(PROMPT_ATT)
            gate_exp(0)
            att_exp(PROMPT_ATT + 1)
            for n in range(PROMPT_ATT, len(ATT)):
                att_take(n)
            for u in range(UNITS):
                t, h = divmod(u, HP)
                gelus(u)
                if h == HP - 1:
                    act.wait_ge(y_read, t + 1)
                    square(2 * TILES + t, x[:, t, :], h2[t % 2])
                if u + 2 < UNITS:
                    gate_exp(u + 2)
                if u + 3 < UNITS:
                    take_q(u + 3)
                if u == 3:
                    act.wait_ge(x1_done, 2 * TILES)
                    square(TILES + 1, x[:, 1, :], h2[1])
                    square(TILES + 2, x[:, 2, :], sq)
                if h == HP - 4 and t + 1 < TILES:
                    h2_take(t + 1)

        @block.vector
        def _(dve):
            V = nc.vector
            count = {}

            def then(ins, s=chain):
                key = s.name
                count[key] = count.get(key, 0) + 1
                ins.then_inc(s, 1)
                dve.wait_ge(s, count[key])

            def mean_square(n):
                dve.wait_ge(sqd, n + 1)
                then(V.tensor_scalar(ms[:, n:n + 1], sumsq[:, n:n + 1], 1.0 / D, EPS, ALU.mult, ALU.add), msd)

            def normed(out, n, t, gain, s):
                dve.wait_ge(rsd, n + 1)
                then(V.scalar_tensor_tensor(out, x[:, t, :], rstd[:, n:n + 1], gain, ALU.mult, ALU.mult), s)

            dve.wait_ge(g1_in, 16)
            for t in range(TILES):
                mean_square(t)
                normed(hnat[:, t % 2, :], t, t, g1b, hready)
                dve.wait_ge(ht_ps, t + 1)
                then(V.tensor_copy(hT[:, 4:8, t * P:(t + 1) * P], ps[:, 2 * (t % 2) + 1, :].rearrange(
                    "p (c t) -> p c t", c=4)), ht_dve)
            dve.wait_ge(ident_in, 32)
            then(V.tensor_copy(ident_bf[:], ident[:]))
            dve.wait_ge(kt_ps, 1)
            then(V.tensor_copy(kaT, ps[:, 0, 0:NTOK]), kt_sb)
            then(V.tensor_copy(kiwT[0:DH + HI, :], ps[0:DH + HI, 1, 0:NTOK]), kt_sb)
            dve.wait_ge(w_ps, 1)
            dve.wait_ge(wz_zero, 1)
            dve.wait_ge(small_in, 16 * 7)
            for t in range(TILES):
                then(V.tensor_tensor(
                    wz[:, t, :].rearrange("p (g s) -> p g s", s=144)[:, :, 0:STEPS],
                    ps[:, 2, t * P:(t + 1) * P].rearrange("p (g s) -> p g s", g=8),
                    m16[:].rearrange("p (a s) -> p a s", a=1).broadcast_to([P, 8, STEPS]), ALU.mult), wz_set)
            def att_max(n):
                t, i = ATT[n]
                c = n % 2
                dve.wait_ge(sc_ps, n + 1)
                w = 2 if t < 2 else 1
                if t < 2:
                    src = ps[:, 2 * c:2 * c + 2, 0:KEYS[t]]
                else:
                    src = psf[:, 1024 * c:1024 * c + 640]
                then(V.tensor_reduce(rowmax[:, 0:w], src, AX.X, ALU.max))
                if n >= 2:
                    dve.wait_ge(expd, n - 1)
                then(V.tensor_scalar(negmax[:, c, 0:w], rowmax[:, 0:w], -(DH ** -0.5), None, ALU.mult), smax)

            def att_scale(n):
                t, i = ATT[n]
                c = n % 2
                w = 2 if t < 2 else 1
                dve.wait_ge(expd, n + 1)
                then(V.reciprocal(resum[:, 0:w], esum[:, c, 0:w]))
                if t < 2:
                    then(V.tensor_scalar(prob_p[:, c, 0:KEYS[t]], prob_p[:, c, 0:KEYS[t]], resum[:, 0:1], None, ALU.mult))
                    then(V.tensor_scalar(prob_p[:, c, 256:256 + KEYS[t]], prob_p[:, c, 256:256 + KEYS[t]], resum[:, 1:2], None, ALU.mult), pscaled)
                else:
                    then(V.tensor_scalar(prob[:, c, :], prob[:, c, :], resum[:, 0:1], None, ALU.mult), pscaled)

            def att_step(n):
                if n % PROMPT_ATT + 1 < PROMPT_ATT:
                    att_scale(n + 1)
                if n % PROMPT_ATT + 2 < PROMPT_ATT:
                    att_max(n + 2)

            def between(r):
                if r == 7:
                    att_max(0)
                if r == 9:
                    att_max(1)
                    att_scale(0)
                if r in (11, 13, 15):
                    att_step((r - 11) // 2)

            for t in range(TILES):
                k = KEYS[t]
                dve.wait_ge(combined, 8 * (t + 1))
                dve.wait_ge(bar_in, 16)
                if k > P:
                    then(V.tensor_copy(score[:, 0:k - P], psf[:, 2048:2048 + k - P]))
                then(V.tensor_tensor(score[:, k - P:k], psf[:, 2048 + k - P:2048 + k],
                                     bar[:, P * (t // 2):P * (t // 2) + P], ALU.add), scored)
                for r in range(0, TOPK[t], 8):
                    then(V.max(out=top8[:], in_=score[:, 0:k]))
                    if TOPK[t] - r < 8:
                        then(V.memset(top8[:, TOPK[t] - r:8], TAKEN))
                    then(V.match_replace(out=score[:, 0:k], in_to_replace=top8[:], in_values=score[:, 0:k],
                                         imm_value=TAKEN))
                    if t == 2:
                        between(r // 8)
                then(V.tensor_scalar(bias[t], score[:, 0:k], -3.36e38, OFF, ALU.is_gt, ALU.mult), biased)

            def rotate(t):
                dve.wait_ge(proj, QKB + t + 1)
                src = ps[:, 6 + (QKB + t) % 2, :].rearrange("p (q h e d) -> p q h e d", q=2, h=HB, e=2)
                dst = rot[:, t, :, :, :].rearrange("p (q h) e d -> p q h e d", q=2)
                for e in range(2):
                    for i in range(2):
                        tab = cs[:, t, i, :, :].rearrange("p q (a d) -> p q a d", a=1).broadcast_to([P, 2, HB, DK // 2])
                        ins = V.tensor_tensor(prod[:, e, i, :, :, :], src[:, :, :, e, :], tab, ALU.mult)
                then(ins)
                V.tensor_tensor(dst[:, :, :, 0, :], prod[:, 0, 0, :, :, :], prod[:, 1, 1, :, :, :], ALU.subtract)
                then(V.tensor_tensor(dst[:, :, :, 1, :], prod[:, 0, 1, :, :, :], prod[:, 1, 0, :, :, :], ALU.add), proj_dve)

            att_scale(4)
            rotate(0)
            att_max(5)
            att_scale(5)
            att_max(6)
            att_scale(6)
            rotate(1)
            att_max(7)
            att_scale(7)
            rotate(2)

            for b in range(2):
                then(V.tensor_copy(rotq2[:, :, b, :, :], rot[:, 2, 0:HB, :, :]), q_twice)

            dve.wait_ge(s_ps, 1)
            for e in range(2):
                then(V.tensor_tensor(am0[:, e::2, :], ps[:, 4 + e, :].rearrange("p (h i) -> p h i", h=2),
                                     dmask[:, e::2, :], ALU.mult), s_masked)

            def by_parity(v):
                return v.rearrange("p (i e) n -> p e i n", e=2)

            dve.wait_ge(s_ps, 2)
            then(V.tensor_tensor(by_parity(am1), ps[:, 4:6, 0:256].rearrange("p e (i n) -> p e i n", i=2),
                                 by_parity(dmask[:, :, 0:P]), ALU.mult), s_masked)
            dve.wait_ge(dms_in, 16)
            then(V.tensor_tensor(by_parity(am2), ps[:, 4:6, 256:512].rearrange("p e (i n) -> p e i n", i=2),
                                 by_parity(dmask_s.rearrange("p (h i) -> p h i", h=HB)), ALU.mult), s_masked)
            def group_norm(t):
                dve.wait_ge(o_ps, t + 1)
                for h in range(HB):
                    ins = V.bn_stats(out=bn6[:, h, :], in_=ps[:, t, h * P:(h + 1) * P])
                then(ins)
                for h in range(HB):
                    ins = V.bn_aggr(out=mv[:, h, :], in_=bn6[:, h, :])
                then(ins)
                then(V.tensor_scalar(veps[:], mv[:, :, 1], EPS, None, ALU.add), o_var)
                dve.wait_ge(o_rstd, t + 1)
                for h in range(HB):
                    ins = V.tensor_scalar(mixnat[:, t, h * P:(h + 1) * P], ps[:, t, h * P:(h + 1) * P],
                                          mv[:, h, 0:1], rstd4[:, h:h + 1],
                                          ALU.subtract, ALU.mult)
                then(ins)
                then(V.tensor_tensor(mixnat[:, t, :], mixnat[:, t, :], gs[:, t, :], ALU.mult), o_norm)
            group_norm(0)
            for t in range(2):
                then(V.tensor_tensor(kdn[:, t, :, :], rot[:, t, HB:2 * HB, :, :].rearrange("p h e d -> p h (e d)"),
                                     kd[:, t * HB:(t + 1) * HB].rearrange("p (h a) -> p h a", a=1).broadcast_to([P, HB, DK]),
                                     ALU.mult), kdec)
            dve.wait_ge(proj, len(UN))
            for e in range(2):
                decay = kd[:, 2 * HB:].rearrange("p (q e h a) -> p q e h a", q=4, e=2, a=1)[:, :, e, :, :]
                then(V.tensor_tensor(kz[:, :, :, e, :], rot[:, 2:3, HB:2 * HB, :, :].rearrange(
                    "p q h e d -> p q h (e d)").broadcast_to([P, 4, HB, DK]), decay.broadcast_to([P, 4, HB, DK]), ALU.mult), kdec)
            then(V.tensor_copy(selb, ident_bf[:].rearrange("p (b a t) -> p b a t", b=STREAMS, a=1).broadcast_to(
                [P, STREAMS, 8, STEPS])), sel_set)
            dve.wait_ge(zeroed, 1)
            dve.wait_ge(rt_sb, 4)
            for h in range(HB):
                then(V.tensor_tensor(qz[:, h, :].rearrange("p (q n) -> p q n", q=4)[:, :, 0:2 * STEPS],
                                     qTd[:, h, :].rearrange("p (q n) -> p q n", q=4),
                                     qmask[:, h, :].rearrange("p (q n) -> p q n", q=4), ALU.mult), qz_set)
            for k in range(KVH):
                r = slice(64 * k, 64 * k + 64)
                then(V.tensor_copy(qzb[r, :, k, :, :], qaT[r, :, 2 * P:3 * P].rearrange("p g (b t) -> p b g t", b=STREAMS)), qzb_set)
            def carry_states():
                dve.wait_ge(ss_ps, 1)
                dve.wait_ge(o_ps, TILES)
                for h in range(HB):
                    then(V.scalar_tensor_tensor(s0[:, :, h, :], s0[:, :, h, :], float(np.exp(STEPS * LG[h])),
                                                ps[:, 4:8, h * P:(h + 1) * P], ALU.mult, ALU.add), ss_sb)

            def add_mix(t, bank, e):
                dve.wait_ge(wout, 2 * t + e + 1)
                half = x[:, t, e * 512:(e + 1) * 512]
                then(V.tensor_tensor(half, ps[:, bank + e, :], half, ALU.add), x1_done)

            def h2_take(t):
                dve.wait_ge(h2t_ps, t + 1)
                then(V.tensor_copy(h2T[:, 4:8, :], ps[:, 1, :].rearrange("p (c t) -> p c t", c=4)), h2t_dve)

            def top16_halves(u):
                dve.wait_ge(sc2_ps, u + 1)
                s = [sc_psum(u)[:, e * P:(e + 1) * P] for e in range(2)]
                for e in range(2):
                    ins = V.max(out=top[:, e, 0:8], in_=s[e])
                then(ins)
                for e in range(2):
                    ins = V.match_replace(out=rest[e], in_to_replace=top[:, e, 0:8], in_values=s[e], imm_value=TAKEN)
                then(ins)
                for e in range(2):
                    ins = V.max(out=top[:, e, 8:16], in_=rest[e])
                for e in range(2):
                    ins = V.max_index(topi[:, e, 0:8], top[:, e, 0:8], s[e])
                then(ins, topped)
                for e in range(2):
                    ins = V.max_index(topi[:, e, 8:16], top[:, e, 8:16], rest[e])
                then(ins)
                then(V.tensor_copy(topf, topi))

            def top16_pairs(u):
                c4 = cand.rearrange("p (i j) -> p i j", i=KP)
                then(V.tensor_tensor(c4, top[:, 0, :].rearrange("p (i a) -> p i a", a=1).broadcast_to([P, KP, KP]),
                                     top[:, 1:2, :].broadcast_to([P, KP, KP]), ALU.add))
                if u >= 1:
                    dve.wait_ge(gexp, u)
                then(V.max(out=best[:, 0:8], in_=cand))
                then(V.match_replace(out=cand2, in_to_replace=best[:, 0:8], in_values=cand, imm_value=TAKEN))
                then(V.max(out=best[:, 8:16], in_=cand2))
                then(V.tensor_scalar(negbest[:], best[:, 0:1], -1.0, None, ALU.mult), best_set)
                V.max_index(besti[:, 0:8], best[:, 0:8], cand)
                then(V.max_index(besti[:, 8:16], best[:, 8:16], cand2))

            def top16_ids(u):
                V.tensor_scalar(rank[:, 0, :], besti, 4, None, ALU.logical_shift_right)
                then(V.tensor_scalar(rank[:, 1, :], besti, 15, None, ALU.bitwise_and))
                then(V.tensor_copy(rankf, rank))
                for e in range(2):
                    ins = V.tensor_tensor(hot[:, e, :, :],
                                          rankf[:, e, :].rearrange("p (k a) -> p k a", a=1).broadcast_to([P, KP, KP]),
                                          iota[:].rearrange("p (a r) -> p a r", a=1).broadcast_to([P, KP, KP]),
                                          ALU.is_equal)
                then(ins)
                for e in range(2):
                    ins = V.tensor_tensor(hoti[:, e, :, :], hot[:, e, :, :],
                                          topf[:, e:e + 1, :].broadcast_to([P, KP, KP]), ALU.mult)
                then(ins)
                then(V.tensor_reduce(half_id, hoti, AX.X, ALU.add))
                dve.wait_ge(gexp, u + 1)
                then(V.reciprocal(rgsum[:], gsum[:, u % 2:u % 2 + 1]))
                then(V.tensor_scalar(gates[:, u * KP:(u + 1) * KP], ebest[:, u % 2, :], rgsum[:], None, ALU.mult))
                then(V.scalar_tensor_tensor(ids[:, u * KP:(u + 1) * KP], half_id[:, 0, :], float(NK), half_id[:, 1, :],
                                            ALU.mult, ALU.add), picked)

            def top16(u):
                top16_halves(u)
                top16_pairs(u)
                top16_ids(u)

            def picks(u):
                t = u // HP

                def scaled(n, s):
                    dve.wait_ge(gelued, n + 1)
                    gate = gates[:, n:n + 1] if isinstance(n, int) else gates[:, bass.ds(n, 1)]
                    V.tensor_scalar(diag[:, s, :], ident[:], zact[:, s:s + 1], gate,
                                    ALU.mult, ALU.mult).then_inc(diagd, 1)

                def group(g, n):
                    for s in range(G):
                        dve.wait_ge(landed[s], (g + 1) * 16)
                        V.tensor_tensor_reduce(row[s][:, 0:D], row[s][:, 0:D], h2[t % 2], 1.0, 0.0, ALU.mult, ALU.add,
                                               zdot[:, s:s + 1]).then_inc(dotted, 1)
                        if s > 0:
                            scaled(n + (s - 1), s - 1)
                    scaled(n + (G - 1), G - 1)

                if u == 0:
                    group(0, 0)
                    top16(1)
                    group(1, G)
                else:
                    with dve.Fori(0, GROUPS) as i:
                        group(i + u * GROUPS, i * G + u * KP)

            for e in range(2):
                add_mix(0, 2, e)
            dve.wait_ge(keys_in, 32)
            mean_square(TILES)
            normed(h2[0], TILES, 0, g2b[:], hready)
            group_norm(1)
            carry_states()
            h2_take(0)
            group_norm(2)
            top16_halves(0)
            att_max(PROMPT_ATT)
            top16_pairs(0)
            att_scale(PROMPT_ATT)
            att_max(PROMPT_ATT + 1)
            top16_ids(0)
            for n in range(PROMPT_ATT, len(ATT)):
                att_step(n)
            for u in range(UNITS):
                t, h = divmod(u, HP)
                picks(u)
                if h == HP - 1:
                    dve.wait_ge(acc, (u + 1) * KP)
                    then(V.tensor_copy(x[:, t, :], psf[:, 6 * 512:8 * 512]), y_read)
                for tile, e in LATER_OUT.get(u - 1, ()):
                    add_mix(tile, 0, e)
                if h == HP - 4 and t + 1 < TILES:
                    normed(h2[(t + 1) % 2], TILES + t + 1, t + 1, g2b[:], hready)
                if u + 2 < UNITS:
                    top16(u + 2)
                if u == 3:
                    mean_square(TILES + 1)
                    mean_square(TILES + 2)
                if h == 2 and t > 0:
                    dve.wait_ge(gf_in, 16)
                    normed(x[:, t - 1, :], 2 * TILES + t - 1, t - 1, gfb, y_out)
                if h == HP - 1:
                    mean_square(2 * TILES + t)
                if h == HP - 4 and t + 1 < TILES:
                    h2_take(t + 1)
            normed(x[:, TILES - 1, :], 3 * TILES - 1, TILES - 1, gfb, y_out)


def kernel(x_prompt, x_sample, cache_attn_k, cache_attn_v, cache_idx_k, state_retention, ln1_g, w_in, w_out, ln2_g,
           peer_w_query, peer_keys1, peer_keys2, peer_u, peer_v, ln_final_g):
    import concourse.bacc as bacc
    from concourse.bass_utils import run_bass_kernel_spmd

    def chunked(w):
        return w.reshape(KC, P, -1).transpose(1, 0, 2).reshape(P, -1)

    w, wo, wq = (np.asarray(v)[0] for v in (w_in, w_out, peer_w_query))
    c_qa, c_kv, c_qi = 0, HA * DH, HA * DH + 2 * KVH * DH
    c_ki = c_qi + HI * DH
    c_qb = c_ki + DH + HI
    c_vb = c_qb + 2 * HB * DK
    c_gb = c_vb + HB * DV
    qcols = np.arange(HA * DH).reshape(KVH, GRP, DH).transpose(1, 0, 2).reshape(-1)
    rows_out = np.concatenate([qcols, np.arange(HA * DH, D)])
    arrays = {
        "x": np.concatenate([np.asarray(x_prompt).reshape(2, P, D), np.asarray(x_sample).reshape(1, P, D)]),
        "ln1_g": np.asarray(ln1_g)[0], "ln2_g": np.asarray(ln2_g)[0], "ln_final_g": np.asarray(ln_final_g),
        "w_kv": chunked(np.concatenate([w[:, c_kv:c_qi], w[:, c_ki:c_qb]], 1)),
        "w_qi": chunked(w[:, c_qi:c_ki]), "w_qa": chunked(w[:, qcols]),
        "w_qkb": chunked(w[:, c_qb:c_vb]), "w_vb": chunked(w[:, c_vb:c_gb]), "w_gb": chunked(w[:, c_gb:]),
        "keysT": np.stack([np.asarray(peer_keys1)[0].T, np.asarray(peer_keys2)[0].T], 1).reshape(P, -1),
        "cki": np.asarray(cache_idx_k)[0].transpose(0, 2, 1),
        "ckv": np.stack([np.asarray(cache_attn_k)[0].reshape(STREAMS, PAST, P).transpose(0, 2, 1),
                         np.asarray(cache_attn_v)[0].reshape(STREAMS, 4, P, P).transpose(0, 2, 1, 3).reshape(
                             STREAMS, P, PAST)], 1),
        "s0": np.asarray(state_retention)[0].reshape(4, 2, HB, DK, DV).transpose(1, 3, 0, 2, 4),
        "uv": np.concatenate([np.asarray(peer_u)[0], np.asarray(peer_v)[0]], 1),
    }
    for e in range(2):
        arrays[f"w_out{e}"] = chunked(wo[rows_out][:, e * 512:(e + 1) * 512])
    for j in range(4):
        arrays[f"w_q{j}"] = chunked(wq[:, j * 512:(j + 1) * 512])
    arrays.update(constants())
    arrays = {k: np.ascontiguousarray(v) for k, v in arrays.items()}

    nc = bacc.Bacc("TRN2", target_bir_lowering=False, num_devices=1)
    ins = {k: nc.dram_tensor(f"in_{k}", v.shape, mybir.dt.from_np(v.dtype), kind="ExternalInput").ap()
           for k, v in arrays.items()}
    shapes = {"y": (TILES, P, D), "k": (TILES, P, P), "v": (TILES, P, P), "ki": (TILES, P, DH),
              "state_p": (P, 2, DV), "state_s": (2, DK, 4, HB, DV)}
    outs = {k: nc.dram_tensor(f"out_{k}", s, F32, kind="ExternalOutput").ap() for k, s in shapes.items()}
    outs["kv"] = [[outs["k"][t], outs["v"][t], outs["ki"][t]] for t in range(TILES)]
    build(nc, ins, outs)
    r = run_bass_kernel_spmd(nc, [{f"in_{k}": v for k, v in arrays.items()}], core_ids=[0]).results[0]
    y, k, v, ki = (r["out_" + n] for n in ("y", "k", "v", "ki"))
    state_p = r["out_state_p"].reshape(2, DK, 2, DV).transpose(2, 0, 1, 3).reshape(1, 1, HB, DK, DV)
    state_s = r["out_state_s"].transpose(2, 0, 3, 1, 4).reshape(1, STREAMS, HB, DK, DV)
    return (y[:2].reshape(1, 2 * P, D), y[2].reshape(STREAMS, STEPS, D),
            k[:2].reshape(1, 1, 2 * P, KVH, DH), v[:2].reshape(1, 1, 2 * P, KVH, DH), ki[:2].reshape(1, 1, 2 * P, DH),
            np.ascontiguousarray(state_p),
            k[2].reshape(1, STREAMS, STEPS, KVH, DH), v[2].reshape(1, STREAMS, STEPS, KVH, DH),
            ki[2].reshape(1, STREAMS, STEPS, DH), np.ascontiguousarray(state_s))
```
